# Optimizing a Trainium2 kernel written in Bass

```python
import jax, jax.numpy as jnp
from jax import lax
import numpy as np

D_MODEL = 1024
BATCH = 1
SEQ = 1024
DEPTH = 1

CHUNK = 64
HEAD_DIM = 64
RWKV_WIDTH = D_MODEL // 2
RWKV_HEADS = RWKV_WIDTH // HEAD_DIM
ATTN_WIDTH = D_MODEL - RWKV_WIDTH
ATTN_HEADS = ATTN_WIDTH // HEAD_DIM
KV_HEADS = 2
GQA_GROUP = ATTN_HEADS // KV_HEADS
KV_WIDTH = KV_HEADS * HEAD_DIM
WINDOW = 128
WINDOW_CHUNKS = WINDOW // CHUNK
DECAY_LORA = 64
AAA_LORA = 64
GATE_LORA = 128
D_FF = -(-8 * D_MODEL // (3 * 256)) * 256
NORM_EPS = 1e-6
GN_EPS = 64e-5
L2_EPS = 1e-12
NEG_INF = -1e30
RWKV_IN_WIDTH = 3 * RWKV_WIDTH + DECAY_LORA + AAA_LORA + GATE_LORA
IN_WIDTH = RWKV_IN_WIDTH + ATTN_WIDTH + 2 * KV_WIDTH

kernel_name = "hybrid_rwkv7_swa_sink_alibi_block"

def rmsnorm(x, g):
    xf = x.astype(jnp.float32)
    y = xf * lax.rsqrt(jnp.mean(xf * xf, axis=-1, keepdims=True) + NORM_EPS)
    return (y * g.astype(jnp.float32)).astype(x.dtype)

def alibi_slopes():
    return jnp.exp2(-8.0 * jnp.arange(1, ATTN_HEADS + 1, dtype=jnp.float32) / ATTN_HEADS)

def rwkv7_time_mix(p, mu, w0, w_up, a0, a_up, g_up, k_k, k_a, r_k, gn_g, gn_b):
    B, T, _ = p.shape
    H, N, W = RWKV_HEADS, HEAD_DIM, RWKV_WIDTH
    prev = jnp.pad(p[:, :-1], ((0, 0), (1, 0), (0, 0)))
    p = p + (prev - p) * mu
    r, k, v, wd, ad, gd = jnp.split(
        p, [W, 2 * W, 3 * W, 3 * W + DECAY_LORA, 3 * W + DECAY_LORA + AAA_LORA], axis=-1)
    w = -jax.nn.softplus(-(w0 + jnp.tanh(wd) @ w_up)) - 0.5
    decay = jnp.exp(-jnp.exp(w.astype(jnp.float32)))
    a = jax.nn.sigmoid(a0 + ad @ a_up)
    g = jax.nn.sigmoid(gd) @ g_up
    heads = lambda t: t.reshape(B, T, H, N).astype(jnp.float32)
    kk = heads(k * k_k)
    kk = kk / jnp.maximum(jnp.sqrt(jnp.sum(kk * kk, axis=-1, keepdims=True)), L2_EPS)
    k = k * (1.0 + (a - 1.0) * k_a)
    r_h, k_h, v_h, a_h, w_h = heads(r), heads(k), heads(v), heads(a), heads(decay)

    def step(S, inp):
        r_t, w_t, k_t, v_t, kk_t, a_t = inp
        sa = jnp.einsum('bhvk,bhk->bhv', S, -kk_t)
        S = (S * w_t[:, :, None, :]
             + sa[..., None] * (kk_t * a_t)[:, :, None, :]
             + v_t[..., None] * k_t[:, :, None, :])
        return S, jnp.einsum('bhvk,bhk->bhv', S, r_t)

    xs = tuple(jnp.moveaxis(t, 1, 0) for t in (r_h, w_h, k_h, v_h, kk, a_h))
    S0 = jnp.zeros((B, H, N, N), jnp.float32)
    _, o = lax.scan(step, S0, xs)
    o = jnp.moveaxis(o, 0, 1)
    mean = jnp.mean(o, axis=-1, keepdims=True)
    var = jnp.mean(jnp.square(o - mean), axis=-1, keepdims=True)
    o = ((o - mean) * lax.rsqrt(var + GN_EPS)).reshape(B, T, W)
    o = o * gn_g.astype(jnp.float32) + gn_b.astype(jnp.float32)
    bonus = jnp.sum(r_h * k_h * r_k.astype(jnp.float32), axis=-1, keepdims=True) * v_h
    o = o + bonus.reshape(B, T, W)
    return (o * g.astype(jnp.float32)).astype(p.dtype)

def swa_sink_attention(q, k, v, sinks):
    B, T, _ = q.shape
    C, NC, WC = CHUNK, T // CHUNK, WINDOW_CHUNKS
    SB = WC * C
    q = q.reshape(B, NC, C, KV_HEADS, GQA_GROUP, HEAD_DIM)

    def band(t):
        t = t.reshape(B, T, KV_HEADS, HEAD_DIM)
        t = jnp.pad(t, ((0, 0), ((WC - 1) * C, 0), (0, 0), (0, 0)))
        t = t.reshape(B, NC + WC - 1, C, KV_HEADS, HEAD_DIM)
        return jnp.concatenate([t[:, j:j + NC] for j in range(WC)], axis=2)

    kb, vb = band(k), band(v)
    scale = HEAD_DIM ** -0.5
    scores = jnp.einsum('bnqkgd,bnskd->bnkgqs', q, kb).astype(jnp.float32) * scale
    qi = jnp.arange(C, dtype=jnp.float32) + (WC - 1) * C
    si = jnp.arange(SB, dtype=jnp.float32)
    dist = jnp.abs(qi[:, None] - si[None, :])
    slopes = alibi_slopes().reshape(KV_HEADS, GQA_GROUP)
    scores = scores - slopes[None, None, :, :, None, None] * dist
    key_chunk = jnp.arange(NC)[:, None] - (WC - 1) + jnp.arange(SB)[None, :] // C
    valid = (key_chunk >= 0)[None, :, None, None, None, :]
    scores = jnp.where(valid, scores, NEG_INF)
    sink = sinks.astype(jnp.float32).reshape(KV_HEADS, GQA_GROUP)[None, None, :, :, None, None]
    m = jnp.maximum(jnp.max(scores, axis=-1, keepdims=True), sink)
    pexp = jnp.exp(scores - m)
    probs = pexp / (jnp.sum(pexp, axis=-1, keepdims=True) + jnp.exp(sink - m))
    o = jnp.einsum('bnkgqs,bnskd->bnqkgd', probs.astype(v.dtype), vb)
    return o.reshape(B, T, ATTN_WIDTH)

def setup_inputs(seed: int = 0) -> dict:
    key = jax.random.key(seed)
    ks = jax.random.split(key, 24)
    nrm = lambda k, shape, s: jax.random.normal(k, shape, jnp.float32) * s
    L = DEPTH
    return {
        "x": nrm(ks[0], (BATCH, SEQ, D_MODEL), 1.0),
        "norm_mix_g": 1.0 + nrm(ks[1], (L, D_MODEL), 0.02),
        "w_in": nrm(ks[2], (L, D_MODEL, IN_WIDTH), D_MODEL ** -0.5),
        "mu_shift": jax.random.uniform(ks[3], (L, RWKV_IN_WIDTH), jnp.float32),
        "w0": nrm(ks[4], (L, RWKV_WIDTH), 0.5),
        "w_up": nrm(ks[5], (L, DECAY_LORA, RWKV_WIDTH), DECAY_LORA ** -0.5),
        "a0": nrm(ks[6], (L, RWKV_WIDTH), 0.5),
        "a_up": nrm(ks[7], (L, AAA_LORA, RWKV_WIDTH), AAA_LORA ** -0.5),
        "g_up": nrm(ks[8], (L, GATE_LORA, RWKV_WIDTH), GATE_LORA ** -0.5),
        "k_k": 0.85 + nrm(ks[9], (L, RWKV_WIDTH), 0.05),
        "k_a": 1.0 + nrm(ks[10], (L, RWKV_WIDTH), 0.05),
        "r_k": nrm(ks[11], (L, RWKV_HEADS, HEAD_DIM), 0.1),
        "gn_g": 1.0 + nrm(ks[12], (L, RWKV_WIDTH), 0.02),
        "gn_b": nrm(ks[13], (L, RWKV_WIDTH), 0.02),
        "sinks": nrm(ks[14], (L, ATTN_HEADS), 1.0),
        "w_out": nrm(ks[15], (L, D_MODEL, D_MODEL), D_MODEL ** -0.5),
        "norm_ffn_g": 1.0 + nrm(ks[16], (L, D_MODEL), 0.02),
        "w_gate_up": nrm(ks[17], (L, D_MODEL, 2 * D_FF), D_MODEL ** -0.5),
        "w_down": nrm(ks[18], (L, D_FF, D_MODEL), D_FF ** -0.5),
        "norm_final_g": 1.0 + nrm(ks[19], (D_MODEL,), 0.02),
    }

def reference(x, norm_mix_g, w_in, mu_shift, w0, w_up, a0, a_up, g_up, k_k, k_a, r_k,
              gn_g, gn_b, sinks, w_out, norm_ffn_g, w_gate_up, w_down, norm_final_g):
    for l in range(DEPTH):
        h = rmsnorm(x, norm_mix_g[l])
        proj = h @ w_in[l]
        p_rwkv, q, k_att, v_att = jnp.split(
            proj, [RWKV_IN_WIDTH, RWKV_IN_WIDTH + ATTN_WIDTH,
                   RWKV_IN_WIDTH + ATTN_WIDTH + KV_WIDTH], axis=-1)
        o_rwkv = rwkv7_time_mix(p_rwkv, mu_shift[l], w0[l], w_up[l], a0[l], a_up[l], g_up[l],
                                k_k[l], k_a[l], r_k[l], gn_g[l], gn_b[l])
        o_attn = swa_sink_attention(q, k_att, v_att, sinks[l])
        mix = jnp.concatenate([o_rwkv, o_attn], axis=-1)
        x = x + mix @ w_out[l]
        h = rmsnorm(x, norm_ffn_g[l])
        gate, up = jnp.split(h @ w_gate_up[l], 2, axis=-1)
        x = x + (jax.nn.silu(gate) * up) @ w_down[l]
    return rmsnorm(x, norm_final_g)


_drawn_inputs = setup_inputs


def setup_inputs(seed=0):
    import zlib

    import numpy as np

    out = dict(_drawn_inputs(seed))
    spreads = {}
    factors = {'norm_mix_g': 3.053,
     'k_k': 36.311,
     'gn_g': 21.847,
     'gn_b': 21.98,
     'sinks': 25.272,
     'norm_ffn_g': 4.128,
     'norm_final_g': 8.056}
    for name, (base, spread) in spreads.items():
        noise = np.random.default_rng([zlib.crc32(name.encode()), seed]).standard_normal(out[name].shape)
        drawn = base * np.exp(spread * noise) if base else spread * noise
        out[name] = __import__('jax').numpy.asarray(drawn.astype(out[name].dtype))
    for name, factor in factors.items():
        out[name] = (out[name] * factor).astype(out[name].dtype)
    return out
```

```python
from contextlib import ExitStack

import numpy as np

import concourse.bass as bass
from concourse import mybir

ALU = mybir.AluOpType
ACT = mybir.ActivationFunctionType
AX_X = mybir.AxisListType.X
F32 = mybir.dt.float32
F32R = mybir.dt.float32r
U32 = mybir.dt.uint32

P = 128
T = 1024
D = 1024
NT = T // P
KD = D // P
HD = 64
H = 8
NP = H // 2
W = H * HD
NRW = 14
NAT = 6
NIN = NRW + NAT
FF = 2816
HALF = 512
GROUPS = [6, 6, 5, 5]
BAND = 192
DECAY = float(np.exp(-0.5))
EPS = 1e-6
GN_EPS = 64e-5
L2_EPS = 1e-12
NEG = -1e30
LEVELS = [1, 2, 4, 8, 16, 32, 64]

C_ID, C_CUM, C_UP, C_M1T, C_LEV, C_BLK, C_ONE, C_END = np.cumsum([0, P, 2 * P, 2 * P, P, P * 6, P, P]).tolist()
R_MU, R_A0, R_KK, R_KA, R_RK, R_GG, R_GB, R_N1, R_N2, R_END = np.cumsum(
    [0, NRW, NP, NP, NP, NP, NP, NP, KD, KD]).tolist()


def constants():
    s, t = np.arange(P)[:, None], np.arange(P)[None, :]
    mid = P // 2
    c = np.zeros((P, C_END), np.float32)
    c[:, C_ID:C_ID + P] = s == t
    c[:, C_CUM:C_CUM + P] = (s <= t).astype(np.float32) - (s < mid)
    c[:, C_CUM + P:C_CUM + 2 * P] = (s < t).astype(np.float32) - (s < mid)
    c[:, C_UP:C_UP + P] = s < t
    c[:, C_UP + P:C_UP + 2 * P] = s <= t

    def corner(b):
        return (s // (2 * b) == t // (2 * b)) & (s % (2 * b) >= b) & (t % (2 * b) < b)

    c[:, C_M1T:C_M1T + P] = corner(1).T
    for n, b in enumerate(LEVELS[1:]):
        c[:, C_LEV + n * P:C_LEV + (n + 1) * P] = corner(b)
    c[:, C_BLK:C_BLK + P] = s // HD == t // HD
    c[:, C_ONE:C_ONE + P] = 1
    return c


def alibi():
    q, k = np.arange(P)[:, None], np.arange(BAND)[None, :] - HD
    seen = (k // HD <= q // HD) & (k // HD >= q // HD - 1)
    b = np.zeros((P, H * BAND), np.float32)
    for h in range(H):
        slope = np.float32(2.0 ** (-8.0 * (h + 1) / H))
        b[:, h * BAND:(h + 1) * BAND] = np.where(seen, -slope * np.abs(q - k), NEG)
    return b


def hybrid_block(nc, x, norm_mix_g, w_in, mu_shift, w0, w_up, a0, a_up, g_up, k_k, k_a, r_k, gn_g, gn_b,
                 sinks, w_out, norm_ffn_g, w_gate_up, w_down, norm_final_g, consts, bias_in, out):
    root = ExitStack()

    def sem(name):
        return root.enter_context(nc.semaphore(name))

    BASE = (nc.sbuf_base + 31) // 32 * 32
    K = 1024

    def at(name, kb, shape, dt=F32):
        return nc.alloc_sbuf_tensor_at(name, shape, dt, offset=BASE + int(kb * K))

    w_in_v = w_in[0].rearrange("(k p) n -> p k n", p=P)
    w_out_v = w_out[0].rearrange("(k p) n -> p k n", p=P)
    w_gu_v = w_gate_up[0].rearrange("(k p) n -> p k n", p=P)
    w_dn_v = w_down[0].rearrange("(k p) n -> p k n", p=P)
    sg_dram = nc.dram_tensor("sg_scratch", (T, W), F32, kind="Internal").ap()
    v_dram = nc.dram_tensor("v_scratch", (T, W), F32, kind="Internal").ap()

    with root:
        bank = [root.enter_context(nc.psum_tensor(f"bank{b}", [P, HALF], F32)) for b in range(8)]
        full = [sem(f"bank_full{b}") for b in range(8)]
        free = [sem(f"bank_free{b}") for b in range(8)]

        class Jobs:
            base = [0] * 8

            def __init__(self, table):
                self.bank_of, self.nth, self.per = dict(table), {}, [0] * 8
                for job, b in table:
                    self.nth[job] = self.per[b]
                    self.per[b] += 1
                self.start = list(Jobs.base)

            def end(self, tiles):
                for b in range(8):
                    Jobs.base[b] += self.per[b] * tiles

            def before(self, job, t):
                b = self.bank_of[job]
                return t * self.per[b] + (self.start[b] + self.nth[job])

            def claim(self, pe, job, t):
                b = self.bank_of[job]
                pe.wait_ge(free[b], self.before(job, t))
                return bank[b]

            def done(self, mm, job):
                mm.then_inc(full[self.bank_of[job]], 1)

            def result(self, eng, job, t):
                b = self.bank_of[job]
                eng.wait_ge(full[b], self.before(job, t) + 1)
                return bank[b]

            def emptied(self, eng, job, t):
                eng.wait_ge(free[self.bank_of[job]], self.before(job, t) + 1)

            def read(self, ins, job):
                ins.then_inc(free[self.bank_of[job]], 1)

        class Order:

            def __init__(self, eng, name):
                self.eng, self.sem, self.n, self.turn, self.per = eng, sem(name), 0, 0, 0

            def __call__(self, ins):
                ins.then_inc(self.sem, 1)
                self.n += 1
                self.eng.wait_ge(self.sem, self.turn + self.n)

            def tile(self, t, per):
                assert self.per in (0, per) and (not self.per or self.n == self.origin + per)
                if not self.per:
                    self.origin, self.per = self.n, per
                self.turn, self.n = t * per, self.origin

            def leave(self, tiles):
                assert self.n == self.origin + self.per
                self.n, self.turn, self.per = self.origin + self.per * tiles, 0, 0

        cst = at("cst", 0, [P, C_END])
        par = at("par", 7, [P, R_END])
        small = at("small", 7.5, [P, 128])
        ident = cst[:, C_ID:C_ID + P]
        ones_blk = cst[:, C_BLK:C_BLK + P]
        ones = cst[:, C_ONE:C_ONE + P]
        rkv = at("rkv", 8, [P, 12, T])

        hhi = at("hhi", 56, [P, KD, T], F32R)
        hlo = at("hlo", 88, [P, KD, T], F32R)
        xin = at("xin", 188.5, [P, 2, D])
        xs = at("xs", 196.5, [P, 2, D])
        prow = at("prow", 204.5, [P, P])
        s_cst, s_par, s_x = sem("s_cst"), sem("s_par"), [sem("s_x0"), sem("s_x1")]
        s_pc, s_ss, s_sq, s_rs, s_xs, s_hh, s_c0 = (sem(f"s1_{n}") for n in ("pc", "ss", "sq", "rs", "xs", "hh", "c0"))
        J = Jobs([("par", 7), ("x00", 0), ("x01", 1), ("x10", 2), ("x11", 3)])
        with nc.Block() as block:
            @block.sync
            def _(sp):
                sp.dma_start(cst[:, :], consts).then_inc(s_cst, 16)
                rows = [(mu_shift, R_MU, NRW), (a0, R_A0, NP), (k_k, R_KK, NP), (k_a, R_KA, NP), (r_k, R_RK, NP),
                        (gn_g, R_GG, NP), (gn_b, R_GB, NP), (norm_mix_g, R_N1, KD), (norm_ffn_g, R_N2, KD)]
                for a, r, n in rows:
                    v = a[0] if len(a.shape) == 2 else a[0].rearrange("h n -> (h n)")
                    sp.dma_start(prow[r:r + n, :], v.rearrange("(j p) -> j p", p=P)).then_inc(s_par, 16)
                for t in range(NT):
                    if t >= 2:
                        sp.wait_ge(s_xs, t - 1)
                    sp.dma_start(xin[:, t % 2, :], x[0, t * P:(t + 1) * P, :]).then_inc(s_x[t % 2], 16)

            @block.scalar
            def _(act):
                act.wait_ge(s_c0, 1)
                for t in range(NT):
                    act.wait_ge(s_x[t % 2], 16 * (t // 2) + 16)
                    if t >= 2:
                        J.result(act, f"x{t % 2}1", t // 2 - 1)
                    act.activation(xs[:, t % 2, :], xin[:, t % 2, :], ACT.Square,
                                   accum_out=small[:, t:t + 1]).then_inc(s_ss, 1)
                    act.wait_ge(s_ss, t + 1)
                    act.activation(small[:, 8 + t:9 + t], small[:, t:t + 1], ACT.Sqrt, bias=small[:, 32:33],
                                   scale=1.0 / D).then_inc(s_sq, 1)
                    act.wait_ge(s_rs, t + 1)
                    act.mul(xs[:, t % 2, :], xin[:, t % 2, :], small[:, 16 + t:17 + t]).then_inc(s_xs, 1)

            @block.tensor
            def _(pe):
                pe.wait_ge(s_cst, 16)
                pe.wait_ge(s_par, 9 * 16)
                b = J.claim(pe, "par", 0)
                J.done(pe.transpose(b[:, 0:R_END], prow[0:R_END, :], ident[0:R_END, 0:R_END]), "par")
                for t in range(NT):
                    pe.wait_ge(s_xs, t + 1)
                    for g in range(2):
                        b = J.claim(pe, f"x{t % 2}{g}", t // 2)
                        for k in range(4):
                            mm = pe.transpose(b[:, k * P:(k + 1) * P], xs[:, t % 2, (4 * g + k) * P:(4 * g + k + 1) * P],
                                              ident)
                        J.done(mm, f"x{t % 2}{g}")

            @block.vector
            def _(dve):
                dve.memset(small[:, 32:33], EPS).then_inc(s_c0, 1)
                b = J.result(dve, "par", 0)
                J.read(dve.tensor_copy(par[:, :], b[:, 0:R_END]), "par")
                J.emptied(dve, "par", 0)
                for t in range(NT):
                    dve.wait_ge(s_sq, t + 1)
                    dve.reciprocal(small[:, 16 + t:17 + t], small[:, 8 + t:9 + t]).then_inc(s_rs, 1)
                    for g in range(2):
                        b = J.result(dve, f"x{t % 2}{g}", t // 2)
                        ch = slice(4 * g, 4 * g + 4)
                        c = slice(t * P, (t + 1) * P)
                        for k in range(4):
                            gain = par[:, R_N1 + 4 * g + k:R_N1 + 4 * g + k + 1]
                            ins = dve.tensor_scalar(hhi[:, 4 * g + k, c], b[:, k * P:(k + 1) * P], gain, None, ALU.mult)
                        ins.then_inc(s_hh, 1)
                        dve.wait_ge(s_hh, 2 * t + g + 1)
                        for k in range(4):
                            gain = par[:, R_N1 + 4 * g + k:R_N1 + 4 * g + k + 1]
                            ins = dve.scalar_tensor_tensor(hlo[:, 4 * g + k, c], b[:, k * P:(k + 1) * P], gain,
                                                           hhi[:, 4 * g + k, c].bitcast(F32), ALU.mult, ALU.subtract)
                        J.read(ins, f"x{t % 2}{g}")
        J.end(NT // 2)
        Jobs.base[7] -= NT // 2 - 1

        class Layer:
            def __init__(self, tag, view, kt, ring_kb, blocks):
                self.view, self.kt, self.blocks = view, kt, blocks
                self.raw = at(f"{tag}_raw", ring_kb, [P, 2, kt, P])
                self.hi = at(f"{tag}_whi", ring_kb + kt, [P, 2, kt, P], F32R)
                self.lo = at(f"{tag}_wlo", ring_kb + 2 * kt, [P, 2, kt, P], F32R)
                self.landed = [sem(f"{tag}_landed{s}") for s in range(2)]
                self.hi_ready = sem(f"{tag}_hi")
                self.lo_ready = sem(f"{tag}_lo")
                self.J = Jobs([(f"{s}{h}", 2 * s + h) for s in range(2) for h in range(2)])

            def load(self, sp, s, turn, column, rows=0, first=False):
                if not first:
                    sp.wait_ge(self.lo_ready, 2 * turn + (s - 1))
                sp.dma_start(self.raw[:, s, :, :], self.view[:, rows:rows + self.kt, bass.ds(column, P)]
                             ).then_inc(self.landed[s], 16)

            def split_hi(self, act, s, turn, first=False):
                act.wait_ge(self.landed[s], 16 * turn + 16)
                if not first:
                    self.J.result(act, f"{s}1", turn - 1)
                act.activation(self.hi[:, s, :, :], self.raw[:, s, :, :], ACT.Copy).then_inc(self.hi_ready, 1)

            def split_lo(self, dve, s, turn):
                dve.wait_ge(self.hi_ready, 2 * turn + (s + 1))
                dve.tensor_tensor(self.lo[:, s, :, :], self.raw[:, s, :, :], self.hi[:, s, :, :].bitcast(F32),
                                  ALU.subtract).then_inc(self.lo_ready, 1)

            def products(self, pe, s, turn, ahi, alo):
                pe.wait_ge(self.lo_ready, 2 * turn + (s + 1))
                for half in range(2):
                    o = self.J.claim(pe, f"{s}{half}", turn)
                    c = slice(half * HALF, half * HALF + HALF)
                    n, i = 3 * self.kt, 0
                    for k in range(self.kt):
                        for wpart, apart in ((self.hi, ahi), (self.hi, alo), (self.lo, ahi)):
                            mm = pe.matmul(o[:, :], wpart[:, s, k, :], apart[:, k, c], start=i == 0, stop=i == n - 1)
                            i += 1
                    self.J.done(mm, f"{s}{half}")

        wg = at("wg", 120, [P, 2, T])
        att = at("att", 128, [P, NAT, T])
        praw = at("praw", 176, [P, 2, 4 + T])
        pdif = at("pdif", 184.25, [P, T])
        L = Layer("in", w_in_v, KD, 152, NIN)
        s_shift, s_z, s_praw = sem("s_shift"), sem("s_z"), sem("s_praw")
        nsh = NRW // 2
        with nc.Block() as block:
            @block.sync
            def _(sp):
                for s in range(2):
                    L.load(sp, s, 0, s * P, first=True)
                with sp.Fori(1, NIN // 2) as i:
                    for s in range(2):
                        L.load(sp, s, i, (2 * i + s) * P)

            @block.scalar
            def _(act):
                def to_praw(s, turn, first=False):
                    if not first:
                        act.wait_ge(s_shift, 2 * turn + s)
                    for half in range(2):
                        b = L.J.result(act, f"{s}{half}", turn)
                        ins = act.activation(praw[:, s, 4 + half * HALF:4 + (half + 1) * HALF], b[:, :], ACT.Copy)
                        L.J.read(ins, f"{s}{half}")

                def to_att(s, turn):
                    for half in range(2):
                        b = L.J.result(act, f"{s}{half}", turn)
                        ins = act.activation(att[:, bass.ds((turn - nsh) * 2 + s, 1), half * HALF:(half + 1) * HALF]
                                             .rearrange("p a n -> p (a n)"), b[:, :], ACT.Copy)
                        L.J.read(ins, f"{s}{half}")

                for s in range(2):
                    L.split_hi(act, s, 0, first=True)
                for s in range(2):
                    to_praw(s, 0, first=True)
                    L.split_hi(act, s, 1)
                with act.Fori(1, nsh) as i:
                    for s in range(2):
                        to_praw(s, i)
                        L.split_hi(act, s, i + 1)
                with act.Fori(nsh, NIN // 2 - 1) as i:
                    for s in range(2):
                        to_att(s, i)
                        L.split_hi(act, s, i + 1)
                for s in range(2):
                    to_att(s, NIN // 2 - 1)

            @block.vector
            def _(dve):
                order = Order(dve, "shift_order")
                order(dve.memset(praw[:, :, 0:4], 0.0))
                dve.sem_inc(s_shift, 1)

                def shift(s, turn, dst, mu):
                    dve.wait_ge(s_shift, 2 * turn + (s + 1))
                    L.J.emptied(dve, f"{s}1", turn)
                    order(dve.tensor_tensor(pdif[:, :], praw[:, s, 3:3 + T], praw[:, s, 4:4 + T], ALU.subtract))
                    dve.scalar_tensor_tensor(dst, pdif[:, :], mu, praw[:, s, 4:4 + T], ALU.mult, ALU.add
                                             ).then_inc(s_shift, 1)

                for s in range(2):
                    L.split_lo(dve, s, 0)
                with dve.Fori(0, nsh - 1) as i:
                    order.tile(i, 2)
                    for s in range(2):
                        shift(s, i, rkv[:, bass.ds(2 * i + s, 1), :].rearrange("p a n -> p (a n)"),
                              par[:, bass.ds(2 * i + (s + R_MU), 1)])
                        L.split_lo(dve, s, i + 1)
                order.leave(nsh - 1)
                for s in range(2):
                    shift(s, nsh - 1, wg[:, s, :], par[:, R_MU + 12 + s:R_MU + 13 + s])
                    L.split_lo(dve, s, nsh)
                with dve.Fori(nsh, NIN // 2 - 1) as i:
                    for s in range(2):
                        L.split_lo(dve, s, i + 1)

            @block.tensor
            def _(pe):
                with pe.Fori(0, NIN // 2) as i:
                    for s in range(2):
                        L.products(pe, s, i, hhi, hlo)
        L.J.end(NIN // 2)

        mix = at("mix", 152, [P, 8, T])
        kpad = at("kpad", 56, [P, 2, 2, HD + T])
        vpad = at("vpad", 73, [P, HD + T + HD])
        vt = at("vt", 78, [P, NT + 1, P])
        bias = at("bias", 83, [P, H, BAND])
        sc = at("sc", 89, [P, H, BAND])
        pr = at("pr", 95, [P, H, 2 * P])
        pt = at("pt", 103, [P, H, 2, P])
        qst = at("qst", 111, [P, NP, P])
        vst = at("vst", 113, [P, 2, P])
        snk = at("snk", 114, [P, H])
        st8 = at("st8", 114.25, [P, 6, H])
        s_bias, s_snk, s_kp, s_zero = sem("s_bias"), sem("s_snk"), sem("s_kp"), sem("s_zero")
        s_vp, s_vt, s_st, s_sc, s_mx, s_es, s_pe, s_pn, s_pt, s_mo = (
            sem(f"s3_{n}") for n in ("vp", "vt", "stage", "sc", "mx", "es", "exp", "norm", "pt", "out"))
        A = Jobs([("vt0", 0), ("vt1", 1), ("vt2", 2)])
        with nc.Block() as block:
            @block.sync
            def _(sp):
                sp.dma_start(bias[:, :, :], bias_in.rearrange("p (h n) -> p h n", h=H)).then_inc(s_bias, 16)
                sp.dma_start(snk[:, :], sinks.to_broadcast([P, H])).then_inc(s_snk, 16)
                sp.wait_ge(s_zero, 2)
                for e in range(2):
                    for g in range(2):
                        sp.dma_start(kpad[HD * e:HD * e + HD, e, g, HD:], att[HD * g:HD * g + HD, 4, :]).then_inc(s_kp, 16)

            @block.gpsimd
            def _(pool):
                pool.memset(vpad[:, :], 0.0).then_inc(s_zero, 1)
                pool.memset(kpad[:, :, :, :], 0.0).then_inc(s_zero, 1)
                pool.memset(pr[:, :, :], 0.0).then_inc(s_zero, 1)

            @block.scalar
            def _(act):
                act.wait_ge(s_zero, 1)
                act.activation(vpad[:, HD:HD + T], att[:, 5, :], ACT.Copy).then_inc(s_vp, 1)
                for n in range(3):
                    b = A.result(act, f"vt{n}", 0)
                    m = min(4, NT + 1 - 4 * n)
                    A.read(act.activation(vt[:, 4 * n:4 * n + m, :], b[:, 0:m * P], ACT.Copy), f"vt{n}")

            @block.tensor
            def _(pe):
                pe.wait_ge(s_vp, 1)
                for n in range(3):
                    b = A.claim(pe, f"vt{n}", 0)
                    m = min(4, NT + 1 - 4 * n)
                    for j in range(m):
                        mm = pe.transpose(b[:, j * P:(j + 1) * P], vpad[:, (4 * n + j) * P:(4 * n + j + 1) * P], ident)
                    A.done(mm, f"vt{n}")
        A.end(1)
        A = Jobs([(f"sc{p}", p) for p in range(NP)] + [(f"pt{p}", 4 + p) for p in range(NP)] + [("pv", 0)])
        with nc.Block() as block:
            def tiles(eng, body):
                body(0, 0)
                with eng.Fori(1, NT) as t:
                    body(t, 1)

            @block.gpsimd
            def _(pool):
                def body(t, later):
                    if later:
                        A.result(pool, "pv", t - 1)
                    pool.tensor_copy(qst[:, :, :], att[:, 0:NP, bass.ds(t * P, P)]).then_inc(s_st, 1)
                    pool.tensor_copy(vst[:, :, :], vt[:, bass.ds(t, 2), :]).then_inc(s_st, 1)
                tiles(pool, body)

            @block.tensor
            def _(pe):
                pe.wait_ge(s_kp, 4 * 16)

                def body(t, later):
                    pe.wait_ge(s_st, 2 * t + 2)
                    for p in range(NP):
                        b = A.claim(pe, f"sc{p}", t)
                        for e in range(2):
                            mm = pe.matmul(b[:, e * BAND:(e + 1) * BAND], qst[:, p, :],
                                           kpad[:, e, p // 2, bass.ds(t * P, BAND)], start=e == 0, stop=e == 1,
                                           skip_group_check=True)
                        A.done(mm, f"sc{p}")
                    pe.wait_ge(s_pn, t + 1)
                    for p in range(NP):
                        b = A.claim(pe, f"pt{p}", t)
                        for j in range(4):
                            mm = pe.transpose(b[:, j * P:(j + 1) * P], pr[:, 2 * p + j // 2, (j % 2) * P:(j % 2 + 1) * P],
                                              ident)
                        A.done(mm, f"pt{p}")
                    b = A.claim(pe, "pv", t)
                    A.emptied(pe, f"pt{NP - 1}", t)
                    for p in range(NP):
                        for e in range(2):
                            for j in range(2):
                                mm = pe.matmul(b[HD * e:HD * e + HD, p * P:(p + 1) * P],
                                               vst[:, j, (p // 2) * HD:(p // 2 + 1) * HD], pt[:, 2 * p + e, j, :],
                                               start=p == 0 and j == 0, stop=p == NP - 1 and j == 1,
                                               skip_group_check=True)
                    A.done(mm, "pv")
                tiles(pe, body)

            @block.vector
            def _(dve):
                order = Order(dve, "att_order")
                dve.wait_ge(s_bias, 16)
                dve.wait_ge(s_snk, 16)
                dve.wait_ge(s_zero, 3)

                def body(t, later):
                    order.tile(t, 4)
                    for p in range(NP):
                        b = A.result(dve, f"sc{p}", t)
                        ins = dve.scalar_tensor_tensor(sc[:, 2 * p:2 * p + 2, :],
                                                       b[:, 0:2 * BAND].rearrange("p (a n) -> p a n", a=2), HD ** -0.5,
                                                       bias[:, 2 * p:2 * p + 2, :], ALU.mult, ALU.add)
                        A.read(ins, f"sc{p}")
                    A.emptied(dve, f"sc{NP - 1}", t)
                    if not later:
                        dve.memset(sc[:, :, 0:HD], NEG).then_inc(s_sc, 1)
                        dve.wait_ge(s_sc, 1)
                    order(dve.tensor_reduce(st8[:, 0, :], sc[:, :, :], AX_X, ALU.max))
                    order(dve.tensor_tensor(st8[:, 1, :], st8[:, 0, :], snk[:, :], ALU.max))
                    dve.tensor_tensor(st8[:, 2, :], snk[:, :], st8[:, 1, :], ALU.subtract).then_inc(s_mx, 1)
                    dve.tensor_scalar(st8[:, 3, :], st8[:, 1, :], -1.0, None, ALU.mult).then_inc(s_mx, 1)
                    dve.wait_ge(s_pe, 9 * t + 9)
                    order(dve.tensor_tensor(st8[:, 5, :], st8[:, 5, :], st8[:, 4, :], ALU.add))
                    order(dve.reciprocal(st8[:, 5, :], st8[:, 5, :]))
                    dve.tensor_tensor(pr[:, :, 0:BAND], pr[:, :, 0:BAND],
                                      st8[:, 5, :].unsqueeze(2).to_broadcast([P, H, BAND]), ALU.mult).then_inc(s_pn, 1)
                    b = A.result(dve, "pv", t)
                    ins = dve.tensor_copy(mix[:, NP:2 * NP, bass.ds(t * P, P)],
                                          b[:, :].rearrange("p (a n) -> p a n", a=NP))
                    A.read(ins, "pv")
                tiles(dve, body)

            @block.scalar
            def _(act):
                def body(t, later):
                    act.wait_ge(s_mx, 2 * t + 2)
                    act.activation(st8[:, 4, :], st8[:, 2, :], ACT.Exp).then_inc(s_pe, 1)
                    for h in range(H):
                        act.activation(pr[:, h, 0:BAND], sc[:, h, :], ACT.Exp, bias=st8[:, 3, h:h + 1],
                                       accum_out=st8[:, 5, h:h + 1]).then_inc(s_pe, 1)
                    for p in range(NP):
                        b = A.result(act, f"pt{p}", t)
                        if p == 0 and later:
                            A.result(act, "pv", t - 1)
                        ins = act.activation(pt[:, 2 * p:2 * p + 2, :, :].rearrange("p a b n -> p (a b n)"), b[:, :],
                                             ACT.Copy)
                        A.read(ins, f"pt{p}")
                tiles(act, body)
        A.end(NT)

        kkn = at("kkn", 56, [P, NP, T])
        ab = at("ab", 72, [P, NP, T])
        lora = at("lora", 88, [P, 4, W])
        sq = at("sq", 96, [P, 2, T])
        tm = at("tm", 104, [P, 2, T])
        sgo = at("sgo", 112, [P, 2, W])
        vo = at("vo", 116, [P, 2, W])
        omka = small[:, 40:40 + NP]
        rT, kT, vT = rkv[:, 0:4, :], rkv[:, 4:8, :], rkv[:, 8:12, :]
        s_lz, s_lora, s_wd, s_gd = sem("s_lz"), sem("s_lora"), sem("s_wd"), sem("s_gd")
        s_sgo, s_sgd, s_vd = sem("s_sgo"), [sem("s_sgd0"), sem("s_sgd1")], [sem("s_vd0"), sem("s_vd1")]
        s_kkr, s_sqr, s_nrm, s_root, s_prod = sem("s_kkr"), sem("s_sqr"), sem("s_nrm"), sem("s_root"), sem("s_prod")
        B = Jobs([(f"{kind}{n}", n) for kind in ("a", "sg", "ss", "bs", "v", "g") for n in range(8)])
        with nc.Block() as block:
            @block.sync
            def _(sp):
                sp.dma_start(lora[:, 2, :], g_up[0]).then_inc(s_lora, 16)
                sp.dma_start(lora[:, 3, :], w0.to_broadcast([P, W])).then_inc(s_lora, 16)
                sp.wait_ge(s_lz, 1)
                sp.dma_start(lora[0:HD, 0, :], w_up[0]).then_inc(s_lora, 16)
                sp.dma_start(lora[HD:P, 1, :], a_up[0]).then_inc(s_lora, 16)
                for n in range(NT):
                    sp.wait_ge(s_sgo, n + 1)
                    sp.dma_start(sg_dram[n * P:(n + 1) * P, :], sgo[:, n % 2, :]).then_inc(s_sgd[n % 2], 16)
                for n in range(NT):
                    B.emptied(sp, f"v{n}", 0)
                    sp.dma_start(v_dram[n * P:(n + 1) * P, :], vo[:, n % 2, :]).then_inc(s_vd[n % 2], 16)
                for n in range(2):
                    sp.wait_ge(s_sgd[n], 16 * NT // 2)
                    sp.wait_ge(s_vd[n], 16 * NT // 2)

            @block.gpsimd
            def _(pool):
                pool.memset(lora[:, 0:2, :], 0.0).then_inc(s_lz, 1)

            @block.tensor
            def _(pe):
                pe.wait_ge(s_lora, 4 * 16)
                pe.wait_ge(s_wd, 1)
                for n in range(8):
                    b = B.claim(pe, f"a{n}", 0)
                    B.done(pe.matmul(b[:, :], lora[:, 1, (n // 2) * P:(n // 2 + 1) * P],
                                     wg[:, 0, (n % 2) * HALF:(n % 2 + 1) * HALF], start=True, stop=True), f"a{n}")
                for n in range(8):
                    b = B.claim(pe, f"sg{n}", 0)
                    B.done(pe.matmul(b[:, :], wg[:, 0, n * P:(n + 1) * P], lora[:, 0, :], start=True, stop=True), f"sg{n}")
                for kind, ready in (("ss", s_sqr), ("bs", s_prod)):
                    src = sq if kind == "ss" else tm
                    for n in range(8):
                        b = B.claim(pe, f"{kind}{n}", 0)
                        pe.wait_ge(ready, n // 2 + 1)
                        B.done(pe.matmul(b[:, :], ones_blk, src[:, (n // 2) % 2, (n % 2) * HALF:(n % 2 + 1) * HALF],
                                         start=True, stop=True), f"{kind}{n}")
                for n in range(8):
                    b = B.claim(pe, f"v{n}", 0)
                    for p in range(NP):
                        mm = pe.transpose(b[:, p * P:(p + 1) * P], vT[:, p, n * P:(n + 1) * P], ident)
                    B.done(mm, f"v{n}")
                pe.wait_ge(s_gd, 1)
                for n in range(8):
                    b = B.claim(pe, f"g{n}", 0)
                    B.done(pe.matmul(b[:, :], lora[:, 2, (n // 2) * P:(n // 2 + 1) * P],
                                     wg[:, 1, (n % 2) * HALF:(n % 2 + 1) * HALF], start=True, stop=True), f"g{n}")

            @block.scalar
            def _(act):
                act.activation(wg[0:HD, 0, :], wg[0:HD, 0, :], ACT.Tanh).then_inc(s_wd, 1)
                act.activation(wg[:, 1, :], wg[:, 1, :], ACT.Sigmoid).then_inc(s_gd, 1)
                for n in range(8):
                    b = B.result(act, f"a{n}", 0)
                    B.read(act.activation(ab[:, n // 2, (n % 2) * HALF:(n % 2 + 1) * HALF], b[:, :], ACT.Sigmoid,
                                          bias=par[:, R_A0 + n // 2:R_A0 + n // 2 + 1]), f"a{n}")
                for n in range(8):
                    B.emptied(act, f"sg{n}", 0)
                    act.activation(sgo[:, n % 2, :], sgo[:, n % 2, :], ACT.Sigmoid).then_inc(s_sgo, 1)
                for p in range(NP):
                    act.wait_ge(s_kkr, p + 1)
                    if p >= 2:
                        B.result(act, f"ss{2 * p - 3}", 0)
                    act.activation(sq[:, p % 2, :], kkn[:, p, :], ACT.Square).then_inc(s_sqr, 1)
                for p in range(NP):
                    act.wait_ge(s_nrm, 2 * p + 2)
                    act.activation(tm[:, p % 2, :], tm[:, p % 2, :], ACT.Sqrt).then_inc(s_root, 1)
                for n in range(8):
                    b = B.result(act, f"v{n}", 0)
                    if n >= 2:
                        act.wait_ge(s_vd[n % 2], 16 * (n // 2))
                    B.read(act.activation(vo[:, n % 2, :], b[:, :], ACT.Copy), f"v{n}")

            @block.vector
            def _(dve):
                order = Order(dve, "prep_order")
                order(dve.tensor_scalar(omka, par[:, R_KA:R_KA + NP], -1.0, 1.0, ALU.mult, ALU.add))
                for p in range(NP):
                    dve.tensor_scalar(kkn[:, p, :], kT[:, p, :], par[:, R_KK + p:R_KK + p + 1], None, ALU.mult
                                      ).then_inc(s_kkr, 1)
                for n in range(8):
                    b = B.result(dve, f"sg{n}", 0)
                    if n >= 2:
                        dve.wait_ge(s_sgd[n % 2], 16 * (n // 2))
                    ins = dve.tensor_tensor(sgo[:, n % 2, :], b[:, :], lora[:, 3, :], ALU.add)
                    B.read(ins, f"sg{n}")
                for p in range(NP):
                    for h in range(2):
                        n = 2 * p + h
                        b = B.result(dve, f"ss{n}", 0)
                        ins = dve.tensor_scalar(tm[:, p % 2, h * HALF:(h + 1) * HALF], b[:, :], L2_EPS * L2_EPS, None,
                                                ALU.max)
                        B.read(ins, f"ss{n}")
                        B.emptied(dve, f"ss{n}", 0)
                        dve.sem_inc(s_nrm, 1)
                    dve.wait_ge(s_root, p + 1)
                    order(dve.reciprocal(tm[:, p % 2, :], tm[:, p % 2, :]))
                    order(dve.tensor_tensor(kkn[:, p, :], kkn[:, p, :], tm[:, p % 2, :], ALU.mult))
                    order(dve.tensor_scalar(tm[:, p % 2, :], ab[:, p, :], par[:, R_KA + p:R_KA + p + 1],
                                            omka[:, p:p + 1], ALU.mult, ALU.add))
                    order(dve.tensor_tensor(kT[:, p, :], kT[:, p, :], tm[:, p % 2, :], ALU.mult))
                    order(dve.scalar_tensor_tensor(ab[:, p, :], kkn[:, p, :], -1.0, ab[:, p, :], ALU.mult, ALU.mult))
                for p in range(NP):
                    if p >= 2:
                        B.result(dve, f"bs{2 * p - 3}", 0)
                    dve.scalar_tensor_tensor(tm[:, p % 2, :], rT[:, p, :], par[:, R_RK + p:R_RK + p + 1], kT[:, p, :],
                                             ALU.mult, ALU.mult).then_inc(s_prod, 1)
                    for n in (2 * p, 2 * p + 1):
                        b = B.result(dve, f"bs{n}", 0)
                        c = slice((n % 2) * HALF, (n % 2 + 1) * HALF)
                        B.read(dve.tensor_tensor(mix[:, p, c], b[:, :], vT[:, p, c], ALU.mult), f"bs{n}")
                B.result(dve, "v7", 0)
                for n in range(8):
                    p, c = n // 2, slice((n % 2) * HALF, (n % 2 + 1) * HALF)
                    b = B.result(dve, f"g{n}", 0)
                    B.emptied(dve, f"bs{n}", 0)
                    dve.scalar_tensor_tensor(mix[:, p, c], mix[:, p, c], par[:, R_GB + p:R_GB + p + 1], b[:, :],
                                             ALU.add, ALU.mult)
                    B.read(dve.tensor_scalar(vT[:, p, c], b[:, :], par[:, R_GG + p:R_GG + p + 1], None, ALU.mult), f"g{n}")
        B.end(1)

        gT = vT
        apad = at("apad", 88, [P, H, 2, P])
        NB = at("NB", 96, [P, H, 2, P])
        KB = at("KB", 104, [P, H, 2, P])
        X = at("X", 112, [P, H, P])
        XT = at("XT", 116, [P, H, P])
        Ts = at("Ts", 120, [P, H, P])
        alpha, rho, beta, kappa = (at(n, 124 + 2 * i, [P, NP, P]) for i, n in enumerate(("alpha", "rho", "beta", "kappa")))
        ein, einv, eex = (at(n, 132 + 2 * i, [P, NP, P]) for i, n in enumerate(("ein", "einv", "eex")))
        bt, kt_, rs_, us_ = (at(n, 138 + 2 * i, [P, W]) for i, n in enumerate(("bt", "kt", "rs", "us")))
        S, Sn = at("S", 146, [P, NP, P]), at("Sn", 148, [P, NP, P])
        oc, osq, on = at("oc", 150, [P, H, HD]), at("osq", 184, [P, H, HD]), at("on", 186, [P, H, HD])
        sgt, vtk = at("sgt", 188, [P, W]), at("vtk", 190, [P, W])
        sm = at("sm", 192, [P, 10, H])
        em, ec, fac, mean, var, rstd, expo = (sm[:, i, :] for i in range(7))
        table = [("cum0", 0), ("cum1", 1)]
        table += [(f"ab{g}", 2 + g) for g in range(4)] + [("kb0", 6), ("kb1", 7), ("kb2", 0), ("kb3", 1)]
        table += [("bt", 2), ("kt", 3), ("x0", 4), ("x1", 5)]
        for n in range(1, 7):
            for g in range(2):
                table.append((f"t{n}{g}", g))
            for g in range(2):
                if n < 6:
                    table.append((f"x{n}{g}", 2 + g))
                table.append((f"y{n}{g}", 4 + g))
        table += [("R", 6), ("U", 7), ("O", 6), ("S", 7), ("ot", 2)]
        C = Jobs(table)
        s_z5, s_seen = sem("s_z5"), sem("s_seen")
        (s_sgt, s_vtk, s_e, s_ec, s_prod5, s_pad, s_nbm, s_x1t, s_S, s_oc, s_osq, s_var, s_rstd, s_on) = (
            sem(f"s5_{n}") for n in ("sg", "v", "exp", "ec", "prod", "pad", "mask", "x1t", "S", "oc", "osq", "var",
                                     "rstd", "on"))
        up = cst[:, C_UP:C_UP + 2 * P].bitcast(U32).unsqueeze(1).to_broadcast([P, 2, 2 * P])
        with nc.Block() as block:
            def tiles(eng, body):
                body(0, 0)
                with eng.Fori(1, NT) as t:
                    body(t, 1)

            @block.sync
            def _(sp):
                def body(t, later):
                    if later:
                        C.result(sp, "cum1", t - 1)
                    sp.dma_start(sgt[:, :], sg_dram[bass.ds(t * P, P), :]).then_inc(s_sgt, 16)
                    if later:
                        C.result(sp, "S", t - 1)
                    sp.dma_start(vtk[:, :], v_dram[bass.ds(t * P, P), :]).then_inc(s_vtk, 16)
                tiles(sp, body)

            @block.gpsimd
            def _(pool):
                pool.memset(apad[:, :, :, :], 0.0)
                pool.memset(NB[:, :, :, :], 0.0)
                pool.memset(KB[:, :, :, :], 0.0)
                pool.memset(Sn[:, :, :], 0.0)
                pool.memset(ec, 1.0)
                pool.memset(expo, -0.5).then_inc(s_z5, 1)

                def body(t, later):
                    pool.wait_ge(s_var, t + 1)
                    pool.sem_inc(s_seen, 1)
                    pool.tensor_scalar(rstd, var, 1.0 / HD, GN_EPS, ALU.mult, ALU.add).then_inc(s_rstd, 1)
                    pool.wait_ge(s_rstd, 2 * t + 1)
                    pool.tensor_tensor(rstd, rstd, expo, ALU.pow).then_inc(s_rstd, 1)
                pool.wait_ge(s_z5, 1)
                tiles(pool, body)

            @block.tensor
            def _(pe):
                pe.wait_ge(s_z5, 1)

                def body(t, later):
                    pe.wait_ge(s_sgt, 16 * t + 16)
                    for j in range(2):
                        b = C.claim(pe, f"cum{j}", t)
                        for p in (2 * j, 2 * j + 1):
                            mm = pe.matmul(b[:, (p % 2) * 2 * P:(p % 2 + 1) * 2 * P], sgt[:, p * P:(p + 1) * P],
                                           cst[:, C_CUM:C_CUM + 2 * P], start=p % 2 == 0, stop=p % 2 == 1,
                                           skip_group_check=True)
                        C.done(mm, f"cum{j}")
                    pe.wait_ge(s_pad, 4 * t + 4)
                    pe.wait_ge(s_prod5, 4 * t + 4)
                    for kind, m in (("ab", beta), ("kb", kappa)):
                        for g in range(4):
                            b = C.claim(pe, f"{kind}{g}", t)
                            for h in (2 * g, 2 * g + 1):
                                mm = pe.matmul(b[:, (h % 2) * 2 * P:(h % 2 + 1) * 2 * P], m[:, h // 2, :],
                                               apad[:, h, :, :].rearrange("p a n -> p (a n)"), start=h % 2 == 0,
                                               stop=h % 2 == 1, skip_group_check=True)
                            C.done(mm, f"{kind}{g}")
                    for kind, m in (("bt", beta), ("kt", kappa)):
                        b = C.claim(pe, kind, t)
                        for p in range(NP):
                            mm = pe.transpose(b[:, p * P:(p + 1) * P], m[:, p, :], ident)
                        C.done(mm, kind)
                    pe.wait_ge(s_x1t, 2 * t + 2)
                    for g in range(2):
                        b = C.claim(pe, f"x{g}", t)
                        for j in range(4):
                            mm = pe.transpose(b[:, j * P:(j + 1) * P], XT[:, 4 * g + j, :], ident)
                        C.done(mm, f"x{g}")
                    for n in range(1, 7):
                        for g in range(2):
                            b = C.claim(pe, f"t{n}{g}", t)
                            C.emptied(pe, f"x{g}" if n == 1 else f"x{n - 1}{g}", t)
                            for j in range(4):
                                h = 4 * g + j
                                mm = pe.matmul(b[:, j * P:(j + 1) * P], NB[:, h, 0, :], X[:, h, :], start=j == 0,
                                               stop=j == 3, skip_group_check=True)
                            C.done(mm, f"t{n}{g}")
                        for g in range(2):
                            C.emptied(pe, f"t{n}{g}", t)
                            if n > 1:
                                C.emptied(pe, f"y{n - 1}{g}", t)
                            if n < 6:
                                b = C.claim(pe, f"x{n}{g}", t)
                                for j in range(4):
                                    h = 4 * g + j
                                    mm = pe.matmul(b[:, j * P:(j + 1) * P], XT[:, h, :], Ts[:, h, :], start=j == 0,
                                                   stop=j == 3, skip_group_check=True)
                                C.done(mm, f"x{n}{g}")
                            b = C.claim(pe, f"y{n}{g}", t)
                            for j in range(4):
                                h = 4 * g + j
                                mm = pe.matmul(b[:, j * P:(j + 1) * P], Ts[:, h, :], XT[:, h, :], start=j == 0,
                                               stop=j == 3, skip_group_check=True)
                            C.done(mm, f"y{n}{g}")
                    pe.wait_ge(s_S, t + 1)
                    pe.wait_ge(s_vtk, 16 * t + 16)
                    b = C.claim(pe, "R", t)
                    for p in range(NP):
                        pe.matmul(b[:, p * P:(p + 1) * P], alpha[:, p, :], S[:, p, :], start=p == 0, stop=False,
                                  skip_group_check=True)
                    for h in range(H):
                        mm = pe.matmul(b[:, h * HD:(h + 1) * HD], KB[:, h, 0, :], vtk[:, h * HD:(h + 1) * HD], start=False,
                                       stop=h == H - 1, skip_group_check=True)
                    C.done(mm, "R")
                    b = C.claim(pe, "U", t)
                    C.emptied(pe, "R", t)
                    for g in range(2):
                        C.emptied(pe, f"y6{g}", t)
                    for h in range(H):
                        mm = pe.matmul(b[:, h * HD:(h + 1) * HD], XT[:, h, :], rs_[:, h * HD:(h + 1) * HD], start=h == 0,
                                       stop=h == H - 1, skip_group_check=True)
                    C.done(mm, "U")
                    b = C.claim(pe, "O", t)
                    for p in range(NP):
                        pe.matmul(b[:, p * P:(p + 1) * P], rho[:, p, :], S[:, p, :], start=p == 0, stop=False,
                                  skip_group_check=True)
                    for h in range(H):
                        pe.matmul(b[:, h * HD:(h + 1) * HD], KB[:, h, 1, :], vtk[:, h * HD:(h + 1) * HD], start=False,
                                  stop=False, skip_group_check=True)
                    C.emptied(pe, "U", t)
                    for h in range(H):
                        mm = pe.matmul(b[:, h * HD:(h + 1) * HD], NB[:, h, 1, :], us_[:, h * HD:(h + 1) * HD], start=False,
                                       stop=h == H - 1, skip_group_check=True)
                    C.done(mm, "O")
                    b = C.claim(pe, "S", t)
                    C.emptied(pe, "kt", t)
                    for p in range(NP):
                        c = slice(p * P, (p + 1) * P)
                        pe.matmul(b[:, c], kt_[:, c], vtk[:, c], start=p == 0, stop=False, skip_group_check=True)
                    for p in range(NP):
                        c = slice(p * P, (p + 1) * P)
                        mm = pe.matmul(b[:, c], bt[:, c], us_[:, c], start=False, stop=p == NP - 1, skip_group_check=True)
                    C.done(mm, "S")
                    b = C.claim(pe, "ot", t)
                    pe.wait_ge(s_on, t + 1)
                    for p in range(NP):
                        mm = pe.transpose(b[:, p * P:(p + 1) * P], on[:, 2 * p:2 * p + 2, :].rearrange("p a n -> p (a n)"),
                                          ident)
                    C.done(mm, "ot")
                tiles(pe, body)

            @block.scalar
            def _(act):
                act.wait_ge(s_z5, 1)

                def body(t, later):
                    if later:
                        C.emptied(act, "ot", t - 1)
                    for j in range(2):
                        b = C.result(act, f"cum{j}", t)
                        v = b[:, :].rearrange("p (a n) -> p a n", a=2)
                        c = slice(2 * j, 2 * j + 2)
                        act.activation(ein[:, c, :], v[:, :, 0:P], ACT.Exp, scale=-DECAY)
                        act.activation(einv[:, c, :], v[:, :, 0:P], ACT.Exp, scale=DECAY)
                        act.activation(em[:, c], v[:, :, P], ACT.Exp, scale=DECAY)
                        ins = act.activation(eex[:, c, :], v[:, :, P:2 * P], ACT.Exp, scale=-DECAY)
                        C.read(ins, f"cum{j}")
                    act.wait_ge(s_prod5, 4 * t + 2)
                    for i, m in enumerate((alpha, rho)):
                        for e in range(2):
                            r = slice(HD * e, HD * e + HD)
                            act.activation(apad[r, e::2, i, :], m[r, :, :], ACT.Copy).then_inc(s_pad, 1)
                    for kind, m in (("bt", bt), ("kt", kt_)):
                        b = C.result(act, kind, t)
                        C.read(act.activation(m[:, :], b[:, :], ACT.Copy), kind)
                    for g in range(2):
                        b = C.result(act, f"x{g}", t)
                        C.read(act.activation(X[:, 4 * g:4 * g + 4, :].rearrange("p a n -> p (a n)"), b[:, :], ACT.Copy),
                               f"x{g}")
                    for kind, m in (("R", rs_), ("U", us_)):
                        b = C.result(act, kind, t)
                        C.read(act.activation(m[:, :], b[:, :], ACT.Copy), kind)
                    act.wait_ge(s_S, t + 1)
                    act.activation(ec[:, 0:NP], ein[:, :, P - 1], ACT.Copy).then_inc(s_ec, 1)
                    act.wait_ge(s_oc, t + 1)
                    act.activation(osq[:, :, :], oc[:, :, :], ACT.Square).then_inc(s_osq, 1)
                tiles(act, body)

            @block.vector
            def _(dve):
                order = Order(dve, "rec_order")
                dve.wait_ge(s_z5, 1)

                def body(t, later):
                    order.tile(t, 5)
                    c = bass.ds(t * P, P)
                    C.emptied(dve, "cum1", t)
                    dve.tensor_tensor(alpha[:, :, :], kkn[:, :, c], eex[:, :, :], ALU.mult).then_inc(s_prod5, 1)
                    dve.tensor_tensor(rho[:, :, :], rT[:, :, c], ein[:, :, :], ALU.mult).then_inc(s_prod5, 1)
                    dve.tensor_tensor(beta[:, :, :], ab[:, :, c], einv[:, :, :], ALU.mult).then_inc(s_prod5, 1)
                    dve.tensor_tensor(kappa[:, :, :], kT[:, :, c], einv[:, :, :], ALU.mult).then_inc(s_prod5, 1)
                    if later:
                        dve.wait_ge(s_ec, t)
                    order(dve.tensor_tensor(fac[:, 0:NP], ec[:, 0:NP], em[:, 0:NP], ALU.mult))
                    for p in range(NP):
                        ins = dve.scalar_tensor_tensor(S[:, p, :], Sn[:, p, :], fac[:, p:p + 1], ones_blk, ALU.mult,
                                                       ALU.mult)
                    ins.then_inc(s_S, 1)
                    for kind, m in (("ab", NB), ("kb", KB)):
                        for g in range(4):
                            b = C.result(dve, f"{kind}{g}", t)
                            dve.sem_inc(s_seen, 1)
                            ins = dve.copy_predicated(m[:, 2 * g:2 * g + 2, :, :].rearrange("p h a n -> p h (a n)"), up,
                                                      b[:, :].rearrange("p (h n) -> p h n", h=2))
                            C.read(ins, f"{kind}{g}")
                    C.emptied(dve, "kb3", t)
                    order(dve.tensor_tensor(Ts[:, :, :], NB[:, :, 0, :],
                                            cst[:, C_M1T:C_M1T + P].unsqueeze(1).to_broadcast([P, H, P]), ALU.mult))
                    for g in range(2):
                        dve.tensor_tensor(XT[:, 4 * g:4 * g + 4, :], Ts[:, 4 * g:4 * g + 4, :],
                                          ident.unsqueeze(1).to_broadcast([P, 4, P]), ALU.add).then_inc(s_x1t, 1)
                    for n in range(1, 7):
                        m = cst[:, C_LEV + (n - 1) * P:C_LEV + n * P].unsqueeze(1).to_broadcast([P, 4, P])
                        for g in range(2):
                            q = slice(4 * g, 4 * g + 4)
                            b = C.result(dve, f"t{n}{g}", t)
                            if n > 1:
                                C.result(dve, f"y{n - 1}{g}", t)
                            C.read(dve.tensor_tensor(Ts[:, q, :], b[:, :].rearrange("p (h n) -> p h n", h=4), m, ALU.mult),
                                   f"t{n}{g}")
                        for g in range(2):
                            q = slice(4 * g, 4 * g + 4)
                            if n < 6:
                                b = C.result(dve, f"x{n}{g}", t)
                                C.read(dve.tensor_tensor(X[:, q, :], b[:, :].rearrange("p (h n) -> p h n", h=4),
                                                         X[:, q, :], ALU.add), f"x{n}{g}")
                            b = C.result(dve, f"y{n}{g}", t)
                            C.read(dve.tensor_tensor(XT[:, q, :], b[:, :].rearrange("p (h n) -> p h n", h=4), XT[:, q, :],
                                                     ALU.add), f"y{n}{g}")
                    b = C.result(dve, "O", t)
                    o = b[:, :].rearrange("p (h n) -> p h n", h=H)
                    order(dve.tensor_reduce(mean, o, AX_X, ALU.add))
                    order(dve.tensor_scalar(mean, mean, 1.0 / HD, None, ALU.mult))
                    ins = dve.tensor_tensor(oc[:, :, :], o, mean.unsqueeze(2).to_broadcast([P, H, HD]), ALU.subtract)
                    C.read(ins, "O")
                    C.emptied(dve, "O", t)
                    dve.sem_inc(s_oc, 1)
                    b = C.result(dve, "S", t)
                    C.read(dve.tensor_tensor(Sn[:, :, :], b[:, :].rearrange("p (a n) -> p a n", a=NP), S[:, :, :],
                                             ALU.add), "S")
                    dve.wait_ge(s_osq, t + 1)
                    dve.tensor_reduce(var, osq[:, :, :], AX_X, ALU.add).then_inc(s_var, 1)
                    dve.wait_ge(s_rstd, 2 * t + 2)
                    dve.tensor_tensor(on[:, :, :], oc[:, :, :], rstd.unsqueeze(2).to_broadcast([P, H, HD]), ALU.mult
                                      ).then_inc(s_on, 1)
                    b = C.result(dve, "ot", t)
                    order(dve.tensor_tensor(oc[:, :, :].rearrange("p (a b) n -> p a (b n)", a=NP),
                                            b[:, :].rearrange("p (a n) -> p a n", a=NP), gT[:, :, c], ALU.mult))
                    C.read(dve.tensor_tensor(mix[:, 0:NP, c], oc[:, :, :].rearrange("p (a b) n -> p a (b n)", a=NP),
                                             mix[:, 0:NP, c], ALU.add), "ot")
                    C.emptied(dve, "ot", t)
                    C.emptied(dve, "S", t)
                tiles(dve, body)
        C.end(NT)

        mhi, mlo = at("mhi", 8, [P, KD, T], F32R), at("mlo", 40, [P, KD, T], F32R)
        x1 = at("x1", 72, [P, KD, T])
        xtok = at("xtok", 128, [P, 2, D])
        s_m, s_xt = sem("s_mhi"), [sem("s_xt0"), sem("s_xt1")]
        s_mlo = sem("s_mlo")
        X6 = Jobs([(f"{t}{g}", 2 * t + g) for t in range(2) for g in range(2)])
        with nc.Block() as block:
            @block.sync
            def _(sp):
                for t in range(NT):
                    if t >= 2:
                        X6.result(sp, f"{t % 2}1", t // 2 - 1)
                    sp.dma_start(xtok[:, t % 2, :], x[0, t * P:(t + 1) * P, :]).then_inc(s_xt[t % 2], 16)

            @block.tensor
            def _(pe):
                for t in range(NT):
                    pe.wait_ge(s_xt[t % 2], 16 * (t // 2) + 16)
                    for g in range(2):
                        b = X6.claim(pe, f"{t % 2}{g}", t // 2)
                        for k in range(4):
                            mm = pe.transpose(b[:, k * P:(k + 1) * P],
                                              xtok[:, t % 2, (4 * g + k) * P:(4 * g + k + 1) * P], ident)
                        X6.done(mm, f"{t % 2}{g}")

            @block.scalar
            def _(act):
                for k in range(KD):
                    act.activation(mhi[:, k, :], mix[:, k, :], ACT.Copy).then_inc(s_m, 1)

            @block.vector
            def _(dve):
                for t in range(NT):
                    for g in range(2):
                        b = X6.result(dve, f"{t % 2}{g}", t // 2)
                        X6.read(dve.tensor_copy(x1[:, 4 * g:4 * g + 4, t * P:(t + 1) * P],
                                                b[:, :].rearrange("p (a n) -> p a n", a=4)), f"{t % 2}{g}")
                    dve.wait_ge(s_m, t + 1)
                    dve.tensor_tensor(mlo[:, t, :], mix[:, t, :], mhi[:, t, :].bitcast(F32), ALU.subtract)
        X6.end(NT // 2)

        L = Layer("out", w_out_v, KD, 104, KD)
        with nc.Block() as block:
            @block.sync
            def _(sp):
                for s in range(2):
                    L.load(sp, s, 0, s * P, first=True)
                with sp.Fori(1, KD // 2) as i:
                    for s in range(2):
                        L.load(sp, s, i, (2 * i + s) * P)

            @block.scalar
            def _(act):
                for s in range(2):
                    L.split_hi(act, s, 0, first=True)
                with act.Fori(1, KD // 2) as i:
                    for s in range(2):
                        L.split_hi(act, s, i)

            @block.vector
            def _(dve):
                def add(s, turn):
                    for half in range(2):
                        b = L.J.result(dve, f"{s}{half}", turn)
                        v = x1[:, bass.ds(2 * turn + s, 1), half * HALF:(half + 1) * HALF].rearrange("p a n -> p (a n)")
                        L.J.read(dve.tensor_tensor(v, b[:, :], v, ALU.add), f"{s}{half}")

                for s in range(2):
                    L.split_lo(dve, s, 0)
                with dve.Fori(0, KD // 2 - 1) as i:
                    for s in range(2):
                        L.split_lo(dve, s, i + 1)
                        add(s, i)
                for s in range(2):
                    add(s, KD // 2 - 1)

            @block.tensor
            def _(pe):
                with pe.Fori(0, KD // 2) as i:
                    for s in range(2):
                        L.products(pe, s, i, mhi, mlo)
        L.J.end(KD // 2)

        h2hi, h2lo = at("h2hi", 8, [P, KD, T], F32R), at("h2lo", 40, [P, KD, T], F32R)
        xsq = at("xsq", 128, [P, 2, T])
        rsb = at("rsb", 136, [P, T])
        ht = at("ht", 140, [P, 2, T])
        s_xsq, s_rt, s_ht, s_hh2 = sem("s_xsq"), sem("s_rt"), sem("s_ht"), sem("s_hh2")
        N2 = Jobs([("0", 0), ("1", 1)])
        s_kd = sem("s_kd")
        with nc.Block() as block:
            @block.scalar
            def _(act):
                for k in range(KD):
                    if k >= 2:
                        act.wait_ge(s_kd, k - 1)
                    act.activation(xsq[:, k % 2, :], x1[:, k, :], ACT.Square).then_inc(s_xsq, 1)
                for half in range(2):
                    b = N2.result(act, f"{half}", 0)
                    N2.read(act.activation(rsb[:, half * HALF:(half + 1) * HALF], b[:, :], ACT.Sqrt,
                                           bias=small[:, 32:33], scale=1.0 / D), f"{half}")
                for k in range(KD):
                    act.wait_ge(s_ht, k + 1)
                    act.activation(h2hi[:, k, :], ht[:, k % 2, :], ACT.Copy).then_inc(s_hh2, 1)

            @block.tensor
            def _(pe):
                bs = [N2.claim(pe, f"{half}", 0) for half in range(2)]
                for k in range(KD):
                    pe.wait_ge(s_xsq, k + 1)
                    for half in range(2):
                        mm = pe.matmul(bs[half][:, :], ones, xsq[:, k % 2, half * HALF:(half + 1) * HALF], start=k == 0,
                                       stop=k == KD - 1, skip_group_check=True)
                        if k == KD - 1:
                            N2.done(mm, f"{half}")
                    if k < KD - 1:
                        mm.then_inc(s_kd, 1)

            @block.vector
            def _(dve):
                order = Order(dve, "n2_order")
                for half in range(2):
                    N2.emptied(dve, f"{half}", 0)
                order(dve.reciprocal(rsb[:, :], rsb[:, :]))
                for k in range(KD):
                    order(dve.scalar_tensor_tensor(ht[:, k % 2, :], x1[:, k, :], par[:, R_N2 + k:R_N2 + k + 1],
                                                   rsb[:, :], ALU.mult, ALU.mult))
                    dve.sem_inc(s_ht, 1)
                    dve.wait_ge(s_hh2, k + 1)
                    order(dve.tensor_tensor(h2lo[:, k, :], ht[:, k % 2, :], h2hi[:, k, :].bitcast(F32), ALU.subtract))
        N2.end(1)

        GM = max(GROUPS)
        hidhi, hidlo = at("hidhi", 152, [P, GM, T], F32R), at("hidlo", 152 + 4 * GM, [P, GM, T], F32R)
        sil, hid = at("sil", 128, [P, T]), at("hid", 132, [P, T])
        f0 = 0
        for gi, G in enumerate(GROUPS):
            L = Layer(f"gu{gi}", w_gu_v, KD, 104, 2 * G)
            s_sil, s_hid, s_hh7, s_hl7 = (sem(f"{n}{gi}") for n in ("s_sil", "s_hid", "s_hh7", "s_hl7"))
            with nc.Block() as block:
                @block.sync
                def _(sp):
                    for s in range(2):
                        L.load(sp, s, 0, s * FF + f0 * P, first=True)
                    with sp.Fori(1, G) as i:
                        for s in range(2):
                            L.load(sp, s, i, i * P + (s * FF + f0 * P))

                @block.scalar
                def _(act):
                    def hidden(turn, later):
                        if later:
                            act.wait_ge(s_hid, 2 * turn)
                        for half in range(2):
                            c = slice(half * HALF, (half + 1) * HALF)
                            b = L.J.result(act, f"0{half}", turn)
                            L.J.read(act.activation(sil[:, c], b[:, :], ACT.Silu), f"0{half}")
                        act.wait_ge(s_hid, 2 * turn + 2)
                        act.activation(hidhi[:, bass.ds(turn, 1), :].rearrange("p a n -> p (a n)"), hid[:, :], ACT.Copy
                                       ).then_inc(s_hh7, 1)

                    for s in range(2):
                        L.split_hi(act, s, 0, first=True)
                    for s in range(2):
                        L.split_hi(act, s, 1)
                    hidden(0, 0)
                    with act.Fori(1, G - 1) as i:
                        for s in range(2):
                            L.split_hi(act, s, i + 1)
                        hidden(i, 1)
                    hidden(G - 1, 1)

                @block.vector
                def _(dve):
                    def hidden(turn):
                        dve.wait_ge(s_hl7, turn + 1)
                        for half in range(2):
                            c = slice(half * HALF, (half + 1) * HALF)
                            L.J.emptied(dve, f"0{half}", turn)
                            b = L.J.result(dve, f"1{half}", turn)
                            L.J.read(dve.tensor_tensor(hid[:, c], b[:, :], sil[:, c], ALU.mult), f"1{half}")
                            L.J.emptied(dve, f"1{half}", turn)
                            dve.sem_inc(s_hid, 1)
                        dve.wait_ge(s_hh7, turn + 1)
                        dve.tensor_tensor(hidlo[:, bass.ds(turn, 1), :].rearrange("p a n -> p (a n)"), hid[:, :],
                                          hidhi[:, bass.ds(turn, 1), :].rearrange("p a n -> p (a n)").bitcast(F32),
                                          ALU.subtract).then_inc(s_hl7, 1)

                    dve.sem_inc(s_hl7, 1)
                    for s in range(2):
                        L.split_lo(dve, s, 0)
                    with dve.Fori(0, G - 1) as i:
                        for s in range(2):
                            L.split_lo(dve, s, i + 1)
                        hidden(i)
                    hidden(G - 1)

                @block.tensor
                def _(pe):
                    with pe.Fori(0, G) as i:
                        for s in range(2):
                            L.products(pe, s, i, h2hi, h2lo)
            L.J.end(G)

            L = Layer(f"dn{gi}", w_dn_v, G, 104, KD)
            with nc.Block() as block:
                @block.sync
                def _(sp):
                    for s in range(2):
                        L.load(sp, s, 0, s * P, rows=f0, first=True)
                    with sp.Fori(1, KD // 2) as i:
                        for s in range(2):
                            L.load(sp, s, i, (2 * i + s) * P, rows=f0)

                @block.scalar
                def _(act):
                    for s in range(2):
                        L.split_hi(act, s, 0, first=True)
                    with act.Fori(1, KD // 2) as i:
                        for s in range(2):
                            L.split_hi(act, s, i)

                @block.vector
                def _(dve):
                    def add(s, turn):
                        for half in range(2):
                            b = L.J.result(dve, f"{s}{half}", turn)
                            v = x1[:, bass.ds(2 * turn + s, 1), half * HALF:(half + 1) * HALF].rearrange("p a n -> p (a n)")
                            L.J.read(dve.tensor_tensor(v, b[:, :], v, ALU.add), f"{s}{half}")

                    for s in range(2):
                        L.split_lo(dve, s, 0)
                    with dve.Fori(0, KD // 2 - 1) as i:
                        for s in range(2):
                            L.split_lo(dve, s, i + 1)
                            add(s, i)
                    for s in range(2):
                        add(s, KD // 2 - 1)

                @block.tensor
                def _(pe):
                    with pe.Fori(0, KD // 2) as i:
                        for s in range(2):
                            L.products(pe, s, i, hidhi, hidlo)
            L.J.end(KD // 2)
            f0 += G

        gfin = at("gfin", 104, [P, D])
        xo = at("xo", 108, [P, 2, D])
        fin = at("fin", 116, [P, 2, D])
        st = at("st", 124, [P, 3, NT])
        s_gf, s_f1, s_f2, s_f3, s_out = sem("s_gf"), sem("s_f1"), sem("s_f2"), sem("s_f3"), [sem("s_out0"), sem("s_out1")]
        F = Jobs([(f"{t}{g}", 2 * t + g) for t in range(2) for g in range(2)])
        with nc.Block() as block:
            @block.sync
            def _(sp):
                sp.dma_start(gfin[:, :], norm_final_g.unsqueeze(0).to_broadcast([P, D])).then_inc(s_gf, 16)
                for t in range(NT):
                    sp.wait_ge(s_f3, t + 1)
                    sp.dma_start(out[0, t * P:(t + 1) * P, :], fin[:, t % 2, :]).then_inc(s_out[t % 2], 16)
                for n in range(2):
                    sp.wait_ge(s_out[n], 16 * NT // 2)

            @block.tensor
            def _(pe):
                for t in range(NT):
                    for g in range(2):
                        b = F.claim(pe, f"{t % 2}{g}", t // 2)
                        for k in range(4):
                            mm = pe.transpose(b[:, k * P:(k + 1) * P], x1[:, 4 * g + k, t * P:(t + 1) * P], ident)
                        F.done(mm, f"{t % 2}{g}")

            @block.scalar
            def _(act):
                for t in range(NT):
                    if t >= 2:
                        act.wait_ge(s_f3, t - 1)
                    for g in range(2):
                        b = F.result(act, f"{t % 2}{g}", t // 2)
                        F.read(act.activation(xo[:, t % 2, g * HALF:(g + 1) * HALF], b[:, :], ACT.Copy), f"{t % 2}{g}")
                    F.emptied(act, f"{t % 2}1", t // 2)
                    if t >= 2:
                        act.wait_ge(s_out[t % 2], 16 * (t // 2))
                    act.activation(fin[:, t % 2, :], xo[:, t % 2, :], ACT.Square, accum_out=st[:, 0, t:t + 1]
                                   ).then_inc(s_f1, 1)
                    act.wait_ge(s_f1, 2 * t + 1)
                    act.activation(st[:, 1, t:t + 1], st[:, 0, t:t + 1], ACT.Sqrt, bias=small[:, 32:33], scale=1.0 / D
                                   ).then_inc(s_f1, 1)

            @block.vector
            def _(dve):
                dve.wait_ge(s_gf, 16)
                for t in range(NT):
                    dve.wait_ge(s_f1, 2 * t + 2)
                    dve.reciprocal(st[:, 2, t:t + 1], st[:, 1, t:t + 1]).then_inc(s_f2, 1)
                    dve.wait_ge(s_f2, t + 1)
                    dve.scalar_tensor_tensor(fin[:, t % 2, :], xo[:, t % 2, :], st[:, 2, t:t + 1], gfin[:, :],
                                             ALU.mult, ALU.mult).then_inc(s_f3, 1)
        F.end(NT // 2)


_INS = ["x", "norm_mix_g", "w_in", "mu_shift", "w0", "w_up", "a0", "a_up", "g_up", "k_k", "k_a", "r_k", "gn_g", "gn_b",
        "sinks", "w_out", "norm_ffn_g", "w_gate_up", "w_down", "norm_final_g"]


def kernel(**inputs):
    import concourse.bacc as bacc
    from concourse.bass_utils import run_bass_kernel_spmd

    nc = bacc.Bacc("TRN2", target_bir_lowering=False, num_devices=1)
    arrays, args = {}, []
    given = {name: np.ascontiguousarray(inputs[name]) for name in _INS}
    given.update(consts=constants(), alibi=alibi())
    for name, a in given.items():
        arrays[f"in_{name}"] = a
        args.append(nc.dram_tensor(f"in_{name}", a.shape, mybir.dt.from_np(a.dtype), kind="ExternalInput").ap())
    args.append(nc.dram_tensor("out_0", (1, T, D), F32, kind="ExternalOutput").ap())
    hybrid_block(nc, *args)
    r = run_bass_kernel_spmd(nc, [arrays], core_ids=[0])
    return r.results[0]["out_0"]
```

```python
from contextlib import ExitStack

import numpy as np

import concourse.bass as bass
from concourse import mybir

ALU = mybir.AluOpType
ACT = mybir.ActivationFunctionType
AX_X = mybir.AxisListType.X
F32 = mybir.dt.float32
F32R = mybir.dt.float32r
U32 = mybir.dt.uint32

P = 128
T = 1024
D = 1024
NT = T // P
KD = D // P
HD = 64
H = 8
NP = H // 2
W = H * HD
NRW = 14
NAT = 6
NIN = NRW + NAT
FF = 2816
HALF = 512
GROUPS = [6, 6, 5, 5]
BAND = 192
DECAY = float(np.exp(-0.5))
EPS = 1e-6
GN_EPS = 64e-5
L2_EPS = 1e-12
NEG = -1e30
LEVELS = [1, 2, 4, 8, 16, 32, 64]

C_ID, C_CUM, C_UP, C_M1T, C_LEV, C_BLK, C_ONE, C_PAIR, C_END = np.cumsum([0, P, 2 * P, 2 * P, P, P * 6, P, P, 4]).tolist()
R_MU, R_A0, R_KK, R_KA, R_RK, R_GG, R_GB, R_N1, R_N2, R_END = np.cumsum(
    [0, NRW, NP, NP, NP, NP, NP, NP, KD, KD]).tolist()


def constants():
    s, t = np.arange(P)[:, None], np.arange(P)[None, :]
    mid = P // 2
    c = np.zeros((P, C_END), np.float32)
    c[:, C_ID:C_ID + P] = s == t
    c[:, C_CUM:C_CUM + P] = (s <= t).astype(np.float32) - (s < mid)
    c[:, C_CUM + P:C_CUM + 2 * P] = (s < t).astype(np.float32) - (s < mid)
    c[:, C_UP:C_UP + P] = s < t
    c[:, C_UP + P:C_UP + 2 * P] = s <= t

    def corner(b):
        return (s // (2 * b) == t // (2 * b)) & (s % (2 * b) >= b) & (t % (2 * b) < b)

    c[:, C_M1T:C_M1T + P] = corner(1).T
    for n, b in enumerate(LEVELS[1:]):
        c[:, C_LEV + n * P:C_LEV + (n + 1) * P] = corner(b)
    c[:, C_BLK:C_BLK + P] = s // HD == t // HD
    c[:, C_ONE:C_ONE + P] = 1
    c[:, C_PAIR:C_PAIR + 2] = s // HD == np.arange(2)[None, :]
    return c


def alibi():
    q, k = np.arange(P)[:, None], np.arange(BAND)[None, :] - HD
    seen = (k // HD <= q // HD) & (k // HD >= q // HD - 1)
    b = np.zeros((P, H * BAND), np.float32)
    for h in range(H):
        slope = np.float32(2.0 ** (-8.0 * (h + 1) / H))
        b[:, h * BAND:(h + 1) * BAND] = np.where(seen, -slope * np.abs(q - k), NEG)
    return b


def hybrid_block(nc, x, norm_mix_g, w_in, mu_shift, w0, w_up, a0, a_up, g_up, k_k, k_a, r_k, gn_g, gn_b,
                 sinks, w_out, norm_ffn_g, w_gate_up, w_down, norm_final_g, consts, bias_in, out):
    root = ExitStack()

    def sem(name):
        return root.enter_context(nc.semaphore(name))

    BASE = (nc.sbuf_base + 31) // 32 * 32
    K = 1024

    def at(name, kb, shape, dt=F32):
        return nc.alloc_sbuf_tensor_at(name, shape, dt, offset=BASE + int(kb * K))

    w_in_v = w_in[0].rearrange("(k p) n -> p k n", p=P)
    w_out_v = w_out[0].rearrange("(k p) n -> p k n", p=P)
    w_gu_v = w_gate_up[0].rearrange("(k p) n -> p k n", p=P)
    w_dn_v = w_down[0].rearrange("(k p) n -> p k n", p=P)
    sg_dram = nc.dram_tensor("sg_scratch", (T, W), F32, kind="Internal").ap()
    v_dram = nc.dram_tensor("v_scratch", (T, W), F32, kind="Internal").ap()

    with root:
        bank = [root.enter_context(nc.psum_tensor(f"bank{b}", [P, HALF], F32)) for b in range(8)]
        full = [sem(f"bank_full{b}") for b in range(8)]
        free = [sem(f"bank_free{b}") for b in range(8)]

        class Jobs:
            base = [0] * 8

            def __init__(self, table, ahead=()):
                table = list(table) + list(ahead)
                self.bank_of, self.nth, self.per = dict(table), {}, [0] * 8
                for job, b in table:
                    self.nth[job] = self.per[b]
                    self.per[b] += 1
                self.start = list(Jobs.base)
                for _, b in ahead:
                    self.start[b] += 1

            def end(self, tiles):
                for b in range(8):
                    Jobs.base[b] += self.per[b] * tiles

            def before(self, job, t):
                b = self.bank_of[job]
                return t * self.per[b] + (self.start[b] + self.nth[job])

            def claim(self, pe, job, t):
                b = self.bank_of[job]
                pe.wait_ge(free[b], self.before(job, t))
                return bank[b]

            def done(self, mm, job):
                mm.then_inc(full[self.bank_of[job]], 1)

            def result(self, eng, job, t):
                b = self.bank_of[job]
                eng.wait_ge(full[b], self.before(job, t) + 1)
                return bank[b]

            def emptied(self, eng, job, t):
                eng.wait_ge(free[self.bank_of[job]], self.before(job, t) + 1)

            def read(self, ins, job):
                ins.then_inc(free[self.bank_of[job]], 1)

        class Order:

            def __init__(self, eng, name):
                self.eng, self.sem, self.n, self.turn, self.per = eng, sem(name), 0, 0, 0

            def __call__(self, ins):
                ins.then_inc(self.sem, 1)
                self.n += 1
                self.eng.wait_ge(self.sem, self.turn + self.n)

            def tile(self, t, per):
                assert self.per in (0, per) and (not self.per or self.n == self.origin + per)
                if not self.per:
                    self.origin, self.per = self.n, per
                self.turn, self.n = t * per, self.origin

            def leave(self, tiles):
                assert self.n == self.origin + self.per
                self.n, self.turn, self.per = self.origin + self.per * tiles, 0, 0

        cst = at("cst", 0, [P, C_END])
        par = at("par", 7.0625, [P, R_END])
        small = at("small", 7.375, [P, 128])
        omka = small[:, 40:40 + NP]
        rn = small[:, 64:128]
        ident = cst[:, C_ID:C_ID + P]
        ones_blk = cst[:, C_BLK:C_BLK + P]
        ones = cst[:, C_ONE:C_ONE + P]
        rkv = at("rkv", 8, [P, 12, T])
        rT, kT, vT = rkv[:, 0:4, :], rkv[:, 4:8, :], rkv[:, 8:12, :]
        hhi, hlo = at("hhi", 56, [P, KD, T], F32R), at("hlo", 88, [P, KD, T], F32R)
        wg = at("wg", 120, [P, 2, T])
        att = at("att", 128, [P, NP, T])
        vt = at("vt", 144, [P, NT + 1, P])
        RING1 = 152
        praw = at("praw", 176, [P, 2, 4 + T])
        pdif = at("pdif", 184.25, [P, T])
        vpad = at("vpad", 176, [P, HD + T + HD])
        xin = at("xin", 188.5, [P, 3, D])
        kk2 = at("kk2", 188.5, [P, 2, HD + T])
        qst = at("qst", 197, [P, H, P])
        rsb = at("rsb", 201, [P, T])
        dg = at("dg", 205, [P, P])
        prow = at("prow", 205.5, [P, P])
        kkn = at("kkn", 56, [P, NP, T])
        ab = at("ab", 72, [P, NP, T])
        lora = at("lora", 88, [P, 4, W])
        bias = at("bias", 96, [P, H, BAND])
        pt = at("pt", 108, [P, 2, 2, 2, P])
        tm = at("tm", 112, [P, 2, HALF])
        sgo = at("sgo", 116, [P, 2, W])
        vst = at("vst", 148.5, [P, 2, P])
        vo = at("vo", 149.5, [P, W])
        st8 = at("st8", 151.5, [P, 6, H])
        snk = at("snk", 151.75, [P, H])
        mix = at("mix", 152, [P, 8, T])
        prod = at("prod", 184, [P, 2, HALF])
        sb = [at("scores0", 102, [P, H, BAND]), at("scores1", 201, [P, H, BAND])]
        rnx = at("rnx", 116, [P, 2, 4, 2, HD])
        gT = vT
        apad = at("apad", 88, [P, H, 2, P])
        NB = at("NB", 96, [P, H, 2, P])
        KB = at("KB", 104, [P, H, 2, P])
        X = at("X", 112, [P, H, P])
        XT = at("XT", 116, [P, H, P])
        Ts = at("Ts", 120, [P, H, P])
        alpha, rho, beta, kappa = (at(n, 124 + 2 * i, [P, NP, P]) for i, n in enumerate(("alpha", "rho", "beta", "kappa")))
        ein, einv, eex = (at(n, 132 + 2 * i, [P, NP, P]) for i, n in enumerate(("ein", "einv", "eex")))
        bt, kt_, rs_, us_ = (at(n, 138 + 2 * i, [P, W]) for i, n in enumerate(("bt", "kt", "rs", "us")))
        S, Sn = at("S", 146, [P, NP, P]), at("Sn", 148, [P, NP, P])
        oc, osq, on = at("oc", 150, [P, H, HD]), at("osq", 184, [P, H, HD]), at("on", 186, [P, H, HD])
        sgt, vtk = at("sgt", 188, [P, W]), at("vtk", 190, [P, W])
        sm = at("sm", 192, [P, 10, H])
        em, ec, fac, mean, var, rstd, expo = (sm[:, i, :] for i in range(7))
        mhi, mlo = at("mhi", 8, [P, KD, T], F32R), at("mlo", 40, [P, KD, T], F32R)
        x1 = at("x1", 72, [P, KD, T])
        RING2 = 104
        xtok = at("xtok", 196, [P, 2, D])
        GM = max(GROUPS)
        x1hi, x1lo = at("x1hi", 128, [P, KD, T], F32R), at("x1lo", 160, [P, KD, T], F32R)
        xsq = at("xsq", 192, [P, 2, T])
        dg2 = at("dg2", 192, [P, NT, P])
        rsb2 = at("rsb2", 200, [P, T])
        rms2 = small[:, 48:56]
        hidhi, hidlo = at("hidhi", 8, [P, GM, T], F32R), at("hidlo", 8 + 4 * GM, [P, GM, T], F32R)
        sil, hid, gat = at("sil", 192, [P, T]), at("hid", 196, [P, T]), at("gat", 56, [P, T])
        gfin = at("gfin", 8, [P, D])
        xo = at("xo", 12, [P, 2, D])
        fin = at("fin", 20, [P, 2, D])
        st = at("st", 28, [P, 3, NT])

        class Ring:
            def __init__(self, tag, kb):
                self.turns = 0
                self.raw = at(f"{tag}_raw", kb, [P, 2, KD, P])
                self.hi = at(f"{tag}_whi", kb + 8, [P, 2, KD, P], F32R)
                self.lo = at(f"{tag}_wlo", kb + 16, [P, 2, KD, P], F32R)
                self.landed = [sem(f"{tag}_landed{s}") for s in range(2)]
                self.hi_ready = sem(f"{tag}_hi")
                self.lo_ready = sem(f"{tag}_lo")

        class Layer:
            def __init__(self, ring, view, kt, turns):
                self.ring, self.view, self.kt, self.t0, self.n = ring, view, kt, ring.turns, turns
                ring.turns += turns
                self.J = Jobs([(f"{s}{h}", 2 * s + h) for s in range(2) for h in range(2)])
                self.J.end(turns)

            def load(self, sp, s, turn, column, rows=0, first=False):
                if not first:
                    sp.wait_ge(self.ring.lo_ready, 2 * turn + (2 * self.t0 + s - 1))
                sp.dma_start(self.ring.raw[:, s, 0:self.kt, :], self.view[:, rows:rows + self.kt, bass.ds(column, P)]
                             ).then_inc(self.ring.landed[s], 16)

            def split_hi(self, act, s, turn, first=False):
                act.wait_ge(self.ring.landed[s], 16 * turn + (16 * self.t0 + 16))
                if not first:
                    act.wait_ge(full[2 * s + 1], self.J.before(f"{s}1", turn))
                act.activation(self.ring.hi[:, s, 0:self.kt, :], self.ring.raw[:, s, 0:self.kt, :], ACT.Copy
                               ).then_inc(self.ring.hi_ready, 1)

            def split_lo(self, dve, s, turn):
                dve.wait_ge(self.ring.hi_ready, 2 * turn + (2 * self.t0 + s + 1))
                dve.tensor_tensor(self.ring.lo[:, s, 0:self.kt, :], self.ring.raw[:, s, 0:self.kt, :],
                                  self.ring.hi[:, s, 0:self.kt, :].bitcast(F32), ALU.subtract
                                  ).then_inc(self.ring.lo_ready, 1)

            def products(self, pe, s, turn, ahi, alo, ready=None):
                pe.wait_ge(self.ring.lo_ready, 2 * turn + (2 * self.t0 + s + 1))
                for half in range(2):
                    o = self.J.claim(pe, f"{s}{half}", turn)
                    c = slice(half * HALF, half * HALF + HALF)
                    n, i = 3 * self.kt, 0
                    for k in range(self.kt):
                        if ready is not None and half == 0:
                            ready(k)
                        for wpart, apart in ((self.ring.hi, ahi), (self.ring.hi, alo), (self.ring.lo, ahi)):
                            mm = pe.matmul(o[:, :], wpart[:, s, k, :], apart[:, k, c], start=i == 0, stop=i == n - 1)
                            i += 1
                    self.J.done(mm, f"{s}{half}")

            def products_late(self, pe, turn, ahi, alo, ready, between=None):
                def tile(s, half, k):
                    o = bank[2 * s + half]
                    c = slice(half * HALF, half * HALF + HALF)
                    for i, (wpart, apart) in enumerate(((self.ring.hi, ahi), (self.ring.hi, alo), (self.ring.lo, ahi))):
                        mm = pe.matmul(o[:, :], wpart[:, s, k, :], apart[:, k, c], start=k == 0 and i == 0,
                                       stop=k == self.kt - 1 and i == 2)
                    return mm

                for s in range(2):
                    pe.wait_ge(self.ring.lo_ready, 2 * turn + (2 * self.t0 + s + 1))
                    for half in range(2):
                        self.J.claim(pe, f"{s}{half}", turn)
                        for k in range(self.kt - 1):
                            if s == half == 0:
                                ready(k)
                            tile(s, half, k)
                    if between:
                        between(s)
                ready(self.kt - 1)
                for s in range(2):
                    for half in range(2):
                        self.J.done(tile(s, half, self.kt - 1), f"{s}{half}")

        ring1, ring2 = Ring("ring1", RING1), Ring("ring2", RING2)

        def row(ap):
            return ap.rearrange("p a n -> p (a n)")

        s_cst, s_cst2, s_par = sem("s_cst"), sem("s_cst2"), sem("s_par")
        s_x = [sem(f"s_x{n}") for n in range(3)]
        s_ss, s_sq, s_rs, s_c0, s_dg, s_hh, s_xr = (sem(f"s1_{n}") for n in ("ss", "sq", "rs", "c0", "dg", "hh", "xr"))
        J1 = Jobs([("par", 7)])
        J1.end(1)
        J = Jobs([("x00", 0), ("x01", 1), ("x10", 2), ("x11", 3)])
        J.end(NT // 2)
        JR = Jobs([("rs0", 4), ("rs1", 5)])
        JR.end(1)
        IN = Layer(ring1, w_in_v, KD, NIN // 2)
        nsh = NRW // 2

        def stage1_sync(sp):
            sp.dma_start(cst[:, C_ID:C_ID + P], consts[:, C_ID:C_ID + P]).then_inc(s_cst, 16)
            for t in range(2):
                sp.dma_start(xin[:, t, :], x[0, t * P:(t + 1) * P, :]).then_inc(s_x[t], 16)
            rows = [(mu_shift, R_MU, NRW), (a0, R_A0, NP), (k_k, R_KK, NP), (k_a, R_KA, NP), (r_k, R_RK, NP),
                    (gn_g, R_GG, NP), (gn_b, R_GB, NP), (norm_mix_g, R_N1, KD), (norm_ffn_g, R_N2, KD)]
            for a, r, n in rows:
                v = a[0] if len(a.shape) == 2 else a[0].rearrange("h n -> (h n)")
                sp.dma_start(prow[r:r + n, :], v.rearrange("(j p) -> j p", p=P)).then_inc(s_par, 16)
            sp.dma_start(xin[:, 2, :], x[0, 2 * P:3 * P, :]).then_inc(s_x[2], 16)
            sp.dma_start(cst[:, C_CUM:], consts[:, C_CUM:]).then_inc(s_cst2, 16)
            for s in range(2):
                IN.load(sp, s, 0, s * P, first=True)
            for t in range(3, NT):
                J.result(sp, f"x{(t - 3) % 2}1", (t - 3) // 2)
                sp.wait_ge(s_ss, t - 2)
                sp.dma_start(xin[:, t % 3, :], x[0, t * P:(t + 1) * P, :]).then_inc(s_x[t % 3], 16)

        def stage1_scalar(act):
            act.wait_ge(s_c0, 1)
            J1.emptied(act, "par", 0)
            for t in range(NT):
                act.wait_ge(s_x[t % 3], 16 * (t // 3) + 16)
                if t:
                    act.wait_ge(s_ss, t)
                act.activation(praw[:, 0, 0:D], xin[:, t % 3, :], ACT.Square, accum_out=small[:, t:t + 1]).then_inc(s_ss, 1)
                for g in range(2):
                    b = J.result(act, f"x{t % 2}{g}", t // 2)
                    for k in range(4):
                        f = 4 * g + k
                        ins = act.activation(hhi[:, f, t * P:(t + 1) * P], b[:, k * P:(k + 1) * P], ACT.Copy,
                                             scale=par[:, R_N1 + f:R_N1 + f + 1])
                    ins.then_inc(s_hh, 1)
                if t == 3:
                    for s in range(2):
                        IN.split_hi(act, s, 0, first=True)
            act.wait_ge(s_ss, NT)
            act.activation(small[:, 8:16], small[:, 0:8], ACT.Sqrt, bias=small[:, 32:33], scale=1.0 / D).then_inc(s_sq, 1)

        def stage1_tensor(pe):
            pe.wait_ge(s_cst, 16)
            for t in range(NT):
                pe.wait_ge(s_x[t % 3], 16 * (t // 3) + 16)
                for g in range(2):
                    b = J.claim(pe, f"x{t % 2}{g}", t // 2)
                    for k in range(4):
                        mm = pe.transpose(b[:, k * P:(k + 1) * P], xin[:, t % 3, (4 * g + k) * P:(4 * g + k + 1) * P],
                                          ident)
                    J.done(mm, f"x{t % 2}{g}")
                if t == 0:
                    pe.wait_ge(s_par, 9 * 16)
                    b = J1.claim(pe, "par", 0)
                    J1.done(pe.transpose(b[:, 0:R_END], prow[0:R_END, :], ident[0:R_END, 0:R_END]), "par")
            pe.wait_ge(s_cst2, 16)
            for t in range(NT):
                if t % 4 == 0:
                    b = JR.claim(pe, f"rs{t // 4}", 0)
                pe.wait_ge(s_dg, t + 1)
                mm = pe.matmul(b[:, (t % 4) * P:(t % 4 + 1) * P], ones, dg[:, :], start=t % 4 == 0, stop=t % 4 == 3,
                               skip_group_check=True)
                if t % 4 == 3:
                    JR.done(mm, f"rs{t // 4}")
                else:
                    mm.then_inc(s_xr, 1)

        def stage1_vector(dve):
            dve.memset(small[:, 32:33], EPS).then_inc(s_c0, 1)
            b = J1.result(dve, "par", 0)
            J1.read(dve.tensor_copy(par[:, :], b[:, 0:R_END]), "par")
            J1.emptied(dve, "par", 0)
            for t in range(NT):
                for g in range(2):
                    b = J.result(dve, f"x{t % 2}{g}", t // 2)
                    dve.wait_ge(s_hh, 2 * t + g + 1)
                    for k in range(4):
                        f = 4 * g + k
                        c = slice(t * P, (t + 1) * P)
                        ins = dve.scalar_tensor_tensor(hlo[:, f, c], b[:, k * P:(k + 1) * P],
                                                       par[:, R_N1 + f:R_N1 + f + 1], hhi[:, f, c].bitcast(F32),
                                                       ALU.mult, ALU.subtract)
                    J.read(ins, f"x{t % 2}{g}")
                if t == 4:
                    for s in range(2):
                        IN.split_lo(dve, s, 0)
            order = Order(dve, "rs_order")
            dve.wait_ge(s_sq, 1)
            order(dve.reciprocal(small[:, 16:24], small[:, 8:16]))
            for t in range(NT):
                if t:
                    if t % 4:
                        dve.wait_ge(s_xr, t - t // 4)
                    else:
                        JR.result(dve, f"rs{t // 4 - 1}", 0)
                dve.tensor_scalar(dg[:, :], ident, small[:, 16 + t:17 + t], None, ALU.mult).then_inc(s_dg, 1)
            for n in range(2):
                b = JR.result(dve, f"rs{n}", 0)
                JR.read(dve.tensor_copy(rsb[:, n * HALF:(n + 1) * HALF], b[:, :]), f"rs{n}")
            JR.emptied(dve, "rs1", 0)

        s_shift, s_praw, s_att, s_z2, s_ks = sem("s_shift"), sem("s_praw"), sem("s_att"), sem("s_z2"), sem("s_ks")
        s_wd, s_gd, s_vt0 = sem("s_wd"), sem("s_gd"), sem("s_vt0")
        VT = Jobs([("vt0", 4), ("vt1", 5), ("vt2", 6)])
        VT.end(1)

        def stage2_sync(sp):
            with sp.Fori(1, nsh) as i:
                for s in range(2):
                    IN.load(sp, s, i, (2 * i + s) * P)
            for s in range(2):
                IN.load(sp, s, nsh, (NRW + NP + s) * P)
            with sp.Fori(nsh + 1, NIN // 2) as i:
                for s in range(2):
                    IN.load(sp, s, i, (2 * i + s - 2) * P)
            sp.wait_ge(s_att, 2)
            for e in range(2):
                sp.dma_start(kk2[HD * e:HD * e + HD, 1, :], kk2[HD - HD * e:P - HD * e, 0, :]).then_inc(s_ks, 16)

        def stage2_gpsimd(pool):
            pool.wait_ge(s_ss, NT)
            J.result(pool, "x11", NT // 2 - 1)
            pool.memset(kk2[:, 0, 0:HD], 0.0)
            pool.memset(qst[:, :, :], 0.0).then_inc(s_z2, 1)

        def stage2_scalar(act):
            with act.Fori(1, NIN // 2) as i:
                for s in range(2):
                    IN.split_hi(act, s, i)
            act.wait_ge(s_shift, NRW + 1)
            act.activation(wg[0:HD, 0, :], wg[0:HD, 0, :], ACT.Tanh).then_inc(s_wd, 1)
            act.activation(wg[:, 1, :], wg[:, 1, :], ACT.Sigmoid).then_inc(s_gd, 1)
            for n in range(3):
                b = VT.result(act, f"vt{n}", 0)
                m = min(4, NT + 1 - 4 * n)
                VT.read(act.activation(vt[:, 4 * n:4 * n + m, :], b[:, 0:m * P], ACT.Copy), f"vt{n}")

        def stage2_vector(dve):
            order = Order(dve, "shift_order")
            order(dve.memset(praw[:, :, 0:4], 0.0))
            dve.sem_inc(s_shift, 1)

            def normed(dst, s, half, turn):
                b = IN.J.result(dve, f"{s}{half}", turn)
                IN.J.read(dve.tensor_tensor(dst, b[:, :], rsb[:, half * HALF:(half + 1) * HALF], ALU.mult), f"{s}{half}")

            def shift(s, turn, dst, mu):
                dve.wait_ge(s_shift, 2 * turn + (s + 1))
                for half in range(2):
                    normed(praw[:, s, 4 + half * HALF:4 + (half + 1) * HALF], s, half, turn)
                IN.J.emptied(dve, f"{s}0", turn)
                IN.J.emptied(dve, f"{s}1", turn)
                order(dve.tensor_tensor(pdif[:, :], praw[:, s, 3:3 + T], praw[:, s, 4:4 + T], ALU.subtract))
                dve.scalar_tensor_tensor(dst, pdif[:, :], mu, praw[:, s, 4:4 + T], ALU.mult, ALU.add
                                         ).then_inc(s_shift, 1)

            with dve.Fori(0, nsh - 1) as i:
                order.tile(i, 2)
                for s in range(2):
                    IN.split_lo(dve, s, i + 1)
                    shift(s, i, row(rkv[:, bass.ds(2 * i + s, 1), :]), par[:, bass.ds(2 * i + (s + R_MU), 1)])
            order.leave(nsh - 1)
            for s in range(2):
                IN.split_lo(dve, s, nsh)
                shift(s, nsh - 1, wg[:, s, :], par[:, R_MU + 12 + s:R_MU + 13 + s])
            dve.wait_ge(s_shift, NRW + 1)
            order(dve.memset(vpad[:, 0:HD], 0.0))
            order(dve.memset(vpad[:, HD + T:], 0.0))
            dve.wait_ge(s_z2, 1)
            for s, dst in ((0, kk2[:, 0, HD:]), (1, vpad[:, HD:HD + T])):
                IN.split_lo(dve, s, nsh + 1)
                for half in range(2):
                    normed(dst[:, half * HALF:(half + 1) * HALF], s, half, nsh)
                IN.J.emptied(dve, f"{s}0", nsh)
                IN.J.emptied(dve, f"{s}1", nsh)
                dve.sem_inc(s_att, 2)
            with dve.Fori(nsh + 1, NIN // 2 - 1) as i:
                for s in range(2):
                    IN.split_lo(dve, s, i + 1)
                    for half in range(2):
                        normed(row(att[:, bass.ds(2 * i + (s - 2 * nsh - 2), 1), half * HALF:(half + 1) * HALF]), s, half, i)
            for s in range(2):
                for half in range(2):
                    normed(att[:, 2 + s, half * HALF:(half + 1) * HALF], s, half, NIN // 2 - 1)

        def stage2_tensor(pe):
            for s in range(2):
                for g in range(2):
                    J.emptied(pe, f"x{s}{g}", NT // 2 - 1)
            with pe.Fori(0, NIN // 2 - 1) as i:
                for s in range(2):
                    IN.products(pe, s, i, hhi, hlo)
            pe.wait_ge(s_att, 4)
            for n in range(3):
                b = VT.claim(pe, f"vt{n}", 0)
                m = min(4, NT + 1 - 4 * n)
                for j in range(m):
                    mm = pe.transpose(b[:, j * P:(j + 1) * P], vpad[:, (4 * n + j) * P:(4 * n + j + 1) * P], ident)
                VT.done(mm, f"vt{n}")
            for s in range(2):
                IN.products(pe, s, NIN // 2 - 1, hhi, hlo)
            pe.wait_ge(s_shift, NRW + 1)

        s_lz, s_lora, s_sgo, s_vd = sem("s_lz"), sem("s_lora"), sem("s_sgo"), sem("s_vd")
        s_sgd = [sem("s_sgd0"), sem("s_sgd1")]
        s_rnx, s_tm, s_gm = sem("s4_rnx"), sem("s4_tm"), sem("s4_gm")
        s_kkr, s_sqr, s_nrm, s_root, s_rn, s_prod = (sem(f"s4_{n}") for n in ("kkr", "sq", "nrm", "root", "rn", "prod"))
        s_bias, s_snk, s_zp = sem("s_bias"), sem("s_snk"), sem("s_zp")
        s_q, s_st, s_sc, s_mx, s_pe, s_pn, s_pv = (sem(f"s3_{n}") for n in ("q", "v", "sc", "mx", "exp", "norm", "pv"))
        B = Jobs([(f"a{n}", n) for n in range(8)] + [(f"v{n}", n) for n in range(8)] + [("ss", 0)]
                 + [(f"sg{n}", n) for n in range(8)])
        B.end(1)
        A = Jobs([(f"pt{p}", 4 + p % 2) for p in range(NP)] + [("pv", 6)],
                 [(f"sc{p}", p) for p in range(NP)] + [("rn", 0), ("g", 7), ("bs", 1)])
        A.end(NT)

        def pipelined(eng, body):
            body(-1, False, True)
            with eng.Fori(0, NT - 1) as t:
                body(t, True, True)
            body(NT - 1, True, False)

        def straight(eng, body):
            for t in range(-1, NT):
                body(t, t >= 0, t < NT - 1)

        def unit(n):
            return n // 2, slice((n % 2) * HALF, (n % 2 + 1) * HALF)

        def stage3_sync(sp):
            IN.J.result(sp, "11", IN.n - 1)
            sp.wait_ge(s_lz, 1)
            sp.dma_start(lora[HD:P, 1, :], a_up[0]).then_inc(s_lora, 16)
            sp.dma_start(lora[0:HD, 0, :], w_up[0]).then_inc(s_lora, 16)
            sp.dma_start(lora[:, 3, :], w0.to_broadcast([P, W])).then_inc(s_lora, 16)
            sp.dma_start(lora[:, 2, :], g_up[0]).then_inc(s_lora, 16)
            sp.dma_start(bias[:, :, :], bias_in.rearrange("p (h n) -> p h n", h=H)).then_inc(s_bias, 16)
            sp.dma_start(snk[:, :], sinks.to_broadcast([P, H])).then_inc(s_snk, 16)
            for n in range(NT):
                B.emptied(sp, f"v{n}", 0)
                sp.dma_start(v_dram[n * P:(n + 1) * P, :], vo[:, :]).then_inc(s_vd, 16)
            for n in range(NT):
                sp.wait_ge(s_sgo, n + 1)
                sp.dma_start(sg_dram[n * P:(n + 1) * P, :], sgo[:, n % 2, :]).then_inc(s_sgd[n % 2], 16)

        def stage3_gpsimd(pool):
            IN.J.result(pool, "11", IN.n - 1)
            pool.memset(lora[:, 0:2, :], 0.0).then_inc(s_lz, 1)
            pool.wait_ge(s_lz, 1)
            pool.memset(pt[:, :, :, :, :], 0.0).then_inc(s_zp, 1)
            pool.wait_ge(s_zp, 1)
            IN.J.emptied(pool, "11", IN.n - 1)
            IN.J.emptied(pool, "01", IN.n - 1)
            IN.J.emptied(pool, "10", IN.n - 1)
            IN.J.emptied(pool, "00", IN.n - 1)

            def body(t, live, more):
                if more:
                    if live:
                        A.result(pool, f"sc{NP - 1}", t - 1)
                    for e in range(2):
                        if e:
                            pool.wait_ge(s_q, 2 * t + 3)
                        elif t > 0:
                            pool.wait_ge(s_st, t)
                        r = slice(HD * e, HD * e + HD)
                        pool.tensor_copy(qst[r, e::2, :], att[r, :, (t + 1) * P:(t + 2) * P]).then_inc(s_q, 1)
                if live:
                    if t:
                        A.result(pool, "pv", t - 1)
                    pool.wait_ge(s_q, 2 * min(t + 2, NT))
                    if t and not more:
                        pool.wait_ge(s_st, t)
                    pool.tensor_copy(vst[:, :, :], vt[:, t:t + 2, :]).then_inc(s_st, 1)
            VT.emptied(pool, "vt2", 0)
            straight(pool, body)

        def stage3_tensor(pe):
            pe.wait_ge(s_lora, 4 * 16)
            pe.wait_ge(s_wd, 1)
            for n in range(8):
                b = B.claim(pe, f"a{n}", 0)
                B.done(pe.matmul(b[:, :], lora[:, 1, (n // 2) * P:(n // 2 + 1) * P],
                                 wg[:, 0, (n % 2) * HALF:(n % 2 + 1) * HALF], start=True, stop=True), f"a{n}")
            for n in range(8):
                b = B.claim(pe, f"v{n}", 0)
                for p in range(NP):
                    mm = pe.transpose(b[:, p * P:(p + 1) * P], vT[:, p, n * P:(n + 1) * P], ident)
                B.done(mm, f"v{n}")
            b = B.claim(pe, "ss", 0)
            pe.wait_ge(s_sqr, NP)
            for t in range(NT):
                for p in range(NP):
                    mm = pe.matmul(b[:, 8 * t + 2 * p:8 * t + 2 * p + 2], mix[:, p, t * P:(t + 1) * P],
                                   cst[:, C_PAIR:C_PAIR + 2], start=t == 0 and p == 0, stop=t == NT - 1 and p == NP - 1,
                                   skip_group_check=True)
            B.done(mm, "ss")
            for n in range(8):
                b = B.claim(pe, f"sg{n}", 0)
                B.done(pe.matmul(b[:, :], wg[:, 0, n * P:(n + 1) * P], lora[:, 0, :], start=True, stop=True), f"sg{n}")
            pe.wait_ge(s_ks, 32)
            pe.wait_ge(s_zp, 1)
            pe.wait_ge(s_gd, 1)

            def body(t, live, more):
                n = t + 1
                if more:
                    pe.wait_ge(s_q, 2 * t + 4)
                    for p in range(NP):
                        b = A.claim(pe, f"sc{p}", t)
                        for e in range(2):
                            mm = pe.matmul(b[:, e * BAND:(e + 1) * BAND], qst[:, 2 * p + e, :],
                                           kk2[:, (p // 2) ^ e, (t + 1) * P:(t + 1) * P + BAND], start=e == 0,
                                           stop=e == 1, skip_group_check=True)
                        A.done(mm, f"sc{p}")

                def transposes(p):
                    if not live:
                        return
                    b = A.claim(pe, f"pt{p}", t)
                    for e in range(2):
                        h = 2 * p + e
                        pe.transpose(b[:, e * P:(e + 1) * P], sb[t % 2][:, h, 0:P], ident)
                    for e in range(2):
                        h = 2 * p + e
                        mm = pe.transpose(b[0:HD, (2 + e) * P:(3 + e) * P], sb[t % 2][:, h, P:BAND], ident)
                    A.done(mm, f"pt{p}")

                def values(p):
                    if not live:
                        return
                    A.emptied(pe, f"pt{p}", t)
                    for e in range(2):
                        for j in range(2):
                            mm = pe.matmul(bank[6][HD * e:HD * e + HD, p * P:(p + 1) * P],
                                           vst[:, j, (p // 2) * HD:(p // 2 + 1) * HD], pt[:, p % 2, j, e, :],
                                           start=p == 0 and j == 0, stop=p == NP - 1 and j == 1,
                                           skip_group_check=True)
                    mm.then_inc(s_pv, 1) if p < NP - 1 else A.done(mm, "pv")

                if live:
                    pe.wait_ge(s_pn, t + 1)
                    transposes(0)
                    transposes(1)
                    A.claim(pe, "pv", t)
                    pe.wait_ge(s_st, t + 1)
                if more:
                    pe.wait_ge(s_rnx, n + 1)
                    b = A.claim(pe, "rn", t)
                    for j in range(4):
                        mm = pe.matmul(b[:, j * P:(j + 1) * P], rnx[:, n % 2, j, :, :].rearrange("p a n -> p (a n)"),
                                       ident, start=j == 0, stop=j == 3, skip_group_check=True)
                    A.done(mm, "rn")
                    b = A.claim(pe, "g", t)
                    A.done(pe.matmul(b[:, :], lora[:, 2, (n // 2) * P:(n // 2 + 1) * P], wg[:, 1, unit(n)[1]],
                                     start=True, stop=True), "g")
                values(0)
                transposes(2)
                values(1)
                transposes(3)
                values(2)
                if more:
                    pe.wait_ge(s_prod, n + 1)
                    b = A.claim(pe, "bs", t)
                    A.done(pe.matmul(b[:, :], ones_blk, prod[:, n % 2, :], start=True, stop=True), "bs")
                values(3)
            straight(pe, body)

        def stage3_scalar(act):
            for n in range(8):
                p, c = unit(n)
                b = B.result(act, f"a{n}", 0)
                B.read(act.activation(ab[:, p, c], b[:, :], ACT.Sigmoid, bias=par[:, R_A0 + p:R_A0 + p + 1]), f"a{n}")
            for p in range(NP):
                act.wait_ge(s_kkr, p + 1)
                act.activation(mix[:, p, :], kkn[:, p, :], ACT.Square).then_inc(s_sqr, 1)
            for n in range(8):
                b = B.result(act, f"v{n}", 0)
                if n:
                    act.wait_ge(s_vd, 16 * n)
                B.read(act.activation(vo[:, :], b[:, :], ACT.Copy), f"v{n}")
            for n in range(8):
                B.emptied(act, f"sg{n}", 0)
                act.activation(sgo[:, n % 2, :], sgo[:, n % 2, :], ACT.Sigmoid).then_inc(s_sgo, 1)
            act.wait_ge(s_nrm, 1)
            act.activation(rn, rn, ACT.Sqrt).then_inc(s_root, 1)
            act.wait_ge(s_rn, 1)

            def spread(n):
                v = rn.rearrange("p (t h) -> p t h", h=H)[:, 4 * (n % 2):4 * (n % 2) + 4, 2 * (n // 2):2 * (n // 2) + 2]
                act.activation(rnx[:, n % 2, :, :, :], v.unsqueeze(3).to_broadcast([P, 4, 2, HD]), ACT.Copy
                               ).then_inc(s_rnx, 1)

            def key_scale(n):
                p, c = unit(n)
                if n >= 2:
                    act.wait_ge(s_prod, n - 1)
                act.activation(tm[:, n % 2, :], ab[:, p, c], ACT.Identity, bias=omka[:, p:p + 1],
                               scale=par[:, R_KA + p:R_KA + p + 1]).then_inc(s_tm, 1)

            for n in range(2):
                act.wait_ge(s_sgd[n], 16 * NT // 2)
            spread(0)
            for n in range(8):
                B.emptied(act, f"a{n}", 0)
            key_scale(0)

            def body(t, live, more):
                n = t + 1
                if live:
                    for p in range(NP):
                        b = A.result(act, f"pt{p}", t)
                        if p >= 2:
                            act.wait_ge(s_pv, 3 * t + p - 1)
                        elif t:
                            A.result(act, "pv", t - 1)
                        act.activation(row(pt[:, p % 2, 0, :, :]), b[:, 0:2 * P], ACT.Copy)
                        ins = act.activation(row(pt[0:HD, p % 2, 1, :, :]), b[0:HD, 2 * P:4 * P], ACT.Copy)
                        A.read(ins, f"pt{p}")
                if more:
                    act.wait_ge(s_mx, 2 * t + 4)
                    act.activation(st8[:, 4, :], st8[:, 2, :], ACT.Exp).then_inc(s_pe, 1)
                    for h in range(H):
                        act.activation(sb[n % 2][:, h, :], sb[n % 2][:, h, :], ACT.Exp, bias=st8[:, 3, h:h + 1],
                                       accum_out=st8[:, 5, h:h + 1]).then_inc(s_pe, 1)
                    if n + 1 < NT:
                        if live:
                            A.result(act, "rn", t - 1)
                        spread(n + 1)
                        key_scale(n + 1)
                if live:
                    b = A.result(act, "pv", t)
                    A.read(act.activation(mix[:, NP:2 * NP, t * P:(t + 1) * P], b[:, :].rearrange("p (a n) -> p a n", a=NP),
                                          ACT.Copy), "pv")
                if more:
                    p, c = unit(n)
                    act.wait_ge(s_gm, n + 1)
                    A.read(act.activation(vT[:, p, c], bank[7][:, :], ACT.Copy, scale=par[:, R_GG + p:R_GG + p + 1]), "g")
            straight(act, body)

        def stage3_vector(dve):
            order = Order(dve, "prep_order")
            order(dve.tensor_scalar(omka, par[:, R_KA:R_KA + NP], -1.0, 1.0, ALU.mult, ALU.add))
            IN.J.result(dve, "11", IN.n - 1)
            for p in range(NP):
                dve.tensor_scalar(kkn[:, p, :], kT[:, p, :], par[:, R_KK + p:R_KK + p + 1], None, ALU.mult
                                  ).then_inc(s_kkr, 1)
            b = B.result(dve, "ss", 0)
            B.read(dve.tensor_scalar(rn, b[:, 0:8 * NT], L2_EPS * L2_EPS, None, ALU.max), "ss")
            B.emptied(dve, "ss", 0)
            dve.sem_inc(s_nrm, 1)
            for n in range(8):
                b = B.result(dve, f"sg{n}", 0)
                if n >= 2:
                    dve.wait_ge(s_sgd[n % 2], 16 * (n // 2))
                B.read(dve.tensor_tensor(sgo[:, n % 2, :], b[:, :], lora[:, 3, :], ALU.add), f"sg{n}")
            dve.wait_ge(s_root, 1)
            dve.reciprocal(rn, rn).then_inc(s_rn, 1)
            dve.wait_ge(s_bias, 16)
            dve.wait_ge(s_snk, 16)

            def body(t, live, more):
                if live:
                    pr = sb[t % 2]
                    dve.wait_ge(s_pe, 9 * t + 9)
                    order(dve.tensor_tensor(st8[:, 5, :], st8[:, 5, :], st8[:, 4, :], ALU.add))
                    order(dve.reciprocal(st8[:, 5, :], st8[:, 5, :]))
                    dve.tensor_tensor(pr[:, :, :], pr[:, :, :], st8[:, 5, :].unsqueeze(2).to_broadcast([P, H, BAND]),
                                      ALU.mult).then_inc(s_pn, 1)
                if more:
                    sc = sb[(t + 1) % 2]
                    if t >= 1:
                        A.result(dve, f"pt{NP - 1}", t - 1)
                    for p in range(NP):
                        b = A.result(dve, f"sc{p}", t)
                        ins = dve.scalar_tensor_tensor(sc[:, 2 * p:2 * p + 2, :],
                                                       b[:, 0:2 * BAND].rearrange("p (a n) -> p a n", a=2), HD ** -0.5,
                                                       bias[:, 2 * p:2 * p + 2, :], ALU.mult, ALU.add)
                        A.read(ins, f"sc{p}")
                    A.emptied(dve, f"sc{NP - 1}", t)
                    if not live:
                        order(dve.memset(sc[:, :, 0:HD], NEG))
                    order(dve.tensor_reduce(st8[:, 0, :], sc[:, :, :], AX_X, ALU.max))
                    order(dve.tensor_tensor(st8[:, 1, :], st8[:, 0, :], snk[:, :], ALU.max))
                    dve.tensor_tensor(st8[:, 2, :], snk[:, :], st8[:, 1, :], ALU.subtract).then_inc(s_mx, 1)
                    dve.tensor_scalar(st8[:, 3, :], st8[:, 1, :], -1.0, None, ALU.mult).then_inc(s_mx, 1)
                    n = t + 1
                    p, c = unit(n)
                    b = A.result(dve, "rn", t)
                    A.read(dve.tensor_tensor(kkn[:, p, c], kkn[:, p, c], b[:, :], ALU.mult), "rn")
                    dve.wait_ge(s_tm, n + 1)
                    order(dve.tensor_tensor(kT[:, p, c], kT[:, p, c], tm[:, n % 2, :], ALU.mult))
                    if n >= 2:
                        A.result(dve, "bs", t - 2)
                    dve.scalar_tensor_tensor(prod[:, n % 2, :], rT[:, p, c], par[:, R_RK + p:R_RK + p + 1], kT[:, p, c],
                                             ALU.mult, ALU.mult).then_inc(s_prod, 1)
                    A.emptied(dve, "rn", t)
                    order(dve.scalar_tensor_tensor(ab[:, p, c], kkn[:, p, c], -1.0, ab[:, p, c], ALU.mult, ALU.mult))
                    b = A.result(dve, "bs", t)
                    A.read(dve.tensor_tensor(mix[:, p, c], b[:, :], vT[:, p, c], ALU.mult), "bs")
                    A.emptied(dve, "bs", t)
                    b = A.result(dve, "g", t)
                    dve.scalar_tensor_tensor(mix[:, p, c], mix[:, p, c], par[:, R_GB + p:R_GB + p + 1], b[:, :],
                                             ALU.add, ALU.mult).then_inc(s_gm, 1)
            straight(dve, body)
            A.emptied(dve, "pv", NT - 1)
            A.emptied(dve, "g", NT - 2)
            dve.wait_ge(s_gm, NT)

        table = []
        for n in range(1, 7):
            table += [(f"t{n}{g}", g) for g in range(2)]
            table += [(f"x{n}{g}", 2 + g) for g in range(2) if n < 6]
            table += [(f"y{n}{g}", 4 + g) for g in range(2)]
        table += [("R", 0), ("O", 1), ("U", 2), ("S", 3), ("ot", 1)]
        C = Jobs(table, [("cum0", 6), ("cum1", 7), ("ab0", 4), ("ab1", 5), ("ab2", 6), ("ab3", 7), ("kb0", 0), ("kb1", 2),
                         ("kb2", 4), ("kb3", 5), ("bt", 6), ("kt", 7), ("x0", 1), ("x1", 3)])
        C.end(NT)
        s_z5, s_seen = sem("s_z5"), sem("s_seen")
        (s_sgt, s_vtk, s_ec, s_bk, s_ar, s_o1, s_pad, s_x1t, s_S, s_oc, s_osq, s_var, s_rstd, s_on) = (
            sem(f"s5_{n}") for n in ("sg", "v", "ec", "beta_kappa", "alpha_rho", "o1", "pad", "x1t", "S", "oc", "osq",
                                     "var", "rstd", "on"))
        up = cst[:, C_UP:C_UP + 2 * P].bitcast(U32).unsqueeze(1).to_broadcast([P, 2, 2 * P])
        def stage5_sync(sp):
            def body(t, live, more):
                if more:
                    if live:
                        C.result(sp, "cum1", t - 1)
                    if not live:
                        A.result(sp, f"pt{NP - 1}", NT - 1)
                    sp.dma_start(sgt[:, :], sg_dram[bass.ds((t + 1) * P, P), :]).then_inc(s_sgt, 16)
                    if live:
                        C.result(sp, "S", t)
                    else:
                        sp.wait_ge(s_vd, 16 * NT)
                    sp.dma_start(vtk[:, :], v_dram[bass.ds((t + 1) * P, P), :]).then_inc(s_vtk, 16)
            pipelined(sp, body)

        def stage5_gpsimd(pool):
            A.result(pool, "pv", NT - 1)
            pool.wait_ge(s_pn, NT)
            for n, (m, value) in enumerate(((apad[:, :, :, :], 0.0), (NB[:, :, :, :], 0.0), (KB[:, :, :, :], 0.0),
                                            (Sn[:, :, :], 0.0), (ec, 1.0), (expo, -0.5))):
                if n:
                    pool.wait_ge(s_z5, n)
                pool.memset(m, value).then_inc(s_z5, 1)
            pool.wait_ge(s_z5, 6)

            def body(t, live, more):
                if live:
                    pool.wait_ge(s_var, t + 1)
                    pool.sem_inc(s_seen, 1)
                    pool.tensor_scalar(rstd, var, 1.0 / HD, GN_EPS, ALU.mult, ALU.add).then_inc(s_rstd, 1)
                    pool.wait_ge(s_rstd, 2 * t + 1)
                    pool.tensor_tensor(rstd, rstd, expo, ALU.pow).then_inc(s_rstd, 1)
            pipelined(pool, body)

        def stage5_tensor(pe):
            pe.wait_ge(s_z5, 6)

            def four(b, g, lhs, rhs):
                for j in range(4):
                    mm = pe.matmul(b[:, j * P:(j + 1) * P], lhs(4 * g + j), rhs(4 * g + j), start=j == 0, stop=j == 3,
                                   skip_group_check=True)
                return mm

            def levels(t, low, high):
                for n in range(low, high):
                    for g in range(2):
                        b = C.claim(pe, f"t{n}{g}", t)
                        if n == 1:
                            C.emptied(pe, f"x{g}", t - 1)
                        else:
                            C.emptied(pe, f"x{n - 1}{g}", t)
                        C.done(four(b, g, lambda h: NB[:, h, 0, :], lambda h: X[:, h, :]), f"t{n}{g}")
                    for g in range(2):
                        C.emptied(pe, f"t{n}{g}", t)
                        if n > 1:
                            C.emptied(pe, f"y{n - 1}{g}", t)
                        if n < 6:
                            b = C.claim(pe, f"x{n}{g}", t)
                            C.done(four(b, g, lambda h: XT[:, h, :], lambda h: Ts[:, h, :]), f"x{n}{g}")
                        b = C.claim(pe, f"y{n}{g}", t)
                        C.done(four(b, g, lambda h: Ts[:, h, :], lambda h: XT[:, h, :]), f"y{n}{g}")

            def body(t, live, more):
                if live:
                    levels(t, 1, 3)
                if more:
                    pe.wait_ge(s_sgt, 16 * t + 32)
                    for j in range(2):
                        b = C.claim(pe, f"cum{j}", t)
                        for p in (2 * j, 2 * j + 1):
                            mm = pe.matmul(b[:, (p % 2) * 2 * P:(p % 2 + 1) * 2 * P], sgt[:, p * P:(p + 1) * P],
                                           cst[:, C_CUM:C_CUM + 2 * P], start=p % 2 == 0, stop=p % 2 == 1,
                                           skip_group_check=True)
                        C.done(mm, f"cum{j}")
                if live:
                    levels(t, 3, 7)
                    pe.wait_ge(s_S, t + 1)
                    pe.wait_ge(s_vtk, 16 * t + 16)
                    b = C.claim(pe, "R", t)
                    for p in range(NP):
                        pe.matmul(b[:, p * P:(p + 1) * P], alpha[:, p, :], S[:, p, :], start=p == 0, stop=False,
                                  skip_group_check=True)
                    for h in range(H):
                        mm = pe.matmul(b[:, h * HD:(h + 1) * HD], KB[:, h, 0, :], vtk[:, h * HD:(h + 1) * HD],
                                       start=False, stop=h == H - 1, skip_group_check=True)
                    C.done(mm, "R")
                    bo = C.claim(pe, "O", t)
                    for h in range(H):
                        pe.matmul(bo[:, h * HD:(h + 1) * HD], KB[:, h, 1, :], vtk[:, h * HD:(h + 1) * HD], start=h == 0,
                                  stop=False, skip_group_check=True)
                    for p in range(NP):
                        mm = pe.matmul(bo[:, p * P:(p + 1) * P], rho[:, p, :], S[:, p, :], start=False, stop=False,
                                       skip_group_check=True)
                    mm.then_inc(s_o1, 1)
                    b = C.claim(pe, "U", t)
                    C.emptied(pe, "R", t)
                    for g in range(2):
                        C.emptied(pe, f"y6{g}", t)
                    for h in range(H):
                        mm = pe.matmul(b[:, h * HD:(h + 1) * HD], XT[:, h, :], rs_[:, h * HD:(h + 1) * HD],
                                       start=h == 0, stop=h == H - 1, skip_group_check=True)
                    C.done(mm, "U")
                    b = C.claim(pe, "S", t)
                    for p in range(NP):
                        c = slice(p * P, (p + 1) * P)
                        pe.matmul(b[:, c], kt_[:, c], vtk[:, c], start=p == 0, stop=False, skip_group_check=True)
                    C.emptied(pe, "U", t)
                    for p in range(NP):
                        c = slice(p * P, (p + 1) * P)
                        mm = pe.matmul(b[:, c], bt[:, c], us_[:, c], start=False, stop=p == NP - 1,
                                       skip_group_check=True)
                    C.done(mm, "S")
                    for h in range(H):
                        mm = pe.matmul(bo[:, h * HD:(h + 1) * HD], NB[:, h, 1, :], us_[:, h * HD:(h + 1) * HD],
                                       start=False, stop=h == H - 1, skip_group_check=True)
                    C.done(mm, "O")
                if more:
                    pe.wait_ge(s_pad, 4 * t + 8)
                    pe.wait_ge(s_bk, 2 * t + 4)
                    for kind, m in (("ab", beta), ("kb", kappa)):
                        for g in range(4):
                            b = C.claim(pe, f"{kind}{g}", t)
                            for h in (2 * g, 2 * g + 1):
                                mm = pe.matmul(b[:, (h % 2) * 2 * P:(h % 2 + 1) * 2 * P], m[:, h // 2, :],
                                               apad[:, h, :, :].rearrange("p a n -> p (a n)"), start=h % 2 == 0,
                                               stop=h % 2 == 1, skip_group_check=True)
                            C.done(mm, f"{kind}{g}")
                    for kind, m in (("bt", beta), ("kt", kappa)):
                        b = C.claim(pe, kind, t)
                        for p in range(NP):
                            mm = pe.transpose(b[:, p * P:(p + 1) * P], m[:, p, :], ident)
                        C.done(mm, kind)
                if live:
                    b = C.claim(pe, "ot", t)
                    pe.wait_ge(s_on, t + 1)
                    for p in range(NP):
                        mm = pe.transpose(b[:, p * P:(p + 1) * P],
                                          on[:, 2 * p:2 * p + 2, :].rearrange("p a n -> p (a n)"), ident)
                    C.done(mm, "ot")
                if more:
                    pe.wait_ge(s_x1t, 2 * t + 4)
                    for g in range(2):
                        b = C.claim(pe, f"x{g}", t)
                        for j in range(4):
                            mm = pe.transpose(b[:, j * P:(j + 1) * P], XT[:, 4 * g + j, :], ident)
                        C.done(mm, f"x{g}")
            pipelined(pe, body)

        def stage5_scalar(act):
            act.wait_ge(s_z5, 6)

            def body(t, live, more):
                if more:
                    if live:
                        act.wait_ge(s_S, t + 1)
                        act.activation(ec[:, 0:NP], ein[:, :, P - 1], ACT.Copy).then_inc(s_ec, 1)
                        act.wait_ge(s_ec, t + 1)
                    for j in range(2):
                        b = C.result(act, f"cum{j}", t)
                        v = b[:, :].rearrange("p (a n) -> p a n", a=2)
                        c = slice(2 * j, 2 * j + 2)
                        act.activation(ein[:, c, :], v[:, :, 0:P], ACT.Exp, scale=-DECAY)
                        act.activation(einv[:, c, :], v[:, :, 0:P], ACT.Exp, scale=DECAY)
                        act.activation(em[:, c], v[:, :, P], ACT.Exp, scale=DECAY)
                        ins = act.activation(eex[:, c, :], v[:, :, P:2 * P], ACT.Exp, scale=-DECAY)
                        C.read(ins, f"cum{j}")
                if live:
                    for kind, m in (("R", rs_), ("U", us_)):
                        b = C.result(act, kind, t)
                        C.read(act.activation(m[:, :], b[:, :], ACT.Copy), kind)
                if more:
                    act.wait_ge(s_ar, 2 * t + 4)
                    for i, m in enumerate((alpha, rho)):
                        for e in range(2):
                            r = slice(HD * e, HD * e + HD)
                            act.activation(apad[r, e::2, i, :], m[r, :, :], ACT.Copy).then_inc(s_pad, 1)
                if live:
                    act.wait_ge(s_oc, t + 1)
                    act.activation(osq[:, :, :], oc[:, :, :], ACT.Square).then_inc(s_osq, 1)
                if more:
                    for kind, m in (("bt", bt), ("kt", kt_)):
                        b = C.result(act, kind, t)
                        C.read(act.activation(m[:, :], b[:, :], ACT.Copy), kind)
                    for g in range(2):
                        b = C.result(act, f"x{g}", t)
                        C.read(act.activation(X[:, 4 * g:4 * g + 4, :].rearrange("p a n -> p (a n)"), b[:, :],
                                              ACT.Copy), f"x{g}")
            pipelined(act, body)

        def stage5_vector(dve):
            head, tail = Order(dve, "rec_order0"), Order(dve, "rec_order1")
            dve.wait_ge(s_z5, 6)

            def levels(t, low, high):
                for n in range(low, high):
                    m = cst[:, C_LEV + (n - 1) * P:C_LEV + n * P].unsqueeze(1).to_broadcast([P, 4, P])
                    for g in range(2):
                        q = slice(4 * g, 4 * g + 4)
                        b = C.result(dve, f"t{n}{g}", t)
                        if n > 1:
                            C.result(dve, f"y{n - 1}{g}", t)
                        C.read(dve.tensor_tensor(Ts[:, q, :], b[:, :].rearrange("p (h n) -> p h n", h=4), m, ALU.mult),
                               f"t{n}{g}")
                    for g in range(2):
                        q = slice(4 * g, 4 * g + 4)
                        if n < 6:
                            b = C.result(dve, f"x{n}{g}", t)
                            C.read(dve.tensor_tensor(X[:, q, :], b[:, :].rearrange("p (h n) -> p h n", h=4),
                                                     X[:, q, :], ALU.add), f"x{n}{g}")
                        b = C.result(dve, f"y{n}{g}", t)
                        C.read(dve.tensor_tensor(XT[:, q, :], b[:, :].rearrange("p (h n) -> p h n", h=4), XT[:, q, :],
                                                 ALU.add), f"y{n}{g}")

            def body(t, live, more):
                c, c1 = bass.ds(t * P, P) if live else None, bass.ds((t + 1) * P, P)
                if live:
                    head.tile(t, 3)
                    levels(t, 1, 5)
                if more:
                    C.emptied(dve, "cum1", t)
                    dve.tensor_tensor(beta[:, :, :], ab[:, :, c1], einv[:, :, :], ALU.mult).then_inc(s_bk, 1)
                    dve.tensor_tensor(kappa[:, :, :], kT[:, :, c1], einv[:, :, :], ALU.mult).then_inc(s_bk, 1)
                if live:
                    levels(t, 5, 7)
                if more:
                    if live:
                        dve.wait_ge(s_o1, t + 1)
                    dve.tensor_tensor(alpha[:, :, :], kkn[:, :, c1], eex[:, :, :], ALU.mult).then_inc(s_ar, 1)
                    dve.tensor_tensor(rho[:, :, :], rT[:, :, c1], ein[:, :, :], ALU.mult).then_inc(s_ar, 1)
                if live:
                    b = C.result(dve, "S", t)
                    C.read(dve.tensor_tensor(Sn[:, :, :], b[:, :].rearrange("p (a n) -> p a n", a=NP), S[:, :, :],
                                             ALU.add), "S")
                    b = C.result(dve, "O", t)
                    o = b[:, :].rearrange("p (h n) -> p h n", h=H)
                    head(dve.tensor_reduce(mean, o, AX_X, ALU.add))
                    head(dve.tensor_scalar(mean, mean, 1.0 / HD, None, ALU.mult))
                    ins = dve.tensor_tensor(oc[:, :, :], o, mean.unsqueeze(2).to_broadcast([P, H, HD]), ALU.subtract)
                    C.read(ins, "O")
                    C.emptied(dve, "O", t)
                    dve.sem_inc(s_oc, 1)
                if more:
                    tail.tile(t + 1, 2)
                    if live:
                        dve.wait_ge(s_ec, t + 1)
                        C.emptied(dve, "S", t)
                    tail(dve.tensor_tensor(fac[:, 0:NP], ec[:, 0:NP], em[:, 0:NP], ALU.mult))
                    for p in range(NP):
                        ins = dve.scalar_tensor_tensor(S[:, p, :], Sn[:, p, :], fac[:, p:p + 1], ones_blk, ALU.mult,
                                                       ALU.mult)
                    ins.then_inc(s_S, 1)
                if live:
                    dve.wait_ge(s_osq, t + 1)
                    dve.tensor_reduce(var, osq[:, :, :], AX_X, ALU.add).then_inc(s_var, 1)

                def masked(kind, m):
                    for g in range(4):
                        b = C.result(dve, f"{kind}{g}", t)
                        dve.sem_inc(s_seen, 1)
                        ins = dve.copy_predicated(m[:, 2 * g:2 * g + 2, :, :].rearrange("p h a n -> p h (a n)"), up,
                                                  b[:, :].rearrange("p (h n) -> p h n", h=2))
                        C.read(ins, f"{kind}{g}")

                if more:
                    masked("ab", NB)
                    C.emptied(dve, "ab3", t)
                    tail(dve.tensor_tensor(Ts[:, :, :], NB[:, :, 0, :],
                                           cst[:, C_M1T:C_M1T + P].unsqueeze(1).to_broadcast([P, H, P]), ALU.mult))
                    for g in range(2):
                        dve.tensor_tensor(XT[:, 4 * g:4 * g + 4, :], Ts[:, 4 * g:4 * g + 4, :],
                                          ident.unsqueeze(1).to_broadcast([P, 4, P]), ALU.add).then_inc(s_x1t, 1)
                if live:
                    dve.wait_ge(s_rstd, 2 * t + 2)
                    dve.tensor_tensor(on[:, :, :], oc[:, :, :], rstd.unsqueeze(2).to_broadcast([P, H, HD]), ALU.mult
                                      ).then_inc(s_on, 1)
                if more:
                    masked("kb", KB)
                if live:
                    b = C.result(dve, "ot", t)
                    head(dve.tensor_tensor(oc[:, :, :].rearrange("p (a b) n -> p a (b n)", a=NP),
                                           b[:, :].rearrange("p (a n) -> p a n", a=NP), gT[:, :, c], ALU.mult))
                    ins = dve.tensor_tensor(mix[:, 0:NP, c], oc[:, :, :].rearrange("p (a b) n -> p a (b n)", a=NP),
                                            mix[:, 0:NP, c], ALU.add)
                    C.read(ins, "ot")
                    C.emptied(dve, "ot", t)
            pipelined(dve, body)

        s_m, s_mlo, s_xt = sem("s_mhi"), sem("s_mlo"), [sem("s_xt0"), sem("s_xt1")]
        s_x1, s_xsq, s_x1hi, s_x1lo, s_acc, s_dg2 = (sem(f"s6_{n}") for n in ("x1", "xsq", "x1hi", "x1lo", "acc", "diag"))
        X6 = Jobs([(f"{t}{g}", 4 + 2 * t + g) for t in range(2) for g in range(2)])
        X6.end(NT // 2)
        OUT = Layer(ring2, w_out_v, KD, KD // 2)
        N2 = Jobs([("col", 4), ("rs0", 4), ("rs1", 5)])
        N2.end(1)

        def layer_of(b):
            return OUT if b < KD else following[0]

        def turn_of(b):
            return b % KD // 2

        def stage6_sync(sp):
            for t in range(NT):
                if t >= 2:
                    X6.result(sp, f"{t % 2}1", t // 2 - 1)
                sp.dma_start(xtok[:, t % 2, :], x[0, t * P:(t + 1) * P, :]).then_inc(s_xt[t % 2], 16)
                if t == 1:
                    C.emptied(sp, "ot", NT - 1)
                    for s in range(2):
                        OUT.load(sp, s, 0, s * P, first=True)
            for turn in range(1, OUT.n):
                for s in range(2):
                    OUT.load(sp, s, turn, (2 * turn + s) * P)

        def stage6_tensor(pe):
            C.emptied(pe, "ot", NT - 1)
            for t in range(NT):
                pe.wait_ge(s_xt[t % 2], 16 * (t // 2) + 16)
                for g in range(2):
                    b = X6.claim(pe, f"{t % 2}{g}", t // 2)
                    for k in range(4):
                        mm = pe.transpose(b[:, k * P:(k + 1) * P], xtok[:, t % 2, (4 * g + k) * P:(4 * g + k + 1) * P],
                                          ident)
                    X6.done(mm, f"{t % 2}{g}")

            for turn in range(OUT.n):
                for s in range(2):
                    OUT.products(pe, s, turn, mhi, mlo, (lambda k: pe.wait_ge(s_mlo, k + 1)) if turn + s == 0 else None)

        def norm2_tensor(pe):
            def between(s):
                if s == 0:
                    b = N2.claim(pe, "col", 0)
                    pe.wait_ge(s_acc, KD - 1)
                    for t in range(NT):
                        mm = pe.matmul(b[:, t:t + 1], rsb2[:, t * P:(t + 1) * P], ones[:, 0:1], start=t == 0,
                                       stop=t == NT - 1, skip_group_check=True)
                    N2.done(mm, "col")
                else:
                    for half in range(2):
                        b = N2.claim(pe, f"rs{half}", 0)
                        pe.wait_ge(s_dg2, 4 * half + 5)
                        for t in range(4):
                            mm = pe.matmul(b[:, t * P:(t + 1) * P], ones, dg2[:, 4 * half + t, :], start=t == 0,
                                           stop=t == 3, skip_group_check=True)
                        N2.done(mm, f"rs{half}")
            return between

        def stage6_scalar(act):
            C.emptied(act, "ot", NT - 1)
            for k in range(KD):
                act.activation(mhi[:, k, :], mix[:, k, :], ACT.Copy).then_inc(s_m, 1)
                if k == 3:
                    for s in range(2):
                        OUT.split_hi(act, s, 0, first=True)
            for k in range(KD):
                layer_of(k + 2).split_hi(act, k % 2, turn_of(k + 2))
                act.wait_ge(s_x1, 2 * k + 2)
                act.wait_ge(s_mlo, KD)
                act.activation(x1hi[:, k, :], x1[:, k, :], ACT.Copy, scale=par[:, R_N2 + k:R_N2 + k + 1]).then_inc(s_x1hi, 1)
                if k >= 2:
                    act.wait_ge(s_acc, k - 1)
                act.activation(xsq[:, k % 2, :], x1[:, k, :], ACT.Square).then_inc(s_xsq, 1)
            b = N2.result(act, "col", 0)
            N2.read(act.activation(rms2, b[:, 0:NT], ACT.Sqrt, bias=small[:, 32:33], scale=1.0 / D), "col")
            for half in range(2):
                b = N2.result(act, f"rs{half}", 0)
                N2.read(act.activation(rsb2[:, half * HALF:(half + 1) * HALF], b[:, :], ACT.Copy), f"rs{half}")

        def stage6_vector(dve):
            C.emptied(dve, "ot", NT - 1)

            def low(k):
                dve.wait_ge(s_m, k + 1)
                dve.tensor_tensor(mlo[:, k, :], mix[:, k, :], mhi[:, k, :].bitcast(F32), ALU.subtract).then_inc(s_mlo, 1)
            for t in range(NT):
                for g in range(2):
                    b = X6.result(dve, f"{t % 2}{g}", t // 2)
                    X6.read(dve.tensor_copy(x1[:, 4 * g:4 * g + 4, t * P:(t + 1) * P],
                                            b[:, :].rearrange("p (a n) -> p a n", a=4)), f"{t % 2}{g}")
                low(t)
                if t == 5:
                    for s in range(2):
                        OUT.split_lo(dve, s, 0)
            for s in range(2):
                for g in range(2):
                    X6.emptied(dve, f"{s}{g}", NT // 2 - 1)
            def add_squares(k):
                dve.wait_ge(s_xsq, k + 1)
                if k > 1:
                    dve.wait_ge(s_acc, k - 1)
                dve.tensor_tensor(rsb2[:, :], xsq[:, 0, :] if k == 1 else rsb2[:, :], xsq[:, k % 2, :], ALU.add
                                  ).then_inc(s_acc, 1)

            for k in range(KD):
                s, turn = k % 2, k // 2
                layer_of(k + 2).split_lo(dve, s, turn_of(k + 2))
                for half in range(2):
                    b = OUT.J.result(dve, f"{s}{half}", turn)
                    v = x1[:, k, half * HALF:(half + 1) * HALF]
                    OUT.J.read(dve.tensor_tensor(v, b[:, :], v, ALU.add), f"{s}{half}")
                    OUT.J.emptied(dve, f"{s}{half}", turn)
                    dve.sem_inc(s_x1, 1)
                if k >= 2:
                    add_squares(k - 1)
                dve.wait_ge(s_x1hi, k + 1)
                dve.scalar_tensor_tensor(x1lo[:, k, :], x1[:, k, :], par[:, R_N2 + k:R_N2 + k + 1],
                                         x1hi[:, k, :].bitcast(F32), ALU.mult, ALU.subtract).then_inc(s_x1lo, 1)
            add_squares(KD - 1)
            N2.emptied(dve, "col", 0)
            dve.reciprocal(rms2, rms2).then_inc(s_dg2, 1)
            dve.wait_ge(s_dg2, 1)
            dve.wait_ge(s_acc, KD - 1)
            for t in range(NT):
                dve.tensor_scalar(dg2[:, t, :], ident, rms2[:, t:t + 1], None, ALU.mult).then_inc(s_dg2, 1)

        s_gat, s_sil, s_hid, s_hh7, s_hl7, s_add = (sem(f"s7_{n}") for n in ("gat", "sil", "hid", "hh", "hl", "add"))

        def feed_forward(gi, G, f0):
            GU = Layer(ring2, w_gu_v, KD, G)
            DN = Layer(ring2, w_dn_v, G, KD // 2)
            last = gi == len(GROUPS) - 1
            tiles0 = f0
            adds0 = gi * KD

            def ff_sync(sp):
                with sp.Fori(0, G) as i:
                    for s in range(2):
                        GU.load(sp, s, i, i * P + (s * FF + f0 * P))
                with sp.Fori(0, DN.n) as i:
                    for s in range(2):
                        DN.load(sp, s, i, (2 * i + s) * P, rows=f0)

            def ff_scalar(act):
                def silu(turn):
                    for half in range(2):
                        c = slice(half * HALF, (half + 1) * HALF)
                        act.wait_ge(s_gat, 2 * turn + (2 * tiles0 + half + 1))
                        act.activation(sil[:, c], gat[:, c], ACT.Silu).then_inc(s_sil, 1)

                def high(turn):
                    act.wait_ge(s_hid, 2 * turn + (2 * tiles0 + 2))
                    act.activation(row(hidhi[:, bass.ds(turn, 1), :]), hid[:, :], ACT.Copy).then_inc(s_hh7, 1)

                def hidden(turn, more=True):
                    silu(turn)
                    if more:
                        for s in range(2):
                            GU.split_hi(act, s, turn + 1)
                    high(turn)

                with act.Fori(0, G - 1) as i:
                    hidden(i)
                silu(G - 1)
                for s in range(2):
                    DN.split_hi(act, s, 0)
                high(G - 1)
                with act.Fori(1, DN.n) as i:
                    for s in range(2):
                        DN.split_hi(act, s, i)

            def ff_vector(dve):
                def hidden(turn, low):
                    for half in range(2):
                        c = slice(half * HALF, (half + 1) * HALF)
                        if half == 0:
                            dve.wait_ge(s_hl7, turn + (tiles0 + 1))
                        b = GU.J.result(dve, f"0{half}", turn)
                        GU.J.read(dve.tensor_tensor(gat[:, c], b[:, :], rsb2[:, c], ALU.mult), f"0{half}")
                        GU.J.emptied(dve, f"0{half}", turn)
                        dve.sem_inc(s_gat, 1)
                    low()
                    for half in range(2):
                        c = slice(half * HALF, (half + 1) * HALF)
                        b = GU.J.result(dve, f"1{half}", turn)
                        GU.J.read(dve.tensor_tensor(hid[:, c], b[:, :], rsb2[:, c], ALU.mult), f"1{half}")
                        GU.J.emptied(dve, f"1{half}", turn)
                        dve.wait_ge(s_sil, 2 * turn + (2 * tiles0 + half + 1))
                        dve.tensor_tensor(hid[:, c], hid[:, c], sil[:, c], ALU.mult).then_inc(s_hid, 1)
                    dve.wait_ge(s_hh7, turn + (tiles0 + 1))
                    dve.tensor_tensor(row(hidlo[:, bass.ds(turn, 1), :]), hid[:, :],
                                      row(hidhi[:, bass.ds(turn, 1), :]).bitcast(F32), ALU.subtract).then_inc(s_hl7, 1)

                def lows(layer, turn):
                    for s in range(2):
                        layer.split_lo(dve, s, turn)

                with dve.Fori(0, G - 1) as i:
                    hidden(i, lambda: lows(GU, i + 1))
                hidden(G - 1, lambda: lows(DN, 0))

                def add(s, turn):
                    for half in range(2):
                        b = DN.J.result(dve, f"{s}{half}", turn)
                        v = row(x1[:, bass.ds(2 * turn + s, 1), half * HALF:(half + 1) * HALF])
                        DN.J.read(dve.tensor_tensor(v, b[:, :], v, ALU.add), f"{s}{half}")

                with dve.Fori(0, DN.n - 1) as i:
                    for s in range(2):
                        DN.split_lo(dve, s, i + 1)
                        add(s, i)
                for s in range(2):
                    if not last:
                        following[gi + 1].split_lo(dve, s, 0)
                    add(s, DN.n - 1)

            def ff_tensor(pe):
                if gi == 0:
                    GU.products_late(pe, 0, x1hi, x1lo, lambda k: pe.wait_ge(s_x1lo, k + 1), norm2_tensor(pe))
                else:
                    for s in range(2):
                        GU.products(pe, s, 0, x1hi, x1lo)
                with pe.Fori(1, G) as i:
                    for s in range(2):
                        GU.products(pe, s, i, x1hi, x1lo)
                DN.products_late(pe, 0, hidhi, hidlo, lambda k: pe.wait_ge(s_hl7, tiles0 + k + 2))
                with pe.Fori(1, DN.n) as i:
                    for s in range(2):
                        DN.products(pe, s, i, hidhi, hidlo)

            following[gi] = GU
            ends.append(DN)
            return ff_sync, ff_scalar, ff_vector, ff_tensor

        following, ends, groups = {}, [], []
        f0 = 0
        for gi, G in enumerate(GROUPS):
            groups.append(feed_forward(gi, G, f0))
            f0 += G

        def stage7_sync(sp):
            for g in groups:
                g[0](sp)

        def stage7_scalar(act):
            for gi, g in enumerate(groups):
                if gi:
                    for s in range(2):
                        following[gi].split_hi(act, s, 0)
                g[1](act)

        def stage7_vector(dve):
            dve.sem_inc(s_hl7, 1)
            N2.emptied(dve, "rs0", 0)
            N2.emptied(dve, "rs1", 0)
            for g in groups:
                g[2](dve)

        def stage7_tensor(pe):
            for g in groups:
                g[3](pe)

        s_gf, s_f1, s_f2, s_f3, s_out = sem("s_gf"), sem("s_f1"), sem("s_f2"), sem("s_f3"), [sem("s_out0"), sem("s_out1")]
        F = Jobs([(f"{t}{g}", 4 + 2 * t + g) for t in range(2) for g in range(2)])
        F.end(NT // 2)
        DNL = ends[-1]

        def stage8_sync(sp):
            DNL.J.result(sp, "11", DNL.n - 1)
            sp.dma_start(gfin[:, :], norm_final_g.unsqueeze(0).to_broadcast([P, D])).then_inc(s_gf, 16)
            for t in range(NT):
                sp.wait_ge(s_f3, t + 1)
                sp.dma_start(out[0, t * P:(t + 1) * P, :], fin[:, t % 2, :]).then_inc(s_out[t % 2], 16)
            for n in range(2):
                sp.wait_ge(s_out[n], 16 * NT // 2)

        def stage8_tensor(pe):
            for s in range(2):
                for h in range(2):
                    DNL.J.emptied(pe, f"{s}{h}", DNL.n - 1)
            for t in range(NT):
                for g in range(2):
                    b = F.claim(pe, f"{t % 2}{g}", t // 2)
                    for k in range(4):
                        mm = pe.transpose(b[:, k * P:(k + 1) * P], x1[:, 4 * g + k, t * P:(t + 1) * P], ident)
                    F.done(mm, f"{t % 2}{g}")

        def stage8_scalar(act):
            for t in range(NT):
                if t >= 2:
                    act.wait_ge(s_f3, t - 1)
                for g in range(2):
                    b = F.result(act, f"{t % 2}{g}", t // 2)
                    F.read(act.activation(xo[:, t % 2, g * HALF:(g + 1) * HALF], b[:, :], ACT.Copy), f"{t % 2}{g}")
                F.emptied(act, f"{t % 2}1", t // 2)
                if t >= 2:
                    act.wait_ge(s_out[t % 2], 16 * (t // 2))
                act.activation(fin[:, t % 2, :], xo[:, t % 2, :], ACT.Square, accum_out=st[:, 0, t:t + 1]
                               ).then_inc(s_f1, 1)
                act.wait_ge(s_f1, 2 * t + 1)
                act.activation(st[:, 1, t:t + 1], st[:, 0, t:t + 1], ACT.Sqrt, bias=small[:, 32:33], scale=1.0 / D
                               ).then_inc(s_f1, 1)

        def stage8_vector(dve):
            dve.wait_ge(s_gf, 16)
            for t in range(NT):
                dve.wait_ge(s_f1, 2 * t + 2)
                dve.reciprocal(st[:, 2, t:t + 1], st[:, 1, t:t + 1]).then_inc(s_f2, 1)
                dve.wait_ge(s_f2, t + 1)
                dve.scalar_tensor_tensor(fin[:, t % 2, :], xo[:, t % 2, :], st[:, 2, t:t + 1], gfin[:, :],
                                         ALU.mult, ALU.mult).then_inc(s_f3, 1)

        with nc.Block() as block:
            @block.sync
            def _(sp):
                for stage in (stage1_sync, stage2_sync, stage3_sync, stage5_sync, stage6_sync, stage7_sync, stage8_sync):
                    stage(sp)

            @block.gpsimd
            def _(pool):
                for stage in (stage2_gpsimd, stage3_gpsimd, stage5_gpsimd):
                    stage(pool)

            @block.tensor
            def _(pe):
                for stage in (stage1_tensor, stage2_tensor, stage3_tensor, stage5_tensor, stage6_tensor, stage7_tensor,
                              stage8_tensor):
                    stage(pe)

            @block.scalar
            def _(act):
                for stage in (stage1_scalar, stage2_scalar, stage3_scalar, stage5_scalar, stage6_scalar, stage7_scalar,
                              stage8_scalar):
                    stage(act)

            @block.vector
            def _(dve):
                for stage in (stage1_vector, stage2_vector, stage3_vector, stage5_vector, stage6_vector, stage7_vector,
                              stage8_vector):
                    stage(dve)


_INS = ["x", "norm_mix_g", "w_in", "mu_shift", "w0", "w_up", "a0", "a_up", "g_up", "k_k", "k_a", "r_k", "gn_g", "gn_b",
        "sinks", "w_out", "norm_ffn_g", "w_gate_up", "w_down", "norm_final_g"]


def kernel(**inputs):
    import concourse.bacc as bacc
    from concourse.bass_utils import run_bass_kernel_spmd

    nc = bacc.Bacc("TRN2", target_bir_lowering=False, num_devices=1)
    arrays, args = {}, []
    given = {name: np.ascontiguousarray(inputs[name]) for name in _INS}
    given.update(consts=constants(), alibi=alibi())
    for name, a in given.items():
        arrays[f"in_{name}"] = a
        args.append(nc.dram_tensor(f"in_{name}", a.shape, mybir.dt.from_np(a.dtype), kind="ExternalInput").ap())
    args.append(nc.dram_tensor("out_0", (1, T, D), F32, kind="ExternalOutput").ap())
    hybrid_block(nc, *args)
    r = run_bass_kernel_spmd(nc, [arrays], core_ids=[0])
    return r.results[0]["out_0"]
```

```python
from contextlib import ExitStack

import numpy as np

import concourse.bass as bass
from concourse import mybir

ALU = mybir.AluOpType
ACT = mybir.ActivationFunctionType
AX_X = mybir.AxisListType.X
F32 = mybir.dt.float32
F32R = mybir.dt.float32r
U32 = mybir.dt.uint32

P = 128
T = 1024
D = 1024
NT = T // P
KD = D // P
HD = 64
H = 8
NP = H // 2
W = H * HD
NRW = 14
NAT = 6
NIN = NRW + NAT
FF = 2816
HALF = 512
GROUPS = [6, 6, 5, 5]
BAND = 192
DECAY = float(np.exp(-0.5))
EPS = 1e-6
GN_EPS = 64e-5
L2_EPS = 1e-12
NEG = -1e30
LEVELS = [1, 2, 4, 8, 16, 32, 64]

C_ID, C_CUM, C_UP, C_M1T, C_LEV, C_BLK, C_ONE, C_PAIR, C_END = np.cumsum([0, P, 2 * P, 2 * P, P, P * 6, P, P, 4]).tolist()
R_MU, R_A0, R_KK, R_KA, R_RK, R_GG, R_GB, R_N1, R_N2, R_END = np.cumsum(
    [0, NRW, NP, NP, NP, NP, NP, NP, KD, KD]).tolist()


def constants():
    s, t = np.arange(P)[:, None], np.arange(P)[None, :]
    mid = P // 2
    c = np.zeros((P, C_END), np.float32)
    c[:, C_ID:C_ID + P] = s == t
    c[:, C_CUM:C_CUM + P] = (s <= t).astype(np.float32) - (s < mid)
    c[:, C_CUM + P:C_CUM + 2 * P] = (s < t).astype(np.float32) - (s < mid)
    c[:, C_UP:C_UP + P] = s < t
    c[:, C_UP + P:C_UP + 2 * P] = s <= t

    def corner(b):
        return (s // (2 * b) == t // (2 * b)) & (s % (2 * b) >= b) & (t % (2 * b) < b)

    c[:, C_M1T:C_M1T + P] = corner(1).T
    for n, b in enumerate(LEVELS[1:]):
        c[:, C_LEV + n * P:C_LEV + (n + 1) * P] = corner(b)
    c[:, C_BLK:C_BLK + P] = s // HD == t // HD
    c[:, C_ONE:C_ONE + P] = 1
    c[:, C_PAIR:C_PAIR + 2] = s // HD == np.arange(2)[None, :]
    return c


def alibi():
    q, k = np.arange(P)[:, None], np.arange(BAND)[None, :] - HD
    seen = (k // HD <= q // HD) & (k // HD >= q // HD - 1)
    b = np.zeros((P, H * BAND), np.float32)
    for h in range(H):
        slope = np.float32(2.0 ** (-8.0 * (h + 1) / H))
        b[:, h * BAND:(h + 1) * BAND] = np.where(seen, -slope * np.abs(q - k), NEG)
    return b


def hybrid_block(nc, x, norm_mix_g, w_in, mu_shift, w0, w_up, a0, a_up, g_up, k_k, k_a, r_k, gn_g, gn_b,
                 sinks, w_out, norm_ffn_g, w_gate_up, w_down, norm_final_g, consts, bias_in, out):
    root = ExitStack()

    def sem(name):
        return root.enter_context(nc.semaphore(name))

    BASE = (nc.sbuf_base + 31) // 32 * 32
    K = 1024

    def at(name, kb, shape, dt=F32):
        return nc.alloc_sbuf_tensor_at(name, shape, dt, offset=BASE + int(kb * K))

    w_in_v = w_in[0].rearrange("(k p) n -> p k n", p=P)
    w_out_v = w_out[0].rearrange("(k p) n -> p k n", p=P)
    w_gu_v = w_gate_up[0].rearrange("(k p) n -> p k n", p=P)
    w_dn_v = w_down[0].rearrange("(k p) n -> p k n", p=P)
    sg_dram = nc.dram_tensor("sg_scratch", (T, W), F32, kind="Internal").ap()
    v_dram = nc.dram_tensor("v_scratch", (T, W), F32, kind="Internal").ap()

    with root:
        bank = [root.enter_context(nc.psum_tensor(f"bank{b}", [P, HALF], F32)) for b in range(8)]
        full = [sem(f"bank_full{b}") for b in range(8)]
        free = [sem(f"bank_free{b}") for b in range(8)]

        class Jobs:
            base = [0] * 8

            def __init__(self, table, ahead=(), late=()):
                table = list(table) + list(ahead) + list(late)
                self.ahead, self.late = dict(ahead), dict(late)
                self.bank_of, self.nth, self.per = dict(table), {}, [0] * 8
                for job, b in table:
                    self.nth[job] = self.per[b]
                    self.per[b] += 1
                self.start = list(Jobs.base)
                for _, b in ahead:
                    self.start[b] += 1

            def end(self, tiles):
                self.last = tiles - 1
                for b in range(8):
                    Jobs.base[b] += self.per[b] * tiles

            def before(self, job, t):
                b = self.bank_of[job]
                n = self.start[b] + self.nth[job]
                if isinstance(t, int):
                    if t == -1 and job in self.ahead:
                        n += sum(other == b for other in self.late.values())
                    if t == self.last and job in self.late:
                        n -= sum(other == b for other in self.ahead.values())
                return t * self.per[b] + n

            def claim(self, pe, job, t):
                b = self.bank_of[job]
                pe.wait_ge(free[b], self.before(job, t))
                return bank[b]

            def done(self, mm, job):
                mm.then_inc(full[self.bank_of[job]], 1)

            def result(self, eng, job, t):
                b = self.bank_of[job]
                eng.wait_ge(full[b], self.before(job, t) + 1)
                return bank[b]

            def emptied(self, eng, job, t):
                eng.wait_ge(free[self.bank_of[job]], self.before(job, t) + 1)

            def read(self, ins, job):
                ins.then_inc(free[self.bank_of[job]], 1)

        class Order:

            def __init__(self, eng, name):
                self.eng, self.sem, self.n, self.turn, self.per = eng, sem(name), 0, 0, 0

            def __call__(self, ins):
                ins.then_inc(self.sem, 1)
                self.n += 1
                self.eng.wait_ge(self.sem, self.turn + self.n)

            def tile(self, t, per):
                assert self.per in (0, per) and (not self.per or self.n == self.origin + per)
                if not self.per:
                    self.origin, self.per = self.n, per
                self.turn, self.n = t * per, self.origin

            def leave(self, tiles):
                assert self.n == self.origin + self.per
                self.n, self.turn, self.per = self.origin + self.per * tiles, 0, 0

        cst = at("cst", 0, [P, C_END])
        par = at("par", 7.0625, [P, R_END])
        small = at("small", 7.375, [P, 128])
        omka = small[:, 40:40 + NP]
        rn = small[:, 64:128]
        ident = cst[:, C_ID:C_ID + P]
        ones_blk = cst[:, C_BLK:C_BLK + P]
        ones = cst[:, C_ONE:C_ONE + P]
        rkv = at("rkv", 8, [P, 12, T])
        rT, kT, vT = rkv[:, 0:4, :], rkv[:, 4:8, :], rkv[:, 8:12, :]
        hhi, hlo = at("hhi", 56, [P, KD, T], F32R), at("hlo", 88, [P, KD, T], F32R)
        wg = at("wg", 120, [P, 2, T])
        att = at("att", 128, [P, NP, T])
        vt = at("vt", 144, [P, NT + 1, P])
        RING1 = 152
        praw = at("praw", 176, [P, 2, 4 + T])
        pdif = at("pdif", 184.25, [P, T])
        vpad = at("vpad", 176, [P, HD + T + HD])
        xin = at("xin", 184.5, [P, 4, D])
        kk2 = at("kk2", 188.5, [P, 2, HD + T])
        qst = at("qst", 197, [P, H, P])
        rsb = at("rsb", 201, [P, T])
        dg = at("dg", 188.5, [P, NT, P])
        prow = at("prow", 205.5, [P, P])
        kkn = at("kkn", 56, [P, NP, T])
        ab = at("ab", 72, [P, NP, T])
        sq = at("sq", 180.5, [P, T])
        sgo = at("sgo", 180.5, [P, 2, W])
        w_upz = at("w_upz", 184.5, [P, W])
        w0b = at("w0b", 186.5, [P, W])
        a_upz = at("a_upz", 205.5, [P, W])
        gup = at("gup", 94, [P, W])
        bias = at("bias", 96, [P, H, BAND])
        pt = at("pt", 108, [P, 2, 2, 2, P])
        tm = at("tm", 112, [P, 2, HALF])
        vst = at("vst", 148.5, [P, 2, P])
        vo = at("vo", 149.5, [P, W])
        st8 = at("st8", 151.5, [P, 6, H])
        snk = at("snk", 151.75, [P, H])
        mix = at("mix", 152, [P, 8, T])
        prod = at("prod", 184, [P, 2, HALF])
        sb = [at("scores0", 102, [P, H, BAND]), at("scores1", 88, [P, H, BAND])]
        rnx = at("rnx", 116, [P, 2, 4, 2, HD])
        gT = vT
        apad = at("apad", 88, [P, H, 2, P])
        NB = at("NB", 96, [P, H, 2, P])
        KB = at("KB", 104, [P, H, 2, P])
        X = at("X", 112, [P, H, P])
        XT = at("XT", 116, [P, H, P])
        Ts = at("Ts", 120, [P, H, P])
        alpha, rho, beta, kappa = (at(n, 124 + 2 * i, [P, NP, P]) for i, n in enumerate(("alpha", "rho", "beta", "kappa")))
        ein, einv, eex = (at(n, 132 + 2 * i, [P, NP, P]) for i, n in enumerate(("ein", "einv", "eex")))
        bt, kt_, rs_, us_ = (at(n, 138 + 2 * i, [P, W]) for i, n in enumerate(("bt", "kt", "rs", "us")))
        S, Sn = at("S", 146, [P, NP, P]), at("Sn", 148, [P, NP, P])
        oc, osq, on = at("oc", 150, [P, H, HD]), at("osq", 184, [P, H, HD]), at("on", 186, [P, H, HD])
        sgt, vtk = at("sgt", 188, [P, W]), at("vtk", 190, [P, W])
        sm = at("sm", 192, [P, 10, H])
        em, ec, fac, mean, var, rstd, expo = (sm[:, i, :] for i in range(7))
        mhi, mlo = at("mhi", 8, [P, KD, T], F32R), at("mlo", 40, [P, KD, T], F32R)
        x1 = at("x1", 72, [P, KD, T])
        RING2 = 104
        xtok = at("xtok", 196, [P, 4, HALF])
        GM = max(GROUPS)
        x1hi, x1lo = at("x1hi", 128, [P, KD, T], F32R), at("x1lo", 160, [P, KD, T], F32R)
        xsq = at("xsq", 192, [P, 2, T])
        dg2 = at("dg2", 192, [P, NT, P])
        rsb2 = at("rsb2", 200, [P, T])
        rms2 = small[:, 48:56]
        hidhi, hidlo = at("hidhi", 8, [P, GM, T], F32R), at("hidlo", 8 + 4 * GM, [P, GM, T], F32R)
        sil, hid, gat = at("sil", 192, [P, T]), at("hid", 196, [P, T]), at("gat", 56, [P, T])
        gfin = at("gfin", 128, [P, D])
        xo = at("xo", 132, [P, NT, HALF])
        fin = at("fin", 148, [P, NT, D])
        st = at("st", 180, [P, 4, NT])

        class Ring:
            def __init__(self, tag, kb):
                self.turns = 0
                self.raw = at(f"{tag}_raw", kb, [P, 2, KD, P])
                self.hi = at(f"{tag}_whi", kb + 8, [P, 2, KD, P], F32R)
                self.lo = at(f"{tag}_wlo", kb + 16, [P, 2, KD, P], F32R)
                self.landed = [sem(f"{tag}_landed{s}") for s in range(2)]
                self.hi_ready = sem(f"{tag}_hi")
                self.lo_ready = sem(f"{tag}_lo")

        class Layer:
            def __init__(self, ring, view, kt, turns):
                self.ring, self.view, self.kt, self.t0, self.n = ring, view, kt, ring.turns, turns
                ring.turns += turns
                self.J = Jobs([(f"{s}{h}", 2 * s + h) for s in range(2) for h in range(2)])
                self.J.end(turns)

            def load(self, sp, s, turn, column, rows=0, first=False):
                if not first:
                    sp.wait_ge(self.ring.lo_ready, 2 * turn + (2 * self.t0 + s - 1))
                sp.dma_start(self.ring.raw[:, s, 0:self.kt, :], self.view[:, rows:rows + self.kt, bass.ds(column, P)]
                             ).then_inc(self.ring.landed[s], 16)

            def split_hi(self, act, s, turn, first=False):
                act.wait_ge(self.ring.landed[s], 16 * turn + (16 * self.t0 + 16))
                if not first:
                    act.wait_ge(full[2 * s + 1], self.J.before(f"{s}1", turn))
                act.activation(self.ring.hi[:, s, 0:self.kt, :], self.ring.raw[:, s, 0:self.kt, :], ACT.Copy
                               ).then_inc(self.ring.hi_ready, 1)

            def split_lo(self, dve, s, turn):
                dve.wait_ge(self.ring.hi_ready, 2 * turn + (2 * self.t0 + s + 1))
                dve.tensor_tensor(self.ring.lo[:, s, 0:self.kt, :], self.ring.raw[:, s, 0:self.kt, :],
                                  self.ring.hi[:, s, 0:self.kt, :].bitcast(F32), ALU.subtract
                                  ).then_inc(self.ring.lo_ready, 1)

            def products(self, pe, s, turn, ahi, alo, ready=None, after=None):
                for half in range(2):
                    self.half(pe, s, half, turn, ahi, alo, ready if half == 0 else None)
                    if after is not None:
                        after(half)

            def half(self, pe, s, half, turn, ahi, alo, ready=None):
                pe.wait_ge(self.ring.lo_ready, 2 * turn + (2 * self.t0 + s + 1))
                o = self.J.claim(pe, f"{s}{half}", turn)
                c = slice(half * HALF, half * HALF + HALF)
                n, i = 3 * self.kt, 0
                for k in range(self.kt):
                    if ready is not None:
                        ready(k)
                    for wpart, apart in ((self.ring.hi, ahi), (self.ring.hi, alo), (self.ring.lo, ahi)):
                        mm = pe.matmul(o[:, :], wpart[:, s, k, :], apart[:, k, c], start=i == 0, stop=i == n - 1)
                        i += 1
                self.J.done(mm, f"{s}{half}")

            def some(self, pe, s, half, turn, ahi, alo, ks, low, high, ready):
                if low == 0:
                    pe.wait_ge(self.ring.lo_ready, 2 * turn + (2 * self.t0 + s + 1))
                    self.J.claim(pe, f"{s}{half}", turn)
                c = slice(half * HALF, half * HALF + HALF)
                for n in range(low, high):
                    if s == half == 0:
                        ready(n)
                    for i, (wpart, apart) in enumerate(((self.ring.hi, ahi), (self.ring.hi, alo), (self.ring.lo, ahi))):
                        mm = pe.matmul(bank[2 * s + half][:, :], wpart[:, s, ks[n], :], apart[:, ks[n], c],
                                       start=n == 0 and i == 0, stop=n == len(ks) - 1 and i == 2)
                if high == len(ks):
                    self.J.done(mm, f"{s}{half}")

            def products_late(self, pe, turn, ahi, alo, ready, between=None):
                every = range(self.kt)
                for low, high in ((0, self.kt - 1), (self.kt - 1, self.kt)):
                    for half in range(2):
                        self.some(pe, 0, half, turn, ahi, alo, every, low, high, ready)
                if between is not None:
                    between(0)
                self.half(pe, 1, 0, turn, ahi, alo)
                if between is not None:
                    between(1)
                self.half(pe, 1, 1, turn, ahi, alo)

        ring1, ring2 = Ring("ring1", RING1), Ring("ring2", RING2)

        def row(ap):
            return ap.rearrange("p a n -> p (a n)")

        s_cst, s_cst2, s_par = sem("s_cst"), sem("s_cst2"), sem("s_par")
        s_x = [sem(f"s_x{n}") for n in range(4)]
        s_ss, s_sq, s_c0, s_dg, s_hh = (sem(f"s1_{n}") for n in ("ss", "sq", "c0", "dg", "hh"))
        J1 = Jobs([("par", 7)])
        J1.end(1)
        J = Jobs([(f"x{j}", 4 + j) for j in range(4)])
        J.end(NT // 2)
        JR = Jobs([("rs0", 4), ("rs1", 5)])
        JR.end(1)
        IN = Layer(ring1, w_in_v, KD, NIN // 2)
        nsh = NRW // 2

        def stage1_sync(sp):
            sp.dma_start(cst[:, C_ID:C_ID + P], consts[:, C_ID:C_ID + P]).then_inc(s_cst, 16)
            for t in range(2):
                sp.dma_start(xin[:, t, :], x[0, t * P:(t + 1) * P, :]).then_inc(s_x[t], 16)
            rows = [(mu_shift, R_MU, NRW), (a0, R_A0, NP), (k_k, R_KK, NP), (k_a, R_KA, NP), (r_k, R_RK, NP),
                    (gn_g, R_GG, NP), (gn_b, R_GB, NP), (norm_mix_g, R_N1, KD), (norm_ffn_g, R_N2, KD)]
            for a, r, n in rows:
                v = a[0] if len(a.shape) == 2 else a[0].rearrange("h n -> (h n)")
                sp.dma_start(prow[r:r + n, :], v.rearrange("(j p) -> j p", p=P)).then_inc(s_par, 16)
            for t in range(2, 4):
                sp.dma_start(xin[:, t, :], x[0, t * P:(t + 1) * P, :]).then_inc(s_x[t], 16)
            for s in range(2):
                IN.load(sp, s, 0, s * P, first=True)
            for t in range(4, NT):
                J.result(sp, "x3", t // 2 - 2)
                sp.wait_ge(s_ss, t - 3)
                sp.dma_start(xin[:, t % 4, :], x[0, t * P:(t + 1) * P, :]).then_inc(s_x[t % 4], 16)
                if t == 5:
                    sp.dma_start(cst[:, C_CUM:], consts[:, C_CUM:]).then_inc(s_cst2, 16)

        def stage1_scalar(act):
            def squares(t):
                act.wait_ge(s_x[t % 4], 16 * (t // 4) + 16)
                if t:
                    act.wait_ge(s_ss, t)
                act.activation(praw[:, 0, 0:D], xin[:, t % 4, :], ACT.Square, accum_out=small[:, t:t + 1]).then_inc(s_ss, 1)

            def high(g):
                for j in range(4):
                    b = J.result(act, f"x{j}", g)
                    for i in range(2):
                        f = 2 * j + i
                        ins = act.activation(hhi[:, f, 2 * g * P:(2 * g + 2) * P], b[:, 2 * i * P:(2 * i + 2) * P],
                                             ACT.Copy, scale=par[:, R_N1 + f:R_N1 + f + 1])
                    ins.then_inc(s_hh, 1)

            squares(0)
            squares(1)
            act.wait_ge(s_c0, 1)
            J1.emptied(act, "par", 0)
            high(0)
            high(1)
            IN.split_hi(act, 0, 0, first=True)
            squares(2)
            squares(3)
            high(2)
            IN.split_hi(act, 1, 0, first=True)
            squares(4)
            squares(5)
            high(3)
            squares(6)
            squares(7)
            act.wait_ge(s_ss, NT)
            act.activation(small[:, 8:16], small[:, 0:8], ACT.Sqrt, bias=small[:, 32:33], scale=1.0 / D).then_inc(s_sq, 1)

        def stage1_tensor(pe):
            def transposes(g):
                for t in (2 * g, 2 * g + 1):
                    pe.wait_ge(s_x[t % 4], 16 * (t // 4) + 16)
                for j in range(4):
                    b = J.claim(pe, f"x{j}", g)
                    for i in range(2):
                        for t in range(2):
                            f = 2 * j + i
                            mm = pe.transpose(b[:, (2 * i + t) * P:(2 * i + t + 1) * P],
                                              xin[:, (2 * g + t) % 4, f * P:(f + 1) * P], ident)
                    J.done(mm, f"x{j}")

            def parts(g):
                for j in range(4):
                    J.emptied(pe, f"x{j}", g)

            pe.wait_ge(s_cst, 16)
            pe.wait_ge(s_par, 9 * 16)
            b = J1.claim(pe, "par", 0)
            J1.done(pe.transpose(b[:, 0:R_END], prow[0:R_END, :], ident[0:R_END, 0:R_END]), "par")
            for g in range(3):
                transposes(g)
            parts(1)
            IN.half(pe, 0, 0, 0, hhi, hlo)
            transposes(3)
            IN.half(pe, 1, 0, 0, hhi, hlo)
            parts(3)
            IN.half(pe, 0, 1, 0, hhi, hlo)
            pe.wait_ge(s_cst2, 16)
            for n in range(2):
                b = JR.claim(pe, f"rs{n}", 0)
                pe.wait_ge(s_dg, 4 * n + 4)
                for t in range(4):
                    mm = pe.matmul(b[:, t * P:(t + 1) * P], ones, dg[:, 4 * n + t, :], start=t == 0, stop=t == 3,
                                   skip_group_check=True)
                JR.done(mm, f"rs{n}")
            IN.half(pe, 1, 1, 0, hhi, hlo)

        def stage1_vector(dve):
            dve.memset(small[:, 32:33], EPS).then_inc(s_c0, 1)
            b = J1.result(dve, "par", 0)
            J1.read(dve.tensor_copy(par[:, :], b[:, 0:R_END]), "par")
            J1.emptied(dve, "par", 0)
            for g in range(NT // 2):
                for j in range(4):
                    b = J.result(dve, f"x{j}", g)
                    dve.wait_ge(s_hh, 4 * g + j + 1)
                    for i in range(2):
                        f = 2 * j + i
                        c = slice(2 * g * P, (2 * g + 2) * P)
                        ins = dve.scalar_tensor_tensor(hlo[:, f, c], b[:, 2 * i * P:(2 * i + 2) * P],
                                                       par[:, R_N1 + f:R_N1 + f + 1], hhi[:, f, c].bitcast(F32),
                                                       ALU.mult, ALU.subtract)
                    J.read(ins, f"x{j}")
                if g in (1, 2):
                    IN.split_lo(dve, g - 1, 0)
            order = Order(dve, "rs_order")
            dve.wait_ge(s_sq, 1)
            order(dve.reciprocal(small[:, 16:24], small[:, 8:16]))
            for t in range(NT):
                dve.tensor_scalar(dg[:, t, :], ident, small[:, 16 + t:17 + t], None, ALU.mult).then_inc(s_dg, 1)
            for n in range(2):
                b = JR.result(dve, f"rs{n}", 0)
                JR.read(dve.tensor_copy(rsb[:, n * HALF:(n + 1) * HALF], b[:, :]), f"rs{n}")
            JR.emptied(dve, "rs1", 0)

        s_shift, s_att, s_z2, s_ks = sem("s_shift"), sem("s_att"), sem("s_z2"), sem("s_ks")
        s_wd, s_gd, s_ssp = sem("s_wd"), sem("s_gd"), sem("s_ssp")
        s_aup, s_wup, s_gup, s_sgo, s_vd = sem("s_aup"), sem("s_wup"), sem("s_gup"), sem("s_sgo"), sem("s_vd")
        s_sgd = [sem("s_sgd0"), sem("s_sgd1")]
        s_rnx, s_tm, s_gm = sem("s4_rnx"), sem("s4_tm"), sem("s4_gm")
        s_sqr, s_nrm, s_root, s_rn, s_prod = (sem(f"s4_{n}") for n in ("sq", "nrm", "root", "rn", "prod"))
        VT = Jobs([(f"v{n}", 4 + n % 3) for n in range(NT)] + [("ss", 7)] + [("vt0", 4), ("vt1", 5), ("vt2", 6)]
                  + [(f"sg{n}", 4 + n % 4) for n in range(NT)])
        VT.end(1)

        def stage2_sync(sp):
            with sp.Fori(1, nsh) as i:
                for s in range(2):
                    IN.load(sp, s, i, (2 * i + s) * P)
            for s in range(2):
                IN.load(sp, s, nsh, (NRW + NP + s) * P)

            def store_v(*tiles):
                for n in tiles:
                    VT.emptied(sp, f"v{n}", 0)
                    sp.dma_start(v_dram[n * P:(n + 1) * P, :], vo[:, :]).then_inc(s_vd, 16)

            def load_q(s, turn):
                IN.load(sp, s, turn, (2 * turn + s - 2) * P)

            JR.result(sp, "rs1", 0)
            sp.dma_start(a_upz[HD:P, :], a_up[0]).then_inc(s_aup, 16)
            sp.wait_ge(s_shift, NRW + 1)
            sp.dma_start(w_upz[0:HD, :], w_up[0]).then_inc(s_wup, 16)
            sp.dma_start(w0b[:, :], w0.to_broadcast([P, W])).then_inc(s_wup, 16)
            for s in range(2):
                load_q(s, nsh + 1)
            store_v(0, 1, 2, 3)
            load_q(0, nsh + 2)
            store_v(4, 5)
            load_q(1, nsh + 2)
            store_v(6, 7)
            sp.wait_ge(s_att, 2)
            for e in range(2):
                sp.dma_start(kk2[HD * e:HD * e + HD, 1, :], kk2[HD - HD * e:P - HD * e, 0, :]).then_inc(s_ks, 16)
            for n in range(NT):
                sp.wait_ge(s_sgo, n + 1)
                sp.dma_start(sg_dram[n * P:(n + 1) * P, :], sgo[:, n % 2, :]).then_inc(s_sgd[n % 2], 16)

        def stage2_gpsimd(pool):
            pool.wait_ge(s_ss, NT)
            JR.result(pool, "rs1", 0)
            pool.memset(kk2[:, 0, 0:HD], 0.0).then_inc(s_z2, 1)
            pool.wait_ge(s_z2, 1)
            pool.memset(qst[:, :, :], 0.0).then_inc(s_z2, 1)
            pool.wait_ge(s_z2, 2)
            pool.memset(a_upz[0:HD, :], 0.0).then_inc(s_z2, 1)
            pool.wait_ge(s_z2, 3)
            pool.wait_ge(s_shift, NRW + 1)
            pool.memset(w_upz[HD:P, :], 0.0).then_inc(s_z2, 1)
            pool.wait_ge(s_z2, 4)

        def stage2_scalar(act):
            with act.Fori(1, nsh + 1) as i:
                for s in range(2):
                    IN.split_hi(act, s, i)

            def squares(p):
                if p:
                    act.wait_ge(s_ssp, p)
                act.activation(sq[:, :], kT[:, p, :], ACT.Square, scale=par[:, R_KK + p:R_KK + p + 1]).then_inc(s_sqr, 1)

            def keep_v(*tiles):
                for n in tiles:
                    b = VT.result(act, f"v{n}", 0)
                    if n:
                        act.wait_ge(s_vd, 16 * n)
                    VT.read(act.activation(vo[:, :], b[:, :], ACT.Copy), f"v{n}")

            def decay(*tiles):
                for n in tiles:
                    VT.emptied(act, f"sg{n}", 0)
                    act.activation(sgo[:, n % 2, :], sgo[:, n % 2, :], ACT.Sigmoid).then_inc(s_sgo, 1)

            act.wait_ge(s_shift, NRW + 1)
            act.activation(wg[0:HD, 0, :], wg[0:HD, 0, :], ACT.Tanh).then_inc(s_wd, 1)
            act.activation(wg[:, 1, :], wg[:, 1, :], ACT.Sigmoid).then_inc(s_gd, 1)
            squares(0)
            keep_v(0, 1)
            squares(1)
            IN.split_hi(act, 0, nsh + 1)
            keep_v(2, 3)
            squares(2)
            keep_v(4, 5)
            squares(3)
            IN.split_hi(act, 1, nsh + 1)
            keep_v(6, 7)
            for n in range(3):
                b = VT.result(act, f"vt{n}", 0)
                m = min(4, NT + 1 - 4 * n)
                VT.read(act.activation(vt[:, 4 * n:4 * n + m, :], b[:, 0:m * P], ACT.Copy), f"vt{n}")
            IN.split_hi(act, 0, nsh + 2)
            decay(0, 1, 2, 3)
            IN.split_hi(act, 1, nsh + 2)
            decay(4, 5, 6, 7)
            act.wait_ge(s_nrm, 1)
            act.activation(rn, rn, ACT.Sqrt).then_inc(s_root, 1)

        def stage2_vector(dve):
            order = Order(dve, "shift_order")
            order(dve.memset(praw[:, :, 0:4], 0.0))
            dve.sem_inc(s_shift, 1)

            def normed(dst, s, half, turn):
                b = IN.J.result(dve, f"{s}{half}", turn)
                IN.J.read(dve.tensor_tensor(dst, b[:, :], rsb[:, half * HALF:(half + 1) * HALF], ALU.mult), f"{s}{half}")

            def shift(s, turn, dst, mu):
                dve.wait_ge(s_shift, 2 * turn + (s + 1))
                for half in range(2):
                    normed(praw[:, s, 4 + half * HALF:4 + (half + 1) * HALF], s, half, turn)
                IN.J.emptied(dve, f"{s}0", turn)
                IN.J.emptied(dve, f"{s}1", turn)
                order(dve.tensor_tensor(pdif[:, :], praw[:, s, 3:3 + T], praw[:, s, 4:4 + T], ALU.subtract))
                dve.scalar_tensor_tensor(dst, pdif[:, :], mu, praw[:, s, 4:4 + T], ALU.mult, ALU.add
                                         ).then_inc(s_shift, 1)

            with dve.Fori(0, nsh - 1) as i:
                order.tile(i, 2)
                for s in range(2):
                    IN.split_lo(dve, s, i + 1)
                    shift(s, i, row(rkv[:, bass.ds(2 * i + s, 1), :]), par[:, bass.ds(2 * i + (s + R_MU), 1)])
            order.leave(nsh - 1)
            for s in range(2):
                IN.split_lo(dve, s, nsh)
                shift(s, nsh - 1, wg[:, s, :], par[:, R_MU + 12 + s:R_MU + 13 + s])
            dve.wait_ge(s_shift, NRW + 1)
            order(dve.memset(vpad[:, 0:HD], 0.0))
            order(dve.memset(vpad[:, HD + T:], 0.0))
            dve.wait_ge(s_z2, 2)
            for s, dst in ((0, kk2[:, 0, HD:]), (1, vpad[:, HD:HD + T])):
                IN.split_lo(dve, s, nsh + 1)
                for half in range(2):
                    normed(dst[:, half * HALF:(half + 1) * HALF], s, half, nsh)
                IN.J.emptied(dve, f"{s}0", nsh)
                IN.J.emptied(dve, f"{s}1", nsh)
                dve.sem_inc(s_att, 2)
            b = VT.result(dve, "ss", 0)
            VT.read(dve.tensor_scalar(rn, b[:, 0:8 * NT], L2_EPS * L2_EPS, None, ALU.max), "ss")
            VT.emptied(dve, "ss", 0)
            dve.sem_inc(s_nrm, 1)

            def queries(s, turn):
                for half in range(2):
                    normed(att[:, 2 * (turn - nsh - 1) + s, half * HALF:(half + 1) * HALF], s, half, turn)

            def decay(*tiles):
                for n in tiles:
                    b = VT.result(dve, f"sg{n}", 0)
                    if n >= 2:
                        dve.wait_ge(s_sgd[n % 2], 16 * (n // 2))
                    VT.read(dve.tensor_tensor(sgo[:, n % 2, :], b[:, :], w0b[:, :], ALU.add), f"sg{n}")

            dve.wait_ge(s_wup, 32)
            IN.split_lo(dve, 0, nsh + 2)
            queries(0, nsh + 1)
            decay(0, 1)
            queries(1, nsh + 1)
            decay(2, 3)
            IN.split_lo(dve, 1, nsh + 2)
            decay(4, 5, 6, 7)
            queries(0, nsh + 2)
            order(dve.tensor_scalar(omka, par[:, R_KA:R_KA + NP], -1.0, 1.0, ALU.mult, ALU.add))
            dve.wait_ge(s_root, 1)
            dve.reciprocal(rn, rn).then_inc(s_rn, 1)
            queries(1, nsh + 2)

        def stage2_tensor(pe):
            with pe.Fori(1, nsh) as i:
                for s in range(2):
                    IN.products(pe, s, i, hhi, hlo)

            def values(*tiles):
                for n in tiles:
                    b = VT.claim(pe, f"v{n}", 0)
                    for p in range(NP):
                        mm = pe.transpose(b[:, p * P:(p + 1) * P], vT[:, p, n * P:(n + 1) * P], ident)
                    VT.done(mm, f"v{n}")

            def sums(p):
                if p == 0:
                    VT.claim(pe, "ss", 0)
                pe.wait_ge(s_sqr, p + 1)
                for t in range(NT):
                    mm = pe.matmul(bank[7][:, 8 * t + 2 * p:8 * t + 2 * p + 2], sq[:, t * P:(t + 1) * P],
                                   cst[:, C_PAIR:C_PAIR + 2], start=t == 0 and p == 0, stop=t == NT - 1 and p == NP - 1,
                                   skip_group_check=True)
                mm.then_inc(s_ssp, 1) if p < NP - 1 else VT.done(mm, "ss")

            def attention_values():
                pe.wait_ge(s_att, 4)
                for n in range(3):
                    b = VT.claim(pe, f"vt{n}", 0)
                    m = min(4, NT + 1 - 4 * n)
                    for j in range(m):
                        mm = pe.transpose(b[:, j * P:(j + 1) * P], vpad[:, (4 * n + j) * P:(4 * n + j + 1) * P], ident)
                    VT.done(mm, f"vt{n}")

            def decay(*tiles):
                for n in tiles:
                    b = VT.claim(pe, f"sg{n}", 0)
                    VT.done(pe.matmul(b[:, :], wg[:, 0, n * P:(n + 1) * P], w_upz[:, :], start=True, stop=True), f"sg{n}")

            def last_turns(turn, s, half):
                n = 4 * (turn - nsh) + 2 * s + half
                if 1 <= n <= 4:
                    sums(n - 1)
                    values(2 * n - 2, 2 * n - 1)
                elif n == 5:
                    attention_values()
                elif 6 <= n <= 9:
                    if n == 6:
                        pe.wait_ge(s_wd, 1)
                        pe.wait_ge(s_wup, 32)
                        pe.wait_ge(s_z2, 4)
                    decay(2 * n - 12, 2 * n - 11)

            for turn in range(nsh, NIN // 2):
                for s in range(2):
                    IN.products(pe, s, turn, hhi, hlo, after=lambda half: last_turns(turn, s, half))

        s_bias, s_snk, s_zp = sem("s_bias"), sem("s_snk"), sem("s_zp")
        s_q, s_st, s_mx, s_pe, s_pn, s_pv = (sem(f"s3_{n}") for n in ("q", "v", "max", "exp", "norm", "pv"))
        B = Jobs([(f"a{n}", (4 + n) % 8) for n in range(8)])
        B.end(1)
        A = Jobs([(f"pt{p}", 4 + p % 2) for p in range(NP)] + [("pv", 6)],
                 [(f"sc{p}", p) for p in range(NP)] + [("rn", 0), ("g", 7), ("bs", 1)])
        A.end(NT)

        def pipelined(eng, body):
            body(-1, False, True)
            body(0, True, True)
            with eng.Fori(1, NT - 1) as t:
                body(t, True, True)
            body(NT - 1, True, False)

        def straight(eng, body):
            for t in range(-1, NT):
                body(t, t >= 0, t < NT - 1)

        def unit(n):
            return n // 2, slice((n % 2) * HALF, (n % 2 + 1) * HALF)

        def stage3_sync(sp):
            IN.J.result(sp, "11", IN.n - 1)
            sp.dma_start(gup[:, :], g_up[0]).then_inc(s_gup, 16)
            sp.dma_start(bias[:, :, :], bias_in.rearrange("p (h n) -> p h n", h=H)).then_inc(s_bias, 16)
            sp.dma_start(snk[:, :], sinks.to_broadcast([P, H])).then_inc(s_snk, 16)

        def stage3_gpsimd(pool):
            IN.J.emptied(pool, "11", IN.n - 1)
            IN.J.emptied(pool, "01", IN.n - 1)
            IN.J.emptied(pool, "10", IN.n - 1)
            IN.J.emptied(pool, "00", IN.n - 1)

            def body(t, live, more):
                if more:
                    if live:
                        A.result(pool, f"sc{NP - 1}", t - 1)
                    for e in range(2):
                        if e:
                            pool.wait_ge(s_q, 2 * t + 3)
                        elif t > 0:
                            pool.wait_ge(s_st, t)
                        elif t == 0:
                            pool.memset(pt[:, :, :, :, :], 0.0).then_inc(s_zp, 1)
                            pool.wait_ge(s_zp, 1)
                        r = slice(HD * e, HD * e + HD)
                        pool.tensor_copy(qst[r, e::2, :], att[r, :, (t + 1) * P:(t + 2) * P]).then_inc(s_q, 1)
                if live:
                    if t:
                        A.result(pool, "pv", t - 1)
                    pool.wait_ge(s_q, 2 * min(t + 2, NT))
                    if t and not more:
                        pool.wait_ge(s_st, t)
                    pool.tensor_copy(vst[:, :, :], vt[:, t:t + 2, :]).then_inc(s_st, 1)
            VT.emptied(pool, "vt2", 0)
            straight(pool, body)

        def stage3_tensor(pe):
            pe.wait_ge(s_aup, 16)
            for n in range(8):
                b = B.claim(pe, f"a{n}", 0)
                B.done(pe.matmul(b[:, :], a_upz[:, (n // 2) * P:(n // 2 + 1) * P],
                                 wg[:, 0, (n % 2) * HALF:(n % 2 + 1) * HALF], start=True, stop=True), f"a{n}")
            pe.wait_ge(s_ks, 32)
            pe.wait_ge(s_gup, 16)

            def body(t, live, more):
                n = t + 1
                if more:
                    pe.wait_ge(s_q, 2 * t + 4)
                    for p in range(NP):
                        b = A.claim(pe, f"sc{p}", t)
                        for e in range(2):
                            mm = pe.matmul(b[:, e * BAND:(e + 1) * BAND], qst[:, 2 * p + e, :],
                                           kk2[:, (p // 2) ^ e, (t + 1) * P:(t + 1) * P + BAND], start=e == 0,
                                           stop=e == 1, skip_group_check=True)
                        A.done(mm, f"sc{p}")

                def transposes(p):
                    if not live:
                        return
                    b = A.claim(pe, f"pt{p}", t)
                    for e in range(2):
                        h = 2 * p + e
                        pe.transpose(b[:, e * P:(e + 1) * P], sb[t % 2][:, h, 0:P], ident)
                    for e in range(2):
                        h = 2 * p + e
                        mm = pe.transpose(b[0:HD, (2 + e) * P:(3 + e) * P], sb[t % 2][:, h, P:BAND], ident)
                    A.done(mm, f"pt{p}")

                def values(p):
                    if not live:
                        return
                    A.emptied(pe, f"pt{p}", t)
                    for e in range(2):
                        for j in range(2):
                            mm = pe.matmul(bank[6][HD * e:HD * e + HD, p * P:(p + 1) * P],
                                           vst[:, j, (p // 2) * HD:(p // 2 + 1) * HD], pt[:, p % 2, j, e, :],
                                           start=p == 0 and j == 0, stop=p == NP - 1 and j == 1,
                                           skip_group_check=True)
                    mm.then_inc(s_pv, 1) if p < NP - 1 else A.done(mm, "pv")

                if not more:
                    cumulative(pe, -1)
                if live:
                    pe.wait_ge(s_pn, t + 1)
                    transposes(0)
                    transposes(1)
                    A.claim(pe, "pv", t)
                    pe.wait_ge(s_st, t + 1)
                if more:
                    pe.wait_ge(s_rnx, n + 1)
                    b = A.claim(pe, "rn", t)
                    for j in range(4):
                        mm = pe.matmul(b[:, j * P:(j + 1) * P], rnx[:, n % 2, j, :, :].rearrange("p a n -> p (a n)"),
                                       ident, start=j == 0, stop=j == 3, skip_group_check=True)
                    A.done(mm, "rn")
                    b = A.claim(pe, "g", t)
                    A.done(pe.matmul(b[:, :], gup[:, (n // 2) * P:(n // 2 + 1) * P], wg[:, 1, unit(n)[1]],
                                     start=True, stop=True), "g")
                values(0)
                transposes(2)
                values(1)
                transposes(3)
                values(2)
                if more:
                    pe.wait_ge(s_prod, n + 1)
                    b = A.claim(pe, "bs", t)
                    A.done(pe.matmul(b[:, :], ones_blk, prod[:, n % 2, :], start=True, stop=True), "bs")
                values(3)
            straight(pe, body)

        def stage3_scalar(act):
            for n in range(8):
                p, c = unit(n)
                b = B.result(act, f"a{n}", 0)
                B.read(act.activation(ab[:, p, c], b[:, :], ACT.Sigmoid, bias=par[:, R_A0 + p:R_A0 + p + 1]), f"a{n}")
            act.wait_ge(s_rn, 1)

            def spread(n):
                v = rn.rearrange("p (t h) -> p t h", h=H)[:, 4 * (n % 2):4 * (n % 2) + 4, 2 * (n // 2):2 * (n // 2) + 2]
                act.activation(rnx[:, n % 2, :, :, :], v.unsqueeze(3).to_broadcast([P, 4, 2, HD]), ACT.Copy
                               ).then_inc(s_rnx, 1)

            def key_scale(n):
                p, c = unit(n)
                if n >= 2:
                    act.wait_ge(s_prod, n - 1)
                act.activation(tm[:, n % 2, :], ab[:, p, c], ACT.Identity, bias=omka[:, p:p + 1],
                               scale=par[:, R_KA + p:R_KA + p + 1]).then_inc(s_tm, 1)

            for n in range(2):
                act.wait_ge(s_sgd[n], 16 * NT // 2)
            spread(0)
            for n in range(8):
                B.emptied(act, f"a{n}", 0)
            key_scale(0)

            def body(t, live, more):
                n = t + 1
                if not more:
                    exponentials(act, -1)
                if live:
                    if t == 0:
                        act.wait_ge(s_zp, 1)
                    for p in range(NP):
                        b = A.result(act, f"pt{p}", t)
                        if p >= 2:
                            act.wait_ge(s_pv, 3 * t + p - 1)
                        elif t:
                            A.result(act, "pv", t - 1)
                        act.activation(row(pt[:, p % 2, 0, :, :]), b[:, 0:2 * P], ACT.Copy)
                        ins = act.activation(row(pt[0:HD, p % 2, 1, :, :]), b[0:HD, 2 * P:4 * P], ACT.Copy)
                        A.read(ins, f"pt{p}")
                if more:
                    act.wait_ge(s_mx, 2 * t + 4)
                    act.activation(st8[:, 4, :], st8[:, 2, :], ACT.Exp).then_inc(s_pe, 1)
                    for h in range(H):
                        act.activation(sb[n % 2][:, h, :], sb[n % 2][:, h, :], ACT.Exp, bias=st8[:, 3, h:h + 1],
                                       accum_out=st8[:, 5, h:h + 1]).then_inc(s_pe, 1)
                    if n + 1 < NT:
                        if live:
                            A.result(act, "rn", t - 1)
                        spread(n + 1)
                        key_scale(n + 1)
                if live:
                    b = A.result(act, "pv", t)
                    A.read(act.activation(mix[:, NP:2 * NP, t * P:(t + 1) * P], b[:, :].rearrange("p (a n) -> p a n", a=NP),
                                          ACT.Copy), "pv")
                if more:
                    p, c = unit(n)
                    act.wait_ge(s_gm, n + 1)
                    A.read(act.activation(vT[:, p, c], bank[7][:, :], ACT.Copy, scale=par[:, R_GG + p:R_GG + p + 1]), "g")
            straight(act, body)

        def stage3_vector(dve):
            order = Order(dve, "prep_order")
            IN.J.result(dve, "11", IN.n - 1)
            for n in range(2):
                dve.wait_ge(s_sgd[n], 16 * NT // 2)
            dve.wait_ge(s_bias, 16)
            dve.wait_ge(s_snk, 16)

            def body(t, live, more):
                if live:
                    pr = sb[t % 2]
                    dve.wait_ge(s_pe, 9 * t + 9)
                    order(dve.tensor_tensor(st8[:, 5, :], st8[:, 5, :], st8[:, 4, :], ALU.add))
                    order(dve.reciprocal(st8[:, 5, :], st8[:, 5, :]))
                    dve.tensor_tensor(pr[:, :, :], pr[:, :, :], st8[:, 5, :].unsqueeze(2).to_broadcast([P, H, BAND]),
                                      ALU.mult).then_inc(s_pn, 1)
                if not more:
                    beta_kappa(dve, -1)
                    alpha_rho(dve, -1)
                if more:
                    sc = sb[(t + 1) % 2]
                    if t >= 1:
                        A.result(dve, f"pt{NP - 1}", t - 1)
                    for p in range(NP):
                        b = A.result(dve, f"sc{p}", t)
                        ins = dve.scalar_tensor_tensor(sc[:, 2 * p:2 * p + 2, :],
                                                       b[:, 0:2 * BAND].rearrange("p (a n) -> p a n", a=2), HD ** -0.5,
                                                       bias[:, 2 * p:2 * p + 2, :], ALU.mult, ALU.add)
                        A.read(ins, f"sc{p}")
                    A.emptied(dve, f"sc{NP - 1}", t)
                    if not live:
                        order(dve.memset(sc[:, :, 0:HD], NEG))
                    order(dve.tensor_reduce(st8[:, 0, :], sc[:, :, :], AX_X, ALU.max))
                    order(dve.tensor_tensor(st8[:, 1, :], st8[:, 0, :], snk[:, :], ALU.max))
                    dve.tensor_tensor(st8[:, 2, :], snk[:, :], st8[:, 1, :], ALU.subtract).then_inc(s_mx, 1)
                    dve.tensor_scalar(st8[:, 3, :], st8[:, 1, :], -1.0, None, ALU.mult).then_inc(s_mx, 1)
                    n = t + 1
                    p, c = unit(n)
                    b = A.result(dve, "rn", t)
                    A.read(dve.scalar_tensor_tensor(kkn[:, p, c], kT[:, p, c], par[:, R_KK + p:R_KK + p + 1], b[:, :],
                                                    ALU.mult, ALU.mult), "rn")
                    A.emptied(dve, "rn", t)
                    dve.wait_ge(s_tm, n + 1)
                    order(dve.tensor_tensor(kT[:, p, c], kT[:, p, c], tm[:, n % 2, :], ALU.mult))
                    if n >= 2:
                        A.result(dve, "bs", t - 2)
                    dve.scalar_tensor_tensor(prod[:, n % 2, :], rT[:, p, c], par[:, R_RK + p:R_RK + p + 1], kT[:, p, c],
                                             ALU.mult, ALU.mult).then_inc(s_prod, 1)
                    order(dve.scalar_tensor_tensor(ab[:, p, c], kkn[:, p, c], -1.0, ab[:, p, c], ALU.mult, ALU.mult))
                    b = A.result(dve, "bs", t)
                    A.read(dve.tensor_tensor(mix[:, p, c], b[:, :], vT[:, p, c], ALU.mult), "bs")
                    A.emptied(dve, "bs", t)
                    b = A.result(dve, "g", t)
                    dve.scalar_tensor_tensor(mix[:, p, c], mix[:, p, c], par[:, R_GB + p:R_GB + p + 1], b[:, :],
                                             ALU.add, ALU.mult).then_inc(s_gm, 1)
            straight(dve, body)
            A.emptied(dve, "pv", NT - 1)
            A.emptied(dve, "g", NT - 2)
            dve.wait_ge(s_gm, NT)

        table = []
        for n in range(1, 7):
            table += [(f"t{n}{g}", 6 * g) for g in range(2)]
            table += [(f"x{n}{g}", 2 + g) for g in range(2) if n < 6]
            table += [(f"y{n}{g}", 4 + g) for g in range(2)]
        table += [("R", 0), ("O", 6), ("U", 2), ("S", 3), ("kb0", 1), ("kb1", 7), ("kb2", 1), ("kb3", 7)]
        C = Jobs(table, [("cum0", 1), ("cum1", 7), ("ab0", 4), ("ab1", 5), ("ab2", 1), ("ab3", 7), ("bt", 1), ("kt", 7),
                         ("x0", 0), ("x1", 3)], [("ot", 7)])
        C.end(NT)
        XA = Jobs([("x", 1)])
        XA.end(NT)
        XB = Jobs([("0", 4), ("1", 5)])
        XB.end(NT // 2)
        OUT = Layer(ring2, w_out_v, KD, KD // 2)
        s_m, s_mlo, s_xt = sem("s_mhi"), sem("s_mlo"), [sem(f"s_xt{n}") for n in range(4)]
        MIX_ORDER = [4, 5, 6, 7, 0, 1, 2, 3]
        s_z5, s_seen, s_mix = sem("s_z5"), sem("s_seen"), sem("s5_mix")

        def cumulative(pe, t):
            pe.wait_ge(s_sgt, 16 * t + 32)
            for j in range(2):
                b = C.claim(pe, f"cum{j}", t)
                for p in (2 * j, 2 * j + 1):
                    mm = pe.matmul(b[:, (p % 2) * 2 * P:(p % 2 + 1) * 2 * P], sgt[:, p * P:(p + 1) * P],
                                   cst[:, C_CUM:C_CUM + 2 * P], start=p % 2 == 0, stop=p % 2 == 1,
                                   skip_group_check=True)
                C.done(mm, f"cum{j}")

        def exponentials(act, t):
            for j in range(2):
                b = C.result(act, f"cum{j}", t)
                v = b[:, :].rearrange("p (a n) -> p a n", a=2)
                c = slice(2 * j, 2 * j + 2)
                act.activation(ein[:, c, :], v[:, :, 0:P], ACT.Exp, scale=-DECAY)
                act.activation(einv[:, c, :], v[:, :, 0:P], ACT.Exp, scale=DECAY)
                act.activation(em[:, c], v[:, :, P], ACT.Exp, scale=DECAY)
                ins = act.activation(eex[:, c, :], v[:, :, P:2 * P], ACT.Exp, scale=-DECAY)
                C.read(ins, f"cum{j}")

        def beta_kappa(dve, t):
            c1 = bass.ds((t + 1) * P, P)
            C.emptied(dve, "cum1", t)
            dve.tensor_tensor(beta[:, :, :], ab[:, :, c1], einv[:, :, :], ALU.mult).then_inc(s_bk, 1)
            dve.tensor_tensor(kappa[:, :, :], kT[:, :, c1], einv[:, :, :], ALU.mult).then_inc(s_bk, 1)

        def alpha_rho(dve, t):
            c1 = bass.ds((t + 1) * P, P)
            dve.tensor_tensor(alpha[:, :, :], kkn[:, :, c1], eex[:, :, :], ALU.mult).then_inc(s_ar, 1)
            dve.tensor_tensor(rho[:, :, :], rT[:, :, c1], ein[:, :, :], ALU.mult).then_inc(s_ar, 1)

        def mix_high(act, n):
            k = MIX_ORDER[n]
            act.activation(mhi[:, k, :], mix[:, k, :], ACT.Copy).then_inc(s_m, 1)

        def mix_low(dve, n):
            k = MIX_ORDER[n]
            dve.wait_ge(s_m, n + 1)
            dve.tensor_tensor(mlo[:, k, :], mix[:, k, :], mhi[:, k, :].bitcast(F32), ALU.subtract).then_inc(s_mlo, 1)

        def is_last(t):
            return isinstance(t, int) and t == NT - 1

        def second_half(eng, odd):
            for n in range(odd, NT, 2):
                b = XB.result(eng, f"{odd}", n // 2)
                dst, src = x1[:, 4:8, n * P:(n + 1) * P], b[:, :].rearrange("p (a n) -> p a n", a=4)
                XB.read(eng.tensor_copy(dst, src) if odd else eng.activation(dst, src, ACT.Copy), f"{odd}")

        def is_first(t):
            return isinstance(t, int) and t == 0

        (s_sgt, s_vtk, s_ec, s_bk, s_ar, s_o1, s_pad, s_x1t, s_S, s_oc, s_osq, s_var, s_rstd, s_on) = (
            sem(f"s5_{n}") for n in ("sg", "v", "ec", "beta_kappa", "alpha_rho", "o1", "pad", "x1t", "S", "oc", "osq",
                                     "var", "rstd", "on"))
        up = cst[:, C_UP:C_UP + 2 * P].bitcast(U32).unsqueeze(1).to_broadcast([P, 2, 2 * P])
        def stage5_sync(sp):
            def body(t, live, more):
                if more:
                    if live:
                        C.result(sp, "cum1", t - 1)
                    if not live:
                        A.result(sp, f"sc{NP - 1}", NT - 2)
                    sp.dma_start(sgt[:, :], sg_dram[bass.ds((t + 1) * P, P), :]).then_inc(s_sgt, 16)
                    if live:
                        C.result(sp, "S", t)
                    else:
                        sp.wait_ge(s_vd, 16 * NT)
                    sp.dma_start(vtk[:, :], v_dram[bass.ds((t + 1) * P, P), :]).then_inc(s_vtk, 16)
            pipelined(sp, body)

        def stage5_gpsimd(pool):
            A.result(pool, f"sc{NP - 1}", NT - 2)
            through = {2: lambda: (A.emptied(pool, f"sc{NP - 1}", NT - 2), A.result(pool, f"pt{NP - 1}", NT - 2)),
                       3: lambda: A.result(pool, f"pt{NP - 1}", NT - 1),
                       4: lambda: A.result(pool, "pv", NT - 1)}
            for n, (m, value) in enumerate(((ec, 1.0), (expo, -0.5), (NB[:, :, :, :], 0.0), (apad[:, :, :, :], 0.0),
                                            (Sn[:, :, :], 0.0), (KB[:, :, :, :], 0.0))):
                if n in through:
                    through[n]()
                if n:
                    pool.wait_ge(s_z5, n)
                pool.memset(m, value).then_inc(s_z5, 1)
            pool.wait_ge(s_z5, 6)

            def body(t, live, more):
                if live:
                    pool.wait_ge(s_var, t + 1)
                    pool.sem_inc(s_seen, 1)
                    pool.tensor_scalar(rstd, var, 1.0 / HD, GN_EPS, ALU.mult, ALU.add).then_inc(s_rstd, 1)
                    pool.wait_ge(s_rstd, 2 * t + 1)
                    pool.tensor_tensor(rstd, rstd, expo, ALU.pow).then_inc(s_rstd, 1)
            pipelined(pool, body)

        def stage5_tensor(pe):
            def four(b, g, lhs, rhs):
                for j in range(4):
                    mm = pe.matmul(b[:, j * P:(j + 1) * P], lhs(4 * g + j), rhs(4 * g + j), start=j == 0, stop=j == 3,
                                   skip_group_check=True)
                return mm

            def x_tile(n):
                b = XA.claim(pe, "x", n)
                pe.wait_ge(s_xt[n % 4], 16 * (n // 4) + 16)
                for k in range(4):
                    mm = pe.transpose(b[:, k * P:(k + 1) * P], xtok[:, n % 4, k * P:(k + 1) * P], ident)
                XA.done(mm, "x")

            def levels(t, low, high):
                for n in range(low, high):
                    if is_last(t) and n >= 3:
                        x_tile(2 * (n - 3))
                    for g in range(2):
                        b = C.claim(pe, f"t{n}{g}", t)
                        if n == 1:
                            C.emptied(pe, f"x{g}", t - 1)
                        else:
                            C.emptied(pe, f"x{n - 1}{g}", t)
                        C.done(four(b, g, lambda h: NB[:, h, 0, :], lambda h: X[:, h, :]), f"t{n}{g}")
                    if is_last(t) and n >= 3:
                        x_tile(2 * (n - 3) + 1)
                    for g in range(2):
                        C.emptied(pe, f"t{n}{g}", t)
                        b = C.claim(pe, f"y{n}{g}", t)
                        C.done(four(b, g, lambda h: Ts[:, h, :], lambda h: XT[:, h, :]), f"y{n}{g}")
                    for g in range(2):
                        if n < 6:
                            b = C.claim(pe, f"x{n}{g}", t)
                            C.emptied(pe, f"y{n}{g}", t)
                            for j in range(4):
                                mm = pe.transpose(b[:, j * P:(j + 1) * P], XT[:, 4 * g + j, :], ident)
                            C.done(mm, f"x{n}{g}")

            def against(kind, m, t, *groups):
                for g in groups:
                    b = C.claim(pe, f"{kind}{g}", t)
                    for h in (2 * g, 2 * g + 1):
                        mm = pe.matmul(b[:, (h % 2) * 2 * P:(h % 2 + 1) * 2 * P], m[:, h // 2, :],
                                       apad[:, h, :, :].rearrange("p a n -> p (a n)"), start=h % 2 == 0,
                                       stop=h % 2 == 1, skip_group_check=True)
                    C.done(mm, f"{kind}{g}")

            def outputs(t):
                b = C.claim(pe, "ot", t)
                pe.wait_ge(s_on, t + 1)
                for p in range(NP):
                    mm = pe.transpose(b[:, p * P:(p + 1) * P],
                                      on[:, 2 * p:2 * p + 2, :].rearrange("p a n -> p (a n)"), ident)
                C.done(mm, "ot")

            def body(t, live, more):
                if live:
                    levels(t, 1, 2)
                    if not is_first(t):
                        outputs(t - 1)
                    against("kb", kappa, t, 0, 1)
                    levels(t, 2, 3)
                    against("kb", kappa, t, 2, 3)
                if live and more:
                    cumulative(pe, t)
                if live:
                    levels(t, 3, 7)
                    pe.wait_ge(s_S, t + 1)
                    pe.wait_ge(s_vtk, 16 * t + 16)
                    b = C.claim(pe, "R", t)
                    for p in range(NP):
                        pe.matmul(b[:, p * P:(p + 1) * P], alpha[:, p, :], S[:, p, :], start=p == 0, stop=False,
                                  skip_group_check=True)
                    for h in range(H):
                        mm = pe.matmul(b[:, h * HD:(h + 1) * HD], KB[:, h, 0, :], vtk[:, h * HD:(h + 1) * HD],
                                       start=False, stop=h == H - 1, skip_group_check=True)
                    C.done(mm, "R")
                    bo = C.claim(pe, "O", t)
                    for h in range(H):
                        pe.matmul(bo[:, h * HD:(h + 1) * HD], KB[:, h, 1, :], vtk[:, h * HD:(h + 1) * HD], start=h == 0,
                                  stop=False, skip_group_check=True)
                    for p in range(NP):
                        mm = pe.matmul(bo[:, p * P:(p + 1) * P], rho[:, p, :], S[:, p, :], start=False, stop=False,
                                       skip_group_check=True)
                    mm.then_inc(s_o1, 1)
                    b = C.claim(pe, "U", t)
                    C.emptied(pe, "R", t)
                    for g in range(2):
                        C.emptied(pe, f"y6{g}", t)
                    for h in range(H):
                        mm = pe.matmul(b[:, h * HD:(h + 1) * HD], XT[:, h, :], rs_[:, h * HD:(h + 1) * HD],
                                       start=h == 0, stop=h == H - 1, skip_group_check=True)
                    C.done(mm, "U")
                    b = C.claim(pe, "S", t)
                    for p in range(NP):
                        c = slice(p * P, (p + 1) * P)
                        pe.matmul(b[:, c], kt_[:, c], vtk[:, c], start=p == 0, stop=False, skip_group_check=True)
                    C.emptied(pe, "U", t)
                    for p in range(NP):
                        c = slice(p * P, (p + 1) * P)
                        mm = pe.matmul(b[:, c], bt[:, c], us_[:, c], start=False, stop=p == NP - 1,
                                       skip_group_check=True)
                    C.done(mm, "S")
                    for h in range(H):
                        mm = pe.matmul(bo[:, h * HD:(h + 1) * HD], NB[:, h, 1, :], us_[:, h * HD:(h + 1) * HD],
                                       start=False, stop=h == H - 1, skip_group_check=True)
                    C.done(mm, "O")
                if more:
                    pe.wait_ge(s_pad, 4 * t + 8)
                    pe.wait_ge(s_bk, 2 * t + 4)
                    against("ab", beta, t, 0, 1, 2, 3)
                    for kind, m in (("bt", beta), ("kt", kappa)):
                        b = C.claim(pe, kind, t)
                        for p in range(NP):
                            mm = pe.transpose(b[:, p * P:(p + 1) * P], m[:, p, :], ident)
                        C.done(mm, kind)
                if more:
                    for g in range(2):
                        pe.wait_ge(s_x1t, 2 * t + (g + 3))
                        b = C.claim(pe, f"x{g}", t)
                        for j in range(4):
                            mm = pe.transpose(b[:, j * P:(j + 1) * P], XT[:, 4 * g + j, :], ident)
                        C.done(mm, f"x{g}")
            pipelined(pe, body)
            for n in range(NT):
                b = XB.claim(pe, f"{n % 2}", n // 2)
                pe.wait_ge(s_xt[n % 4], 16 * (n // 4) + 48)
                for k in range(4):
                    mm = pe.transpose(b[:, k * P:(k + 1) * P], xtok[:, n % 4, k * P:(k + 1) * P], ident)
                XB.done(mm, f"{n % 2}")
            for s in range(2):
                for half in range(2):
                    OUT.some(pe, s, half, 0, mhi, mlo, MIX_ORDER, 0, 4, lambda n: pe.wait_ge(s_mlo, n + 1))
                if s == 0:
                    outputs(NT - 1)
            for s in range(2):
                for half in range(2):
                    OUT.some(pe, s, half, 0, mhi, mlo, MIX_ORDER, 4, KD, lambda n: pe.wait_ge(s_mlo, n + 1))

        def stage5_scalar(act):
            def keep_x(job, t):
                for g in range(2):
                    b = C.result(act, f"{job}{g}", t)
                    C.read(act.activation(X[:, 4 * g:4 * g + 4, :].rearrange("p a n -> p (a n)"), b[:, :], ACT.Copy),
                           f"{job}{g}")

            def body(t, live, more):
                if live:
                    for n in (1, 2):
                        keep_x(f"x{n}", t)
                        if is_last(t):
                            mix_high(act, 2 * n - 2)
                            mix_high(act, 2 * n - 1)
                if live and more:
                    act.wait_ge(s_S, t + 1)
                    act.activation(ec[:, 0:NP], ein[:, :, P - 1], ACT.Copy).then_inc(s_ec, 1)
                    act.wait_ge(s_ec, t + 1)
                    exponentials(act, t)
                if live:
                    for n in range(3, 7):
                        if is_last(t):
                            for m in (2 * n - 6, 2 * n - 5):
                                b = XA.result(act, "x", m)
                                XA.read(act.activation(x1[:, 0:4, m * P:(m + 1) * P],
                                                       b[:, :].rearrange("p (a n) -> p a n", a=4), ACT.Copy), "x")
                        if n < 6:
                            keep_x(f"x{n}", t)
                if live:
                    for kind, m in (("R", rs_), ("U", us_)):
                        b = C.result(act, kind, t)
                        C.read(act.activation(m[:, :], b[:, :], ACT.Copy), kind)
                if is_last(t):
                    for s in range(2):
                        OUT.split_hi(act, s, 0, first=True)
                if more:
                    act.wait_ge(s_ar, 2 * t + 4)
                    if not live:
                        act.wait_ge(s_z5, 4)
                    for i, m in enumerate((alpha, rho)):
                        for e in range(2):
                            r = slice(HD * e, HD * e + HD)
                            act.activation(apad[r, e::2, i, :], m[r, :, :], ACT.Copy).then_inc(s_pad, 1)
                if live:
                    act.wait_ge(s_oc, t + 1)
                    act.activation(osq[:, :, :], oc[:, :, :], ACT.Square).then_inc(s_osq, 1)
                if more:
                    for kind, m in (("bt", bt), ("kt", kt_)):
                        b = C.result(act, kind, t)
                        C.read(act.activation(m[:, :], b[:, :], ACT.Copy), kind)
                    keep_x("x", t)
            pipelined(act, body)

        def stage5_vector(dve):
            head, tail = Order(dve, "rec_order0"), Order(dve, "rec_order1")

            def levels(t, low, high, between=None):
                for n in range(low, high):
                    m = cst[:, C_LEV + (n - 1) * P:C_LEV + n * P].unsqueeze(1).to_broadcast([P, 4, P])
                    for g in range(2):
                        q = slice(4 * g, 4 * g + 4)
                        b = C.result(dve, f"t{n}{g}", t)
                        if n > 1:
                            C.result(dve, f"y{n - 1}{g}", t)
                        C.read(dve.tensor_tensor(Ts[:, q, :], b[:, :].rearrange("p (h n) -> p h n", h=4), m, ALU.mult),
                               f"t{n}{g}")
                    if between is not None:
                        between()
                    for g in range(2):
                        q = slice(4 * g, 4 * g + 4)
                        b = C.result(dve, f"y{n}{g}", t)
                        C.read(dve.tensor_tensor(XT[:, q, :], b[:, :].rearrange("p (h n) -> p h n", h=4), XT[:, q, :],
                                                 ALU.add), f"y{n}{g}")

            def masked(kind, m, t, *groups):
                for g in groups:
                    b = C.result(dve, f"{kind}{g}", t)
                    dve.sem_inc(s_seen, 1)
                    ins = dve.copy_predicated(m[:, 2 * g:2 * g + 2, :, :].rearrange("p h a n -> p h (a n)"), up,
                                              b[:, :].rearrange("p (h n) -> p h n", h=2))
                    C.read(ins, f"{kind}{g}")

            def normalise(t):
                dve.wait_ge(s_rstd, 2 * t + 2)
                dve.tensor_tensor(on[:, :, :], oc[:, :, :], rstd.unsqueeze(2).to_broadcast([P, H, HD]), ALU.mult
                                  ).then_inc(s_on, 1)

            def outputs(t):
                c = bass.ds(t * P, P)
                b = C.result(dve, "ot", t)
                C.read(dve.tensor_tensor(oc[:, :, :].rearrange("p (a b) n -> p a (b n)", a=NP),
                                         b[:, :].rearrange("p (a n) -> p a n", a=NP), gT[:, :, c], ALU.mult), "ot")
                C.emptied(dve, "ot", t)
                dve.tensor_tensor(mix[:, 0:NP, c], oc[:, :, :].rearrange("p (a b) n -> p a (b n)", a=NP),
                                  mix[:, 0:NP, c], ALU.add).then_inc(s_mix, 1)

            def body(t, live, more):
                if live:
                    head.tile(t, 2)
                    if is_first(t):
                        levels(t, 1, 2)
                        dve.wait_ge(s_z5, 6)
                    else:
                        levels(t, 1, 2, lambda: normalise(t - 1))
                        outputs(t - 1)
                    masked("kb", KB, t, 0, 1)
                    levels(t, 2, 3)
                    masked("kb", KB, t, 2, 3)
                    if is_last(t):
                        for n in range(4):
                            levels(t, 3 + n, 4 + n, lambda: mix_low(dve, n))
                    else:
                        levels(t, 3, 5)
                if live and more:
                    beta_kappa(dve, t)
                if live and not is_last(t):
                    levels(t, 5, 7)
                if live and more:
                    dve.wait_ge(s_o1, t + 1)
                    alpha_rho(dve, t)
                if live:
                    b = C.result(dve, "S", t)
                    C.read(dve.tensor_tensor(Sn[:, :, :], b[:, :].rearrange("p (a n) -> p a n", a=NP), S[:, :, :],
                                             ALU.add), "S")
                    if is_last(t):
                        OUT.split_lo(dve, 0, 0)
                    b = C.result(dve, "O", t)
                    o = b[:, :].rearrange("p (h n) -> p h n", h=H)
                    head(dve.tensor_reduce(mean, o, AX_X, ALU.add))
                    head(dve.tensor_scalar(mean, mean, 1.0 / HD, None, ALU.mult))
                    ins = dve.tensor_tensor(oc[:, :, :], o, mean.unsqueeze(2).to_broadcast([P, H, HD]), ALU.subtract)
                    C.read(ins, "O")
                    C.emptied(dve, "O", t)
                    dve.sem_inc(s_oc, 1)
                if more:
                    tail.tile(t + 1, 3)
                    if not live:
                        dve.wait_ge(s_z5, 5)
                    for g in range(2):
                        q = slice(4 * g, 4 * g + 4)
                        masked("ab", NB, t, 2 * g, 2 * g + 1)
                        C.emptied(dve, f"ab{2 * g + 1}", t)
                        tail(dve.tensor_tensor(Ts[:, q, :], NB[:, q, 0, :],
                                               cst[:, C_M1T:C_M1T + P].unsqueeze(1).to_broadcast([P, 4, P]), ALU.mult))
                        dve.tensor_tensor(XT[:, q, :], Ts[:, q, :], ident.unsqueeze(1).to_broadcast([P, 4, P]), ALU.add
                                          ).then_inc(s_x1t, 1)
                if live:
                    dve.wait_ge(s_osq, t + 1)
                    dve.tensor_reduce(var, osq[:, :, :], AX_X, ALU.add).then_inc(s_var, 1)
                if more:
                    if live:
                        dve.wait_ge(s_ec, t + 1)
                        C.emptied(dve, "S", t)
                    tail(dve.tensor_tensor(fac[:, 0:NP], ec[:, 0:NP], em[:, 0:NP], ALU.mult))
                    for p in range(NP):
                        ins = dve.scalar_tensor_tensor(S[:, p, :], Sn[:, p, :], fac[:, p:p + 1], ones_blk, ALU.mult,
                                                       ALU.mult)
                    ins.then_inc(s_S, 1)
            pipelined(dve, body)
            OUT.split_lo(dve, 1, 0)
            second_half(dve, 1)
            normalise(NT - 1)
            outputs(NT - 1)

        s_x1, s_xsq, s_x1hi, s_x1lo, s_acc, s_dg2 = (sem(f"s6_{n}") for n in ("x1", "xsq", "x1hi", "x1lo", "acc", "diag"))
        N2 = Jobs([("col", 4), ("rs0", 4), ("rs1", 5)])
        N2.end(1)

        def layer_of(b):
            return OUT if b < KD else following[0]

        def turn_of(b):
            return b % KD // 2

        def stage6_sync(sp):
            for n in range(2 * NT):
                if n >= 4:
                    m = n - 4
                    XA.result(sp, "x", m) if m < NT else XB.result(sp, f"{m % 2}", (m - NT) // 2)
                t, g = n % NT, n // NT
                sp.dma_start(xtok[:, n % 4, :], x[0, t * P:(t + 1) * P, g * HALF:(g + 1) * HALF]).then_inc(s_xt[n % 4], 16)
                if n == NT + 3:
                    sp.wait_ge(s_o1, NT)
                    for s in range(2):
                        OUT.load(sp, s, 0, s * P, first=True)
            for turn in range(1, OUT.n):
                for s in range(2):
                    OUT.load(sp, s, turn, (2 * turn + s) * P)

        def stage6_tensor(pe):
            for turn in range(1, OUT.n):
                for s in range(2):
                    OUT.products(pe, s, turn, mhi, mlo)

        def norm2_tensor(pe):
            def between(s):
                if s == 0:
                    b = N2.claim(pe, "col", 0)
                    pe.wait_ge(s_acc, KD - 1)
                    for t in range(NT):
                        mm = pe.matmul(b[:, t:t + 1], rsb2[:, t * P:(t + 1) * P], ones[:, 0:1], start=t == 0,
                                       stop=t == NT - 1, skip_group_check=True)
                    N2.done(mm, "col")
                else:
                    for half in range(2):
                        b = N2.claim(pe, f"rs{half}", 0)
                        pe.wait_ge(s_dg2, 4 * half + 5)
                        for t in range(4):
                            mm = pe.matmul(b[:, t * P:(t + 1) * P], ones, dg2[:, 4 * half + t, :], start=t == 0,
                                           stop=t == 3, skip_group_check=True)
                        N2.done(mm, f"rs{half}")
            return between

        def stage6_scalar(act):
            second_half(act, 0)
            act.wait_ge(s_mix, NT)
            for n in range(4, KD):
                mix_high(act, n)
            for k in range(KD):
                layer_of(k + 2).split_hi(act, k % 2, turn_of(k + 2))
                act.wait_ge(s_x1, 2 * k + 2)
                act.wait_ge(s_mlo, KD)
                act.activation(x1hi[:, k, :], x1[:, k, :], ACT.Copy, scale=par[:, R_N2 + k:R_N2 + k + 1]).then_inc(s_x1hi, 1)
                if k >= 2:
                    act.wait_ge(s_acc, k - 1)
                act.activation(xsq[:, k % 2, :], x1[:, k, :], ACT.Square).then_inc(s_xsq, 1)
            b = N2.result(act, "col", 0)
            N2.read(act.activation(rms2, b[:, 0:NT], ACT.Sqrt, bias=small[:, 32:33], scale=1.0 / D), "col")
            for half in range(2):
                b = N2.result(act, f"rs{half}", 0)
                N2.read(act.activation(rsb2[:, half * HALF:(half + 1) * HALF], b[:, :], ACT.Copy), f"rs{half}")

        def stage6_vector(dve):
            for n in range(4, KD):
                mix_low(dve, n)
            XA.emptied(dve, "x", NT - 1)
            for n in range(2):
                XB.emptied(dve, f"{n}", NT // 2 - 1)

            def add_squares(k):
                dve.wait_ge(s_xsq, k + 1)
                if k > 1:
                    dve.wait_ge(s_acc, k - 1)
                dve.tensor_tensor(rsb2[:, :], xsq[:, 0, :] if k == 1 else rsb2[:, :], xsq[:, k % 2, :], ALU.add
                                  ).then_inc(s_acc, 1)

            for k in range(KD):
                s, turn = k % 2, k // 2
                layer_of(k + 2).split_lo(dve, s, turn_of(k + 2))
                for half in range(2):
                    b = OUT.J.result(dve, f"{s}{half}", turn)
                    v = x1[:, k, half * HALF:(half + 1) * HALF]
                    OUT.J.read(dve.tensor_tensor(v, b[:, :], v, ALU.add), f"{s}{half}")
                    OUT.J.emptied(dve, f"{s}{half}", turn)
                    dve.sem_inc(s_x1, 1)
                if k >= 2:
                    add_squares(k - 1)
                dve.wait_ge(s_x1hi, k + 1)
                dve.scalar_tensor_tensor(x1lo[:, k, :], x1[:, k, :], par[:, R_N2 + k:R_N2 + k + 1],
                                         x1hi[:, k, :].bitcast(F32), ALU.mult, ALU.subtract).then_inc(s_x1lo, 1)
            add_squares(KD - 1)
            N2.emptied(dve, "col", 0)
            dve.reciprocal(rms2, rms2).then_inc(s_dg2, 1)
            dve.wait_ge(s_dg2, 1)
            dve.wait_ge(s_acc, KD - 1)
            for t in range(NT):
                dve.tensor_scalar(dg2[:, t, :], ident, rms2[:, t:t + 1], None, ALU.mult).then_inc(s_dg2, 1)

        s_gat, s_sil, s_hid, s_hh7, s_hl7 = (sem(f"s7_{n}") for n in ("gat", "sil", "hid", "hid_high", "hid_low"))

        def feed_forward(gi, G, f0):
            GU = Layer(ring2, w_gu_v, KD, G)
            DN = Layer(ring2, w_dn_v, G, KD // 2)
            last = gi == len(GROUPS) - 1
            tiles0 = f0
            adds0 = gi * KD

            def ff_sync(sp):
                with sp.Fori(0, G) as i:
                    for s in range(2):
                        GU.load(sp, s, i, i * P + (s * FF + f0 * P))
                with sp.Fori(0, DN.n) as i:
                    for s in range(2):
                        DN.load(sp, s, i, (2 * i + s) * P, rows=f0)

            def ff_scalar(act):
                def silu(turn):
                    for half in range(2):
                        c = slice(half * HALF, (half + 1) * HALF)
                        act.wait_ge(s_gat, 2 * turn + (2 * tiles0 + half + 1))
                        act.activation(sil[:, c], gat[:, c], ACT.Silu).then_inc(s_sil, 1)

                def high(turn):
                    act.wait_ge(s_hid, 2 * turn + (2 * tiles0 + 2))
                    act.activation(row(hidhi[:, bass.ds(turn, 1), :]), hid[:, :], ACT.Copy).then_inc(s_hh7, 1)

                def hidden(turn, more=True):
                    silu(turn)
                    if more:
                        for s in range(2):
                            GU.split_hi(act, s, turn + 1)
                    high(turn)

                with act.Fori(0, G - 1) as i:
                    hidden(i)
                silu(G - 1)
                for s in range(2):
                    DN.split_hi(act, s, 0)
                high(G - 1)
                with act.Fori(1, DN.n) as i:
                    for s in range(2):
                        DN.split_hi(act, s, i)

            def ff_vector(dve):
                def hidden(turn, low):
                    for half in range(2):
                        c = slice(half * HALF, (half + 1) * HALF)
                        if half == 0:
                            dve.wait_ge(s_hl7, turn + (tiles0 + 1))
                        b = GU.J.result(dve, f"0{half}", turn)
                        GU.J.read(dve.tensor_tensor(gat[:, c], b[:, :], rsb2[:, c], ALU.mult), f"0{half}")
                        GU.J.emptied(dve, f"0{half}", turn)
                        dve.sem_inc(s_gat, 1)
                    low()
                    for half in range(2):
                        c = slice(half * HALF, (half + 1) * HALF)
                        b = GU.J.result(dve, f"1{half}", turn)
                        GU.J.read(dve.tensor_tensor(hid[:, c], b[:, :], rsb2[:, c], ALU.mult), f"1{half}")
                        GU.J.emptied(dve, f"1{half}", turn)
                        dve.wait_ge(s_sil, 2 * turn + (2 * tiles0 + half + 1))
                        dve.tensor_tensor(hid[:, c], hid[:, c], sil[:, c], ALU.mult).then_inc(s_hid, 1)
                    dve.wait_ge(s_hh7, turn + (tiles0 + 1))
                    dve.tensor_tensor(row(hidlo[:, bass.ds(turn, 1), :]), hid[:, :],
                                      row(hidhi[:, bass.ds(turn, 1), :]).bitcast(F32), ALU.subtract).then_inc(s_hl7, 1)

                def lows(layer, turn):
                    for s in range(2):
                        layer.split_lo(dve, s, turn)

                with dve.Fori(0, G - 1) as i:
                    hidden(i, lambda: lows(GU, i + 1))
                hidden(G - 1, lambda: lows(DN, 0))

                def add(s, turn):
                    for half in range(2):
                        b = DN.J.result(dve, f"{s}{half}", turn)
                        v = row(x1[:, bass.ds(2 * turn + s, 1), half * HALF:(half + 1) * HALF])
                        DN.J.read(dve.tensor_tensor(v, b[:, :], v, ALU.add), f"{s}{half}")

                with dve.Fori(0, DN.n - 1) as i:
                    for s in range(2):
                        DN.split_lo(dve, s, i + 1)
                        add(s, i)
                for s in range(2):
                    if last:
                        first_half_vector(dve, 4 * s)
                    else:
                        following[gi + 1].split_lo(dve, s, 0)
                    add(s, DN.n - 1)

            def ff_tensor(pe):
                if gi == 0:
                    GU.products_late(pe, 0, x1hi, x1lo, lambda k: pe.wait_ge(s_x1lo, k + 1), norm2_tensor(pe))
                else:
                    for s in range(2):
                        GU.products(pe, s, 0, x1hi, x1lo)
                with pe.Fori(1, G) as i:
                    for s in range(2):
                        GU.products(pe, s, i, x1hi, x1lo)
                DN.products_late(pe, 0, hidhi, hidlo, lambda k: pe.wait_ge(s_hl7, tiles0 + k + 2))
                with pe.Fori(1, DN.n - last) as i:
                    for s in range(2):
                        DN.products(pe, s, i, hidhi, hidlo)
                if last:
                    for s in range(2):
                        first_half_tensor(pe, 4 * s)
                        DN.products(pe, s, DN.n - 1, hidhi, hidlo)

            following[gi] = GU
            ends.append(DN)
            return ff_sync, ff_scalar, ff_vector, ff_tensor

        following, ends, groups = {}, [], []
        f0 = 0
        for gi, G in enumerate(GROUPS):
            groups.append(feed_forward(gi, G, f0))
            f0 += G

        def stage7_sync(sp):
            for g in groups:
                g[0](sp)

        def stage7_scalar(act):
            for gi, g in enumerate(groups):
                if gi:
                    for s in range(2):
                        following[gi].split_hi(act, s, 0)
                g[1](act)

        def stage7_vector(dve):
            dve.sem_inc(s_hl7, 1)
            N2.emptied(dve, "rs0", 0)
            N2.emptied(dve, "rs1", 0)
            for g in groups:
                g[2](dve)

        def stage7_tensor(pe):
            for g in groups:
                g[3](pe)

        s_gf, s_sq8, s_sum, s_rms, s_inv, s_fa, s_fb, s_out = (
            sem(f"s8_{n}") for n in ("gain", "sq", "sum", "rms", "inv", "fin_a", "fin_b", "out"))
        FA = Jobs([(f"{n}", 4 + n) for n in range(4)])
        FA.end(2)
        FB = Jobs([(f"{n}", (4 + n) % 8) for n in range(NT)])
        FB.end(1)
        DNL, GUL = ends[-1], following[len(GROUPS) - 1]

        def by_tokens(pe, b, g, t):
            for k in range(4):
                mm = pe.transpose(b[:, k * P:(k + 1) * P], x1[:, 4 * g + k, t * P:(t + 1) * P], ident)
            return mm

        def first_half_tensor(pe, t0):
            for s in range(2):
                for h in range(2):
                    DNL.J.emptied(pe, f"{s}{h}", 1)
            for n in range(4):
                b = FA.claim(pe, f"{n}", t0 // 4)
                FA.done(by_tokens(pe, b, 0, t0 + n), f"{n}")

        def first_half_vector(dve, t0):
            dve.wait_ge(s_gf, 16)
            for n in range(4):
                b = FA.result(dve, f"{n}", t0 // 4)
                dve.wait_ge(s_sq8, t0 + n + 1)
                FA.read(dve.tensor_tensor(xo[:, t0 + n, :], b[:, :], gfin[:, 0:HALF], ALU.mult), f"{n}")

        def stage8_sync(sp):
            GUL.J.result(sp, "11", GUL.n - 1)
            sp.dma_start(gfin[:, :], norm_final_g.unsqueeze(0).to_broadcast([P, D])).then_inc(s_gf, 16)
            for t in range(NT):
                sp.wait_ge(s_fa, t + 1)
                sp.wait_ge(s_fb, t + 1)
                sp.dma_start(out[0, t * P:(t + 1) * P, :], fin[:, t, :]).then_inc(s_out, 16)
            sp.wait_ge(s_out, 16 * NT)

        def stage8_tensor(pe):
            for s in range(2):
                for h in range(2):
                    DNL.J.emptied(pe, f"{s}{h}", DNL.n - 1)
            for t in range(NT):
                b = FB.claim(pe, f"{t}", 0)
                FB.done(by_tokens(pe, b, 1, t), f"{t}")

        def stage8_scalar(act):
            def squares(b, g, t):
                act.activation(fin[:, t, g * HALF:(g + 1) * HALF], b[:, :], ACT.Square, accum_out=st[:, g, t:t + 1]
                               ).then_inc(s_sq8, 1)

            def root(n):
                c = slice(4 * n, 4 * n + 4)
                act.wait_ge(s_sum, n + 1)
                act.activation(st[:, 2, c], st[:, 2, c], ACT.Sqrt, bias=small[:, 32:33], scale=1.0 / D).then_inc(s_rms, 1)

            def first_half(n):
                act.wait_ge(s_inv, n + 1)
                for t in range(4 * n, 4 * n + 4):
                    act.activation(fin[:, t, 0:HALF], xo[:, t, :], ACT.Copy, scale=st[:, 3, t:t + 1]).then_inc(s_fa, 1)

            for t in range(NT):
                squares(FA.result(act, f"{t % 4}", t // 4), 0, t)
            for n in range(2):
                for t in range(4 * n, 4 * n + 4):
                    squares(FB.result(act, f"{t}", 0), 1, t)
                root(n)
                if n:
                    first_half(0)
            first_half(1)

        def stage8_vector(dve):
            for n in range(2):
                c = slice(4 * n, 4 * n + 4)
                dve.wait_ge(s_sq8, NT + 4 * n + 4)
                dve.tensor_tensor(st[:, 2, c], st[:, 0, c], st[:, 1, c], ALU.add).then_inc(s_sum, 1)
                dve.wait_ge(s_rms, n + 1)
                dve.reciprocal(st[:, 3, c], st[:, 2, c]).then_inc(s_inv, 1)
                dve.wait_ge(s_inv, n + 1)
                for t in range(4 * n, 4 * n + 4):
                    b = FB.result(dve, f"{t}", 0)
                    FB.read(dve.scalar_tensor_tensor(fin[:, t, HALF:], b[:, :], st[:, 3, t:t + 1], gfin[:, HALF:],
                                                     ALU.mult, ALU.mult), f"{t}")
                    FB.emptied(dve, f"{t}", 0)
                    dve.sem_inc(s_fb, 1)

        with nc.Block() as block:
            @block.sync
            def _(sp):
                for stage in (stage1_sync, stage2_sync, stage3_sync, stage5_sync, stage6_sync, stage7_sync, stage8_sync):
                    stage(sp)

            @block.gpsimd
            def _(pool):
                for stage in (stage2_gpsimd, stage3_gpsimd, stage5_gpsimd):
                    stage(pool)

            @block.tensor
            def _(pe):
                for stage in (stage1_tensor, stage2_tensor, stage3_tensor, stage5_tensor, stage6_tensor, stage7_tensor,
                              stage8_tensor):
                    stage(pe)

            @block.scalar
            def _(act):
                for stage in (stage1_scalar, stage2_scalar, stage3_scalar, stage5_scalar, stage6_scalar, stage7_scalar,
                              stage8_scalar):
                    stage(act)

            @block.vector
            def _(dve):
                for stage in (stage1_vector, stage2_vector, stage3_vector, stage5_vector, stage6_vector, stage7_vector,
                              stage8_vector):
                    stage(dve)


_INS = ["x", "norm_mix_g", "w_in", "mu_shift", "w0", "w_up", "a0", "a_up", "g_up", "k_k", "k_a", "r_k", "gn_g", "gn_b",
        "sinks", "w_out", "norm_ffn_g", "w_gate_up", "w_down", "norm_final_g"]


def kernel(**inputs):
    import concourse.bacc as bacc
    from concourse.bass_utils import run_bass_kernel_spmd

    nc = bacc.Bacc("TRN2", target_bir_lowering=False, num_devices=1)
    arrays, args = {}, []
    given = {name: np.ascontiguousarray(inputs[name]) for name in _INS}
    given.update(consts=constants(), alibi=alibi())
    for name, a in given.items():
        arrays[f"in_{name}"] = a
        args.append(nc.dram_tensor(f"in_{name}", a.shape, mybir.dt.from_np(a.dtype), kind="ExternalInput").ap())
    args.append(nc.dram_tensor("out_0", (1, T, D), F32, kind="ExternalOutput").ap())
    hybrid_block(nc, *args)
    r = run_bass_kernel_spmd(nc, [arrays], core_ids=[0])
    return r.results[0]["out_0"]
```
